# Optimizing a Trainium2 kernel written in Bass

```python
import jax
import jax.numpy as jnp
from jax import lax
import numpy as np

D_MODEL = 2048
BATCH = 1
SEQ = 256
DEPTH = 2

N_MIXERS = 3
NORM_EPS = 1e-6

MOBA_HEADS = 16
MOBA_HEAD_DIM = D_MODEL // MOBA_HEADS
MOBA_BLOCK = 256
MOBA_TOPK = 3
MOBA_QCHUNK = 16
ROPE_THETA = 500000.0
ROT_DIM = MOBA_HEAD_DIM // 4

RWKV_HEAD_SIZE = 64
RWKV_HEADS = D_MODEL // RWKV_HEAD_SIZE
RWKV_DECAY_LORA = max(32, int(round(1.8 * D_MODEL ** 0.5 / 32)) * 32)
RWKV_AAA_LORA = max(32, int(round(1.8 * D_MODEL ** 0.5 / 32)) * 32)
RWKV_GATE_LORA = max(32, int(round(0.6 * D_MODEL ** 0.8 / 32)) * 32)
RWKV_GN_EPS = 64e-5

MLSTM_HEADS = 8
MLSTM_DV = D_MODEL // MLSTM_HEADS
MLSTM_DQK = MLSTM_DV // 2
MLSTM_CHUNK = 64
GATE_SOFTCAP = 15.0

D_FF = ((8 * D_MODEL // 3 + 255) // 256) * 256
CONV_WIDTH = 3

N_MOBA_LAYERS = len(range(0, DEPTH, N_MIXERS))
N_RWKV_LAYERS = len(range(1, DEPTH, N_MIXERS))
N_MLSTM_LAYERS = len(range(2, DEPTH, N_MIXERS))

kernel_name = 'hybrid_moba_rwkv7_mlstm_convffn'

def rms_norm(x, gain, eps=NORM_EPS):
    xf = x.astype(jnp.float32)
    y = xf * lax.rsqrt(jnp.mean(xf * xf, axis=-1, keepdims=True) + eps)
    return (y * gain.astype(jnp.float32)).astype(x.dtype)

def rope_tables(seq_len):
    inv_freq = jnp.float32(ROPE_THETA) ** (-jnp.arange(0, ROT_DIM, 2, dtype=jnp.float32) / ROT_DIM)
    ang = jnp.arange(seq_len, dtype=jnp.float32)[:, None] * inv_freq[None, :]
    return jnp.cos(ang), jnp.sin(ang)

def apply_partial_rope(x, cos, sin):
    half = ROT_DIM // 2
    x1 = x[..., :half].astype(jnp.float32)
    x2 = x[..., half:ROT_DIM].astype(jnp.float32)
    r1 = (x1 * cos - x2 * sin).astype(x.dtype)
    r2 = (x2 * cos + x1 * sin).astype(x.dtype)
    return jnp.concatenate([r1, r2, x[..., ROT_DIM:]], axis=-1)

def moba_attention(h, wqkv, wo, q_gain, k_gain, cos, sin):
    B, S, _ = h.shape
    H, Dh, BLK, QC = MOBA_HEADS, MOBA_HEAD_DIM, MOBA_BLOCK, MOBA_QCHUNK
    qkv = (h @ wqkv).reshape(B, S, 3, H, Dh)
    q = jnp.transpose(qkv[:, :, 0], (0, 2, 1, 3))
    k = jnp.transpose(qkv[:, :, 1], (0, 2, 1, 3))
    v = jnp.transpose(qkv[:, :, 2], (0, 2, 1, 3))
    q = apply_partial_rope(rms_norm(q, q_gain), cos, sin)
    k = apply_partial_rope(rms_norm(k, k_gain), cos, sin)
    n_blocks = -(-S // BLK)
    s_pad = n_blocks * BLK
    pad = ((0, 0), (0, 0), (0, s_pad - S), (0, 0))
    q, k, v = jnp.pad(q, pad), jnp.pad(k, pad), jnp.pad(v, pad)
    scale = Dh ** -0.5
    k_blocks = k.reshape(B, H, n_blocks, BLK, Dh)
    v_blocks = v.reshape(B, H, n_blocks, BLK, Dh)
    n_sel = min(MOBA_TOPK, n_blocks - 1)
    if n_sel > 0:
        k_mean = jnp.mean(k_blocks.astype(jnp.float32), axis=3)
        gate = jnp.einsum('bhsd,bhnd->bhsn', q.astype(jnp.float32), k_mean)
        q_block = jnp.arange(s_pad) // BLK
        fully_past = jnp.arange(n_blocks)[None, :] < q_block[:, None]
        gate = jnp.where(fully_past, gate, -jnp.inf)
        _, sel = lax.top_k(gate, n_sel)
    else:
        sel = jnp.zeros((B, H, s_pad, 0), jnp.int32)
    n_chunks = s_pad // QC
    q_chunks = jnp.transpose(q.reshape(B, H, n_chunks, QC, Dh), (2, 0, 1, 3, 4))
    sel_chunks = jnp.transpose(sel.reshape(B, H, n_chunks, QC, n_sel), (2, 0, 1, 3, 4))
    starts = jnp.arange(n_chunks, dtype=jnp.int32) * QC
    b_idx = jnp.arange(B)[:, None, None, None]
    h_idx = jnp.arange(H)[None, :, None, None]

    def chunk_attn(args):
        q_c, sel_c, start = args
        own = start // BLK
        q_pos = start + jnp.arange(QC)
        k_own = lax.dynamic_slice_in_dim(k, own * BLK, BLK, axis=2)
        v_own = lax.dynamic_slice_in_dim(v, own * BLK, BLK, axis=2)
        k_pos = own * BLK + jnp.arange(BLK)
        s_own = jnp.einsum('bhqd,bhkd->bhqk', q_c, k_own).astype(jnp.float32) * scale
        s_own = jnp.where(k_pos[None, :] <= q_pos[:, None], s_own, -jnp.inf)
        k_sel = k_blocks[b_idx, h_idx, sel_c]
        v_sel = v_blocks[b_idx, h_idx, sel_c]
        s_sel = jnp.einsum('bhqd,bhqnkd->bhqnk', q_c, k_sel).astype(jnp.float32) * scale
        slot_ok = jnp.arange(n_sel) < own
        s_sel = jnp.where(slot_ok[:, None], s_sel, -jnp.inf)
        s_all = jnp.concatenate([s_sel.reshape(B, H, QC, n_sel * BLK), s_own], axis=-1)
        p = jax.nn.softmax(s_all, axis=-1).astype(v.dtype)
        p_sel = p[..., :n_sel * BLK].reshape(B, H, QC, n_sel, BLK)
        p_own = p[..., n_sel * BLK:]
        return (jnp.einsum('bhqnk,bhqnkd->bhqd', p_sel, v_sel)
                + jnp.einsum('bhqk,bhkd->bhqd', p_own, v_own))

    out = lax.map(chunk_attn, (q_chunks, sel_chunks, starts))
    out = jnp.transpose(out, (1, 0, 3, 2, 4)).reshape(B, s_pad, H * Dh)[:, :S]
    return out @ wo

def rwkv7_time_mix(h, mu, w_r, w_k, w_v, w_o, w0, w1, w2, a0, a1, a2, g1, g2,
                   k_k, k_a, r_k, lnx_w, lnx_b):
    B, S, D = h.shape
    H, N = RWKV_HEADS, RWKV_HEAD_SIZE
    f32 = jnp.float32
    xx = jnp.pad(h, ((0, 0), (1, 0), (0, 0)))[:, :S] - h
    x_r = h + xx * mu[0]
    x_w = h + xx * mu[1]
    x_k = h + xx * mu[2]
    x_v = h + xx * mu[3]
    x_a = h + xx * mu[4]
    x_g = h + xx * mu[5]
    r = x_r @ w_r
    k = x_k @ w_k
    v = x_v @ w_v
    w_log = -jax.nn.softplus(-(w0 + jnp.tanh(x_w @ w1) @ w2).astype(f32)) - 0.5
    decay = jnp.exp(-jnp.exp(w_log))
    a = jax.nn.sigmoid((a0 + (x_a @ a1) @ a2).astype(f32))
    g = jax.nn.sigmoid(x_g @ g1) @ g2
    kk = (k * k_k).astype(f32).reshape(B, S, H, N)
    kk = kk / jnp.maximum(jnp.sqrt(jnp.sum(kk * kk, axis=-1, keepdims=True)), 1e-12)
    kk = kk.reshape(B, S, D)
    k_mod = k.astype(f32) * (1.0 + (a - 1.0) * k_a)
    r32, v32 = r.astype(f32), v.astype(f32)

    def heads_tm(t):
        return jnp.transpose(t.reshape(B, S, H, N), (1, 0, 2, 3))

    xs = (heads_tm(r32), heads_tm(decay), heads_tm(k_mod), heads_tm(v32),
          heads_tm(-kk), heads_tm(kk * a))

    def step(state, inp):
        r_t, w_t, k_t, v_t, a_t, b_t = inp
        sa = jnp.einsum('bhvk,bhk->bhv', state, a_t)
        state = (state * w_t[:, :, None, :] + sa[..., None] * b_t[:, :, None, :]
                 + v_t[..., None] * k_t[:, :, None, :])
        return state, jnp.einsum('bhvk,bhk->bhv', state, r_t)

    _, y = lax.scan(step, jnp.zeros((B, H, N, N), f32), xs)
    y = jnp.transpose(y, (1, 0, 2, 3))
    mean = jnp.mean(y, axis=-1, keepdims=True)
    var = jnp.mean(jnp.square(y - mean), axis=-1, keepdims=True)
    y = ((y - mean) * lax.rsqrt(var + RWKV_GN_EPS)).reshape(B, S, D)
    y = y * lnx_w.astype(f32) + lnx_b.astype(f32)
    bonus = jnp.sum(r32.reshape(B, S, H, N) * k_mod.reshape(B, S, H, N) * r_k.astype(f32),
                    axis=-1, keepdims=True) * v32.reshape(B, S, H, N)
    out = (y + bonus.reshape(B, S, D)) * g.astype(f32)
    return out.astype(h.dtype) @ w_o

def mlstm_mixer(h, w_in, b_if, head_gain, w_out):
    B, S, _ = h.shape
    H, Dk, Dv, L = MLSTM_HEADS, MLSTM_DQK, MLSTM_DV, MLSTM_CHUNK
    f32 = jnp.float32
    proj = h @ w_in
    o0, o1, o2, o3, o4 = H * Dk, 2 * H * Dk, 2 * H * Dk + H * Dv, 2 * H * Dk + 2 * H * Dv, 2 * H * Dk + 2 * H * Dv + H
    q, k, v, o = proj[..., :o0], proj[..., o0:o1], proj[..., o1:o2], proj[..., o2:o3]
    i_pre, f_pre = proj[..., o3:o4], proj[..., o4:]

    def heads(t, d):
        return jnp.transpose(t.reshape(B, S, H, d), (0, 2, 1, 3)).astype(f32)

    q = heads(q, Dk)
    k = heads(k, Dk) * (Dk ** -0.5)
    v = heads(v, Dv)
    cap = lambda z: GATE_SOFTCAP * jnp.tanh(z / GATE_SOFTCAP)
    log_i = jnp.transpose(cap(i_pre.astype(f32) + b_if[0].astype(f32)), (0, 2, 1))
    log_f = jnp.transpose(jax.nn.log_sigmoid(cap(f_pre.astype(f32) + b_if[1].astype(f32))), (0, 2, 1))
    nc = S // L

    def chunk(t):
        return jnp.moveaxis(t.reshape(B, H, nc, L, *t.shape[3:]), 2, 0)

    causal = jnp.tril(jnp.ones((L, L), dtype=bool))

    def step(carry, inp):
        C, n, m = carry
        q_c, k_c, v_c, li, lf = inp
        b = jnp.cumsum(lf, axis=-1)
        dmat = jnp.where(causal, b[..., :, None] - b[..., None, :] + li[..., None, :], -jnp.inf)
        inter = b + m[..., None]
        m_t = jnp.maximum(inter, jnp.max(dmat, axis=-1))
        s = jnp.einsum('bhtd,bhsd->bhts', q_c, k_c) * jnp.exp(dmat - m_t[..., None])
        w_inter = jnp.exp(inter - m_t)
        num = (jnp.einsum('bhts,bhsv->bhtv', s, v_c)
               + w_inter[..., None] * jnp.einsum('bhvd,bhtd->bhtv', C, q_c))
        den = jnp.sum(s, axis=-1) + w_inter * jnp.einsum('bhd,bhtd->bht', n, q_c)
        h_c = num / jnp.maximum(jnp.abs(den), jnp.exp(-m_t))[..., None]
        b_last = b[..., -1]
        d_s = b_last[..., None] - b + li
        m_new = jnp.maximum(b_last + m, jnp.max(d_s, axis=-1))
        w_s = jnp.exp(d_s - m_new[..., None])
        w_c = jnp.exp(b_last + m - m_new)
        C_new = w_c[..., None, None] * C + jnp.einsum('bhs,bhsv,bhsd->bhvd', w_s, v_c, k_c)
        n_new = w_c[..., None] * n + jnp.einsum('bhs,bhsd->bhd', w_s, k_c)
        return (C_new, n_new, m_new), h_c

    carry0 = (jnp.zeros((B, H, Dv, Dk), f32), jnp.zeros((B, H, Dk), f32), jnp.zeros((B, H), f32))
    _, hs = lax.scan(step, carry0, (chunk(q), chunk(k), chunk(v), chunk(log_i), chunk(log_f)))
    hs = jnp.moveaxis(hs, 0, 2).reshape(B, H, S, Dv)
    hs = jnp.transpose(hs, (0, 2, 1, 3))
    hs = rms_norm(hs, head_gain.reshape(H, Dv)).reshape(B, S, H * Dv)
    out = hs * jax.nn.sigmoid(o.astype(f32))
    return out.astype(h.dtype) @ w_out

def conv_ffn(h, w_up, conv_w, conv_b, w_down):
    u = h @ w_up
    u = lax.conv_general_dilated(u, conv_w[:, None, :], window_strides=(1,),
                                 padding=[(CONV_WIDTH - 1, 0)],
                                 dimension_numbers=('NWC', 'WIO', 'NWC'),
                                 feature_group_count=u.shape[-1]) + conv_b
    gate, up = u[..., :D_FF], u[..., D_FF:]
    return (jax.nn.silu(gate) * up) @ w_down

def setup_inputs(seed: int = 0) -> dict:
    key = jax.random.key(seed)
    ks = iter(jax.random.split(key, 40))

    def nrm(shape, scale):
        return jax.random.normal(next(ks), shape, jnp.float32) * scale

    def gain(shape):
        return 1.0 + nrm(shape, 0.02)

    D, F = D_MODEL, D_FF
    nA, nB, nC = N_MOBA_LAYERS, N_RWKV_LAYERS, N_MLSTM_LAYERS
    d_in_mlstm = MLSTM_HEADS * (2 * MLSTM_DQK + 2 * MLSTM_DV + 2)
    return {
        'x': nrm((BATCH, SEQ, D), 1.0),
        'moba_norm': gain((nA, D)),
        'moba_wqkv': nrm((nA, D, 3 * D), D ** -0.5),
        'moba_q_gain': gain((nA, MOBA_HEAD_DIM)),
        'moba_k_gain': gain((nA, MOBA_HEAD_DIM)),
        'moba_wo': nrm((nA, D, D), D ** -0.5),
        'rwkv_norm': gain((nB, D)),
        'rwkv_mu': jax.random.uniform(next(ks), (nB, 6, D), jnp.float32),
        'rwkv_w_r': nrm((nB, D, D), D ** -0.5),
        'rwkv_w_k': nrm((nB, D, D), D ** -0.5),
        'rwkv_w_v': nrm((nB, D, D), D ** -0.5),
        'rwkv_w_o': nrm((nB, D, D), D ** -0.5),
        'rwkv_w0': nrm((nB, D), 0.5),
        'rwkv_w1': nrm((nB, D, RWKV_DECAY_LORA), D ** -0.5),
        'rwkv_w2': nrm((nB, RWKV_DECAY_LORA, D), RWKV_DECAY_LORA ** -0.5),
        'rwkv_a0': nrm((nB, D), 0.1),
        'rwkv_a1': nrm((nB, D, RWKV_AAA_LORA), D ** -0.5),
        'rwkv_a2': nrm((nB, RWKV_AAA_LORA, D), RWKV_AAA_LORA ** -0.5),
        'rwkv_g1': nrm((nB, D, RWKV_GATE_LORA), D ** -0.5),
        'rwkv_g2': nrm((nB, RWKV_GATE_LORA, D), RWKV_GATE_LORA ** -0.5),
        'rwkv_k_k': 0.85 + nrm((nB, D), 0.05),
        'rwkv_k_a': 1.0 + nrm((nB, D), 0.05),
        'rwkv_r_k': nrm((nB, RWKV_HEADS, RWKV_HEAD_SIZE), 0.1),
        'rwkv_lnx_w': gain((nB, D)),
        'rwkv_lnx_b': nrm((nB, D), 0.02),
        'mlstm_norm': gain((nC, D)),
        'mlstm_w_in': nrm((nC, D, d_in_mlstm), D ** -0.5),
        'mlstm_b_if': nrm((nC, 2, MLSTM_HEADS), 0.1) + jnp.array([0.0, 3.0], jnp.float32)[None, :, None],
        'mlstm_head_gain': gain((nC, MLSTM_HEADS * MLSTM_DV)),
        'mlstm_w_out': nrm((nC, MLSTM_HEADS * MLSTM_DV, D), (MLSTM_HEADS * MLSTM_DV) ** -0.5),
        'ffn_norm': gain((DEPTH, D)),
        'ffn_w_up': nrm((DEPTH, D, 2 * F), D ** -0.5),
        'ffn_conv_w': nrm((DEPTH, CONV_WIDTH, 2 * F), CONV_WIDTH ** -0.5),
        'ffn_conv_b': nrm((DEPTH, 2 * F), 0.02),
        'ffn_w_down': nrm((DEPTH, F, D), F ** -0.5),
    }

def reference(x, moba_norm, moba_wqkv, moba_q_gain, moba_k_gain, moba_wo,
              rwkv_norm, rwkv_mu, rwkv_w_r, rwkv_w_k, rwkv_w_v, rwkv_w_o,
              rwkv_w0, rwkv_w1, rwkv_w2, rwkv_a0, rwkv_a1, rwkv_a2, rwkv_g1, rwkv_g2,
              rwkv_k_k, rwkv_k_a, rwkv_r_k, rwkv_lnx_w, rwkv_lnx_b,
              mlstm_norm, mlstm_w_in, mlstm_b_if, mlstm_head_gain, mlstm_w_out,
              ffn_norm, ffn_w_up, ffn_conv_w, ffn_conv_b, ffn_w_down):
    cos, sin = rope_tables(x.shape[1])
    for i in range(DEPTH):
        kind, j = i % N_MIXERS, i // N_MIXERS
        if kind == 0:
            x = x + moba_attention(rms_norm(x, moba_norm[j]), moba_wqkv[j], moba_wo[j],
                                   moba_q_gain[j], moba_k_gain[j], cos, sin)
        elif kind == 1:
            x = x + rwkv7_time_mix(rms_norm(x, rwkv_norm[j]), rwkv_mu[j], rwkv_w_r[j], rwkv_w_k[j],
                                   rwkv_w_v[j], rwkv_w_o[j], rwkv_w0[j], rwkv_w1[j], rwkv_w2[j],
                                   rwkv_a0[j], rwkv_a1[j], rwkv_a2[j], rwkv_g1[j], rwkv_g2[j],
                                   rwkv_k_k[j], rwkv_k_a[j], rwkv_r_k[j], rwkv_lnx_w[j], rwkv_lnx_b[j])
        else:
            x = x + mlstm_mixer(rms_norm(x, mlstm_norm[j]), mlstm_w_in[j], mlstm_b_if[j],
                                mlstm_head_gain[j], mlstm_w_out[j])
        x = x + conv_ffn(rms_norm(x, ffn_norm[i]), ffn_w_up[i], ffn_conv_w[i], ffn_conv_b[i], ffn_w_down[i])
    return x


_drawn_inputs = setup_inputs


def setup_inputs(seed=0):
    import zlib

    import numpy as np

    out = dict(_drawn_inputs(seed))
    spreads = {}
    factors = {'moba_norm': 5.685,
     'moba_q_gain': 8.0,
     'moba_k_gain': 8.0,
     'rwkv_norm': 3.02,
     'rwkv_k_k': 60.258,
     'rwkv_lnx_w': 40.323,
     'rwkv_lnx_b': 38.418,
     'ffn_norm': 8.0,
     'ffn_conv_b': 8.0}
    for name, (base, spread) in spreads.items():
        noise = np.random.default_rng([zlib.crc32(name.encode()), seed]).standard_normal(out[name].shape)
        drawn = base * np.exp(spread * noise) if base else spread * noise
        out[name] = jnp.asarray(drawn.astype(out[name].dtype))
    for name, factor in factors.items():
        out[name] = (out[name] * factor).astype(out[name].dtype)
    return out
```

```python
import concourse.bass as bass
from concourse import mybir

P = 128
T = 256
D = 2048
KT = D // P
FF = 5632
FKT = FF // P
NORM_EPS = 1e-6
GN_EPS = 64e-5
HD = 128
NH = D // HD
RH = 64
LORA = 96
UNIT = 512
RAW = 3
SPLIT = 2
PAN = 2048
HALF_A = 6
HALF_B = 5
LEVELS = 6
EXPM05 = 0.6065306597126334
SEED = 8
QT = 4 * T


def columns(*specs):
    at, got = 0, {}
    for name, w in specs:
        got[name] = (at, at + w)
        at += w
    return got, at


CONST, NCONST = columns(("ident", P), ("ones", P), ("blk", P), ("mb", 2 * P), ("mk", 2 * P), ("mx1", P), ("mx1t", P),
                        ("lv", P * LEVELS), ("ksum", 32), ("kbc", 4 * P), ("eps", 4))
ROPE, NROPE = columns(("perm", P), ("cos", T), ("sin", T), ("cmask", 384), ("ssum", 16), ("sbc", 4 * P))
PA, PB, PC, PCV = 0, 128, 240, 274
PRM_COLS = PCV + 8 * 88
G_MOBA, G_RWKV, MU = 0, 16, 32
W0, A0, K_K, K_A, R_K, LNW, LNB = (PB + 16 * i for i in range(7))
G_FFN, QG, KG = PC, PC + 32, PC + 33
OMKA = PRM_COLS
ROW_LOADS = 3 + 7 + 3 + 2 * 4


class Job:

    def __init__(self, name, n, units, accs):
        self.name, self.n, self.units, self.accs = name, n, units, accs
        self.m = sum(units)
        self.last_panel = [sum(units[:k + 1]) - 1 for k in range(len(units))]

    def panel(self, i, j):
        return self.first_panel + i * self.m + j

    def unit(self, i, w):
        return self.first_unit + i * self.accs + w

    def panel_end(self, i, j):
        return self.first_panel + i * self.m + (j + 1)

    def unit_end(self, i, w):
        return self.first_unit + i * self.accs + (w + 1)

    def landed(self, i, j):
        s = self.raw[j]
        return i * (16 * self.uses[s]) + 16 * (self.landed0[s] + self.raw[:j + 1].count(s))


def gaps(job, idx, slots, last):
    got = []
    for j, s in enumerate(slots):
        earlier = [q for q in range(j) if slots[q] == s]
        if earlier:
            got.append(j - earlier[-1])
            continue
        back = [idx + j - last[s]]
        if job.n > 1:
            back.append(job.m - max(q for q in range(job.m) if slots[q] == s) + j)
        got.append(min(back))
    for s in set(slots):
        last[s] = idx + (job.n - 1) * job.m + max(q for q in range(job.m) if slots[q] == s)
    return got


def plan(jobs):
    idx, unit = SEED, 2
    landed = [0] * RAW
    last_raw, last_split = [SEED - 1] * RAW, [SEED - 1] * SPLIT
    for job in jobs:
        job.first_panel, job.first_unit = idx, unit
        job.raw = [j % RAW for j in range(job.m)]
        job.hl = [j % SPLIT for j in range(job.m)]
        job.landed0 = list(landed)
        job.uses = [job.raw.count(s) for s in range(RAW)]
        job.raw_gap = gaps(job, idx, job.raw, last_raw)
        job.hl_gap = gaps(job, idx, job.hl, last_split)
        for s in range(RAW):
            landed[s] += job.n * job.uses[s]
        idx += job.n * job.m
        unit += job.n * job.accs


def hybrid_trunk(nc, x, moba_norm, moba_wqkv, moba_q_gain, moba_k_gain, moba_wo,
                 rwkv_norm, rwkv_mu, rwkv_w_r, rwkv_w_k, rwkv_w_v, rwkv_w_o,
                 rwkv_w0, rwkv_w1, rwkv_w2, rwkv_a0, rwkv_a1, rwkv_a2, rwkv_g1, rwkv_g2,
                 rwkv_k_k, rwkv_k_a, rwkv_r_k, rwkv_lnx_w, rwkv_lnx_b,
                 ffn_norm, ffn_w_up, ffn_conv_w, ffn_conv_b, ffn_w_down, const_all, const_rope, out,
                 x_spill, r_spill, v_spill, g_spill, layers=4):
    f32, f32r = mybir.dt.float32, mybir.dt.float32r
    ALU, ACT, AX = mybir.AluOpType, mybir.ActivationFunctionType, mybir.AxisListType

    J = {}
    stages = ((1, "q", 2, [4, 4], 2), (1, "k", 2, [4, 4], 2), (1, "v", 2, [4, 4], 2), (1, "wo", 2, [4, 4], 2),
              (2, "up0a", HALF_A, [4, 4], 2), (2, "dn0a", 2, [6, 6], 2),
              (2, "up0b", HALF_B, [4, 4], 2), (2, "dn0b", 2, [5, 5], 2),
              (3, "rg", 1, [4], 5), (3, "rv", 2, [4, 4], 2), (3, "rw", 1, [2], 5), (3, "ra", 1, [2], 5),
              (3, "rk", 2, [4, 4], 2), (3, "rr", 2, [4, 4], 2), (3, "ro", 2, [4, 4], 2),
              (4, "up1a", HALF_A, [4, 4], 2), (4, "dn1a", 2, [6, 6], 2),
              (4, "up1b", HALF_B, [4, 4], 2), (4, "dn1b", 2, [5, 5], 2))
    for layer, name, n, units, accs in stages:
        if layer <= layers:
            J[name] = Job(name, n, units, accs)
    order = list(J)
    plan([J[n] for n in order])
    final_job = J[order[-1]]

    def rows(w):
        return w.rearrange("(t p) n -> p t n", p=P)

    top = [(nc.sbuf_base + 31) // 32 * 32]
    limit = nc.sbuf_usable_end

    def place(at, *specs):
        fixed = at is None
        at = top[0] if fixed else at
        got = []
        for name, shape, dt in specs:
            size = 4
            for s in shape[1:]:
                size *= s
            assert at + size <= limit, (name, at + size - limit)
            got.append(nc.alloc_sbuf_tensor_at(name, shape, dt, offset=at))
            at += (size + 31) // 32 * 32
        if fixed:
            top[0] = at
        return got

    xT_at = top[0]
    (xT, hH, hL, raw, wh, wl, cst, prm, rstd, rt) = place(
        None, ("xT", [P, KT, T], f32), ("hH", [P, KT, T], f32r), ("hL", [P, KT, T], f32r),
        ("raw", [P, RAW, PAN], f32), ("wh", [P, SPLIT, PAN], f32r), ("wl", [P, SPLIT, PAN], f32r),
        ("cst", [P, NCONST], f32), ("prm", [P, PRM_COLS + 16], f32), ("rstd", [P, T], f32), ("mid", [P, 8], f32))
    mid = rt
    area = top[0]
    K16 = KT * T * 4
    xin, prow = place(area, ("xin", [P, 2, D], f32), ("prow", [P, 11, P], f32))
    norm_at = area + 3 * K16
    sq, sqacc, hf = place(norm_at, ("sq", [P, QT], f32), ("sqacc", [P, QT], f32), ("hf", [P, 2, QT], f32))
    rest_at = norm_at + 4 * QT * 4
    QKV, = place(area, ("QKV", [P, 3 * KT, T], f32))
    rot, nrmd, ssr, rsr, cr = place(rest_at, ("rot", [P, QT], f32), ("nrmd", [P, QT], f32), ("ssr", [4, 2, T], f32),
                                    ("rsr", [4, 2, T], f32), ("cr", [P, NROPE], f32))
    sq2, = place(norm_at + 2 * QT * 4, ("sq2", [P, 2, QT], f32))
    qs, vs, vt, sc, ex, pT, st = place(
        norm_at, ("qs", [P, 2, T], f32), ("vs", [P, 2, T], f32), ("vt", [P, 2, T], f32), ("sc", [P, 2, 384], f32),
        ("ex", [P, 2, 384], f32), ("pT", [P, 2, 384], f32), ("st", [P, 2, 8], f32))
    aH, aL = place(area, ("aH", [P, 4 * HALF_A, T], f32r), ("aL", [P, 4 * HALF_A, T], f32r))
    sg, fu, fc = place(rest_at, ("sg", [P, QT], f32), ("fu", [P, QT], f32), ("fc", [P, QT], f32))
    hb, xx, cw, kb, ab, ru, mt = place(
        area, ("hb", [P, KT, T], f32), ("xx", [P, KT, T], f32), ("cw", [P, KT, 2, 129], f32),
        ("kb", [P, KT, T], f32), ("ab", [P, KT, T], f32), ("ru", [P, QT], f32), ("mt", [P, QT], f32))
    xx_at = area + K16
    kb_at = xx_at + K16 + KT * 258 * 4
    ru_at = kb_at + 2 * K16
    tH, tL = place(kb_at, ("tH", [P, 2, T], f32r), ("tL", [P, 2, T], f32r))
    kkr, kq, kss, krs = place(xx_at, ("kkr", [P, 2, QT], f32), ("kq", [P, QT], f32),
                              ("kss", [8, 2, T], f32), ("krs", [8, 2, T], f32))
    kkb, = place(area, ("kkb", [P, KT, T], f32))
    Qb, X, XT = place(xT_at, ("Qb", [P, LEVELS * 4, P], f32), ("Xb", [P, 2, 2, P], f32), ("XTb", [P, 2, 2, P], f32))
    bt, kt_, mB, mK, tok, rb, vb, y3 = place(
        xx_at, ("bt", [P, 2, P], f32), ("ktl", [P, 2, P], f32),
        ("mBt", [P, 2, 2, 2 * P], f32), ("mKt", [P, 2, 2, 2 * P], f32), ("tok", [P, 4, P], f32),
        ("rb", [P, T], f32), ("vb", [P, T], f32), ("y3", [P, T], f32))
    slot1_at = xT_at + 3 * K16 + RAW * PAN * 4 + PAN * 4
    bp, ys, y2, s0 = place(slot1_at, ("bp", [P, T], f32), ("ys", [P, T], f32), ("y2", [P, T], f32),
                           ("s0", [P, RH], f32))
    ar, e2, gb, e1, zb, ub, scl = place(
        ru_at, ("ar", [P, 2, 2, 2, P], f32), ("e2", [P, 2, P], f32), ("gb", [P, T], f32), ("e1", [P, 2, 129], f32),
        ("zb", [P, 2, 2, RH], f32), ("ub", [P, 2, 2, RH], f32), ("scl", [P, 1], f32))
    xo, = place(area, ("xo", [P, 2, D], f32))

    acc = [nc.alloc_psum_tensor(f"acc{k}", [P, QT], f32) for k in range(2)]
    aux = [nc.alloc_psum_tensor(f"aux{k}", [P, QT], f32) for k in range(2)]

    def bank(k):
        return (acc + aux)[k // 2][:, (k % 2) * 512:(k % 2) * 512 + 512]

    def C(name, a=0, b=None, p=P):
        lo, hi = CONST[name]
        return cst[0:p, lo + a:hi if b is None else lo + b]

    def R(name, a=0, b=None, p=P):
        lo, hi = ROPE[name]
        return cr[0:p, lo + a:hi if b is None else lo + b]

    def quad(ap):
        return ap.rearrange("p (f t) -> p f t", f=4)

    def sem(name):
        return nc.alloc_semaphore(name)

    raw_landed = [sem(f"raw_landed{k}") for k in range(RAW)]
    hi_split, lo_split = sem("hi_split"), sem("lo_split")
    panel_used = sem("panel_used")
    unit_out = sem("unit_out")
    const_in, x_in, rows_in = sem("const_in"), sem("x_in"), sem("rows_in")
    turned, turned_out = sem("turned"), sem("turned_out")
    omka_done = sem("omka_done")

    class Names:

        def __init__(self, phase, *names):
            self.sems = {n: sem(f"{phase}_{n}") for n in names}

        def __getitem__(self, n):
            return self.sems[n]

    norm_names = ("squared", "summed", "total", "rooted", "rstd", "normed", "hi", "lo")
    N = {k: Names(k, *norm_names) for k in ("n0", "n1", "n2", "n3")[:layers]}
    qk = Names("qk", "squared", "summed", "rooted", "inverse", "spread", "normed", "turned", "cosed", "sined", "roped")
    at = Names("at", "staged", "vturned", "vout", "scored", "masked", "maxed", "neg", "exped", "recip", "probs",
               "pturned", "pout", "mixed", "hi", "lo")
    f = Names("ffn", "init", "tap1", "tap0", "silu", "gated", "hi", "lo")
    M = Names("mix", "h", "xx", "mixed", "hi", "lo", "low_hi", "low_lo", "zeroed", "scan", "mid", "cw",
              "kkr", "ksq", "ksum", "kroot", "kmax", "krec", "kspread", "kk", "kfac", "kmod", "kb",
              "x_spilled", "r_spilled", "v_spilled", "g_spilled", "x_back", "low_unit")
    W = Names("core", "zeroed", "exps", "scaled", "bonusp", "turned", "tok", "gram", "gmask", "geye", "xt0",
              "lev0", "x0", "lp", "lq", "lx", "lt", "lxo", "lto", "zmm", "zout", "umm", "uout", "smm", "sout",
              "ymm", "yout", "mean", "cent", "csq", "var", "std", "rec", "norm", "aff", "bmm", "bon", "ysum", "gate",
              "hi", "lo")
    W.sems.update({n: sem(f"core_{n}") for n in ("r_in", "v_in", "g_in")})
    out_turned, out_ready, out_done = sem("out_turned"), sem("out_ready"), sem("out_done")

    block_ctx = nc.Block()
    block = block_ctx.__enter__()

    def run(eng, job, split, first=None, every=None, late=None, last=None):
        first, every, late, last = first or {}, every or {}, late or {}, last or {}

        def body(i, is_first, is_last):
            for j in range(job.m):
                if j + 1 < job.m or not (job is final_job and is_last):
                    split(eng, job, i, j + 1)
                if is_first:
                    for f in first.get(j, ()):
                        f()
                else:
                    for f in late.get(j, ()):
                        f(i - 1)
                for f in every.get(j, ()):
                    f(i)
                if is_last:
                    for f in last.get(j, ()):
                        f()

        body(0, True, job.n == 1)
        if job.n == 2:
            body(1, False, True)
        elif job.n > 2:
            with eng.Fori(1, job.n) as i:
                body(i, False, False)

    following = {order[k]: order[k + 1] for k in range(len(order) - 1)}

    def next_place(job, i, j):
        if j < job.m:
            return job, i, j
        return job, i + 1, 0

    @block.sync
    def _(sp):
        def load(job, src, width=PAN, parts=P, shape=None):
            def body(i):
                base = src(i)
                for j in range(job.m):
                    sp.wait_ge(lo_split, job.panel_end(i, j) - job.raw_gap[j])
                    view = base(j)
                    a, b = view.shape[1], view.shape[2]
                    dst = raw[0:view.shape[0], job.raw[j], 0:a * b].rearrange("p (a b) -> p a b", a=a)
                    sp.dma_start(dst, view).then_inc(raw_landed[job.raw[j]], 16)
            if job.n == 1:
                body(0)
            else:
                with sp.Fori(0, job.n) as i:
                    body(i)

        def plain(w, k0=0, c0=0, per=4):
            def src(i):
                col = sp.snap(i * (2 * UNIT))

                def view(j):
                    u, p = divmod(j, per)
                    cut = w[:, k0 + 4 * p:k0 + 4 * p + 4, c0 + u * UNIT:]
                    return cut[:, :, bass.ds(col, UNIT)]
                return view
            return src

        def gate_up(w, g0):
            def src(i):
                col = sp.snap(i * UNIT)

                def view(j):
                    u, p = divmod(j, 4)
                    cut = w[:, 4 * p:4 * p + 4, u * FF + g0 * UNIT:]
                    return cut[:, :, bass.ds(col, UNIT)]
                return view
            return src

        def fixed(*views):
            return lambda i: lambda j: views[j]

        wqkv = rows(moba_wqkv[0])
        load(J["q"], plain(wqkv))
        load(J["k"], plain(wqkv, c0=D))
        load(J["v"], plain(wqkv, c0=2 * D))
        load(J["wo"], plain(rows(moba_wo[0])))

        def ffn(layer):
            up, down = rows(ffn_w_up[layer]), rows(ffn_w_down[layer])
            load(J[f"up{layer}a"], gate_up(up, 0))
            load(J[f"dn{layer}a"], plain(down, k0=0, per=HALF_A))
            load(J[f"up{layer}b"], gate_up(up, HALF_A))
            load(J[f"dn{layer}b"], plain(down, k0=4 * HALF_A, per=HALF_B))

        if layers >= 2:
            ffn(0)
        if layers >= 3:
            g1 = rows(rwkv_g1[0])
            g2 = rwkv_g2[0].rearrange("(a p) n -> a p n", p=P)
            load(J["rg"], fixed(g1[:, 0:8, :], g1[:, 8:16, :], g2[0:1].rearrange("a p n -> p a n"),
                                g2[1:2].rearrange("a p n -> p a n")))
            load(J["rv"], plain(rows(rwkv_w_v[0])))
            load(J["rw"], fixed(rows(rwkv_w1[0]), rwkv_w2.rearrange("a p n -> p a n")))
            load(J["ra"], fixed(rows(rwkv_a1[0]), rwkv_a2.rearrange("a p n -> p a n")))
            load(J["rk"], plain(rows(rwkv_w_k[0])))
            load(J["rr"], plain(rows(rwkv_w_r[0])))
            load(J["ro"], plain(rows(rwkv_w_o[0])))
        if layers >= 4:
            ffn(1)
        for tt in range(2):
            sp.wait_ge(out_ready, 8)
            sp.dma_start(out[0, tt * P:(tt + 1) * P, :], xo[:, tt, :]).then_inc(out_done, 16)
        sp.wait_ge(out_done, 32)

    def mix_used(J):
        used = {"rg": [J["rg"].first_panel] * 4}
        jg = J["rg"]
        used["rv"] = [jg.panel_end(0, g // 2) for g in range(4)]
        for name, before in (("rw", "rv"), ("rr", "rk")):
            used[name] = [J[before].panel_end(1, 4 + g) for g in range(4)]
        for name, before in (("ra", "rw"), ("rk", "ra")):
            used[name] = [J[before].panel_end(0, 0)] * 4
        return used

    def flat(t, per):
        dims = len(t.shape) - 1
        v = {2: lambda: t[:, :, :].rearrange("p a b -> p (a b)"),
             3: lambda: t[:, :, :, :].rearrange("p a b c -> p (a b c)")}[dims]()
        return lambda p, a=0, n=per, rows=slice(0, P): v[rows, bass.ds(p * per + a, n)]

    cwp, kbp, abp, kkp = flat(cw, 258), flat(kb, T), flat(ab, T), flat(kkb, T)

    def spread(ap, n):
        return ap.unsqueeze(1).to_broadcast([ap.shape[0], n, ap.shape[1]])

    def blocks(ap, s, half):
        return ap.rearrange("p h (b u s) -> p (h b) u s", u=2, s=s)[:, :, half, :]

    def compact(ap, s):
        return ap.rearrange("p (b s) -> p b s", s=s)

    heads = [(h, slice(h * RH, (h + 1) * RH)) for h in range(2)]

    def Ql(level, c):
        at_ = 4 * (level - 1) + 2 * c
        return Qb[:, at_:at_ + 2, :]

    def core_pe(pe):
        with pe.Fori(0, KT) as p:
            pe.wait_ge(W["v_in"], p * 16 + 16)
            pe.wait_ge(W["scaled"], p * 6 + 6)
            for n, src in enumerate((vb[:, 0:P], vb[:, P:T], bt[:, 0, :], kt_[:, 0, :])):
                mm = pe.transpose(bank(0)[:, n * P:(n + 1) * P], src, C("ident"))
            mm.then_inc(W["turned"], 1)
            for c in range(2):
                for h, r in heads:
                    rhs = ar[:, h, c, :, :].rearrange("p a t -> p (a t)")
                    pe.matmul(bank(1 + c)[:, h * T:(h + 1) * T], bt[:, c, :], rhs, start=True, stop=True)
                    mm = pe.matmul(bank(3 + c)[:, h * T:(h + 1) * T], kt_[:, c, :], rhs, start=True, stop=True)
                mm.then_inc(W["gram"], 1)
            pe.wait_ge(W["bonusp"], p * 2 + 2)
            for c in range(2):
                pe.wait_ge(W["geye"], p * 2 + (c + 1))
                for h, r in heads:
                    mm = pe.matmul(bank(5 + c)[:, h * P:(h + 1) * P], mB[:, c, h, 0:P], C("ident"),
                                   start=True, stop=True)
                mm.then_inc(W["lev0"], 1)
            pe.wait_ge(W["tok"], p + 1)
            pe.wait_ge(W["gmask"], p * 4 + 4)
            for level in range(1, LEVELS + 1):
                s = 1 << level
                for c in range(2):
                    if level == 1:
                        pe.wait_ge(W["x0"], p * 2 + (c + 1))
                    else:
                        pe.wait_ge(W["lxo"], p * 10 + (2 * (level - 2) + c + 1))
                    for h, r in heads:
                        low = blocks(X[:, c, h:h + 1, :], s, 0)
                        mm = pe.matmul(bank(c)[:, h * RH:(h + 1) * RH], mB[:, c, h, 0:P], low, start=True, stop=True)
                    mm.then_inc(W["lp"], 1)
                for c in range(2):
                    pe.wait_ge(W["lq"], p * 12 + (2 * (level - 1) + c + 1))
                    if level == 1:
                        pe.wait_ge(W["xt0"], p * 2 + (c + 1))
                    else:
                        pe.wait_ge(W["lto"], p * 12 + (2 * (level - 2) + c + 1))
                    q = Ql(level, c)
                    if level < LEVELS:
                        for h, r in heads:
                            mm = pe.matmul(bank(2 + c)[:, h * RH:(h + 1) * RH], XT[:, c, h, :],
                                           blocks(q[:, h:h + 1, :], s, 0), start=True, stop=True)
                        mm.then_inc(W["lx"], 1)
                    for h, r in heads:
                        mm = pe.matmul(bank(4 + c)[:, h * RH:(h + 1) * RH], q[:, h, :],
                                       blocks(XT[:, c, h:h + 1, :], s, 1), start=True, stop=True)
                    mm.then_inc(W["lt"], 1)
            pe.wait_ge(W["x0"], p * 2 + 2)
            for c in range(2):
                pe.wait_ge(W["lto"], p * 12 + (10 + c + 1))
                if c:
                    pe.wait_ge(W["sout"], p + 1)
                for h, r in heads:
                    z = bank(6 + c)[:, h * RH:(h + 1) * RH]
                    mm = pe.matmul(z, mK[:, c, h, 0:P], tok[:, c, r], start=True, stop=(c == 0))
                    if c:
                        mm = pe.matmul(z, ar[:, h, 1, 0, :], s0[:, :], start=False, stop=True)
                mm.then_inc(W["zmm"], 1)
                pe.wait_ge(W["zout"], p * 2 + (c + 1))
                for h, r in heads:
                    mm = pe.matmul(bank(6 + c)[:, P + h * RH:P + (h + 1) * RH], XT[:, c, h, :], zb[:, c, h, :],
                                   start=True, stop=True)
                mm.then_inc(W["umm"], 1)
                pe.wait_ge(W["uout"], p * 2 + (c + 1))
                if c == 0:
                    pe.wait_ge(W["lto"], p * 12 + 12)
                    for h, r in heads:
                        pe.matmul(bank(5)[r, 0:RH], tok[:, 2, r], ub[:, 0, h, :], start=True, stop=False)
                        mm = pe.matmul(bank(5)[r, 0:RH], tok[:, 3, r], tok[:, 0, r], start=False, stop=True)
                    mm.then_inc(W["smm"], 1)
            for c in range(2):
                for h, r in heads:
                    y = bank(0)[r, c * P:(c + 1) * P]
                    pe.matmul(y, ub[:, c, h, :], mB[:, c, h, P:2 * P], start=True, stop=False)
                    mm = pe.matmul(y, tok[:, c, r], mK[:, c, h, P:2 * P], start=False, stop=(c == 0))
                    if c:
                        mm = pe.matmul(y, s0[:, :], ar[:, h, 1, 1, :], start=False, stop=True)
            mm.then_inc(W["ymm"], 1)
            pe.matmul(bank(3)[:, 0:T], C("blk"), bp[:, :], start=True, stop=True).then_inc(W["bmm"], 1)
            pe.wait_ge(W["yout"], p + 1)
            pe.matmul(bank(1)[:, 0:T], C("blk"), ys[:, :], start=True, stop=True).then_inc(W["mean"], 1)
            pe.wait_ge(W["csq"], p + 1)
            pe.matmul(bank(2)[:, 0:T], C("blk"), ys[:, :], start=True, stop=True).then_inc(W["var"], 1)

    def core_act(act):
        act.wait_ge(M["cw"], 2 * KT)
        act.wait_ge(M["kb"], 4)
        act.wait_ge(M["r_spilled"], 64)
        with act.Fori(0, KT) as p:
            act.wait_ge(W["hi"], p + 1)
            act.activation(e1[:, :, :].rearrange("p c t -> p (c t)"), cwp(p), ACT.Exp).then_inc(W["exps"], 1)
            act.activation(e2[:, :, :], cwp(p).rearrange("p (c t) -> p c t", c=2)[:, :, 1:129], ACT.Exp,
                           scale=-1.0).then_inc(W["exps"], 1)
            act.activation(scl[:, :], cwp(p, 129, 1), ACT.Exp, bias=cwp(p, 128, 1), scale=-1.0)\
               .then_inc(W["exps"], 1)
            act.wait_ge(W["turned"], p + 1)
            act.copy(tok[:, :, :].rearrange("p a n -> p (a n)"), bank(0)).then_inc(W["tok"], 1)
            for level in range(1, LEVELS + 1):
                for c in range(2):
                    act.wait_ge(W["lt"], p * 12 + (2 * (level - 1) + c + 1))
                    act.copy(blocks(XT[:, c], 1 << level, 1), compact(bank(4 + c)[:, 0:P], 1 << level))\
                       .then_inc(W["lto"], 1)
            for c in range(2):
                act.wait_ge(W["zmm"], p * 2 + (c + 1))
                act.copy(zb[:, c].rearrange("p h v -> p (h v)"), bank(6 + c)[:, 0:P]).then_inc(W["zout"], 1)
                act.wait_ge(W["umm"], p * 2 + (c + 1))
                act.copy(ub[:, c].rearrange("p h v -> p (h v)"), bank(6 + c)[:, P:2 * P]).then_inc(W["uout"], 1)
            act.wait_ge(W["ymm"], p + 1)
            act.copy(ys[:, :], bank(0)[:, 0:T]).then_inc(W["yout"], 1)
            act.wait_ge(W["cent"], p + 1)
            act.activation(ys[:, :], y2[:, :], ACT.Square).then_inc(W["csq"], 1)
            act.wait_ge(W["var"], p + 1)
            act.activation(y3[:, :], bank(2)[:, 0:T], ACT.Sqrt, bias=C("eps", 1, 2), scale=1.0 / RH)\
               .then_inc(W["std"], 1)
            act.wait_ge(W["gate"], p + 1)
            act.copy(hH[:, bass.ds(p, 1), :], y2[:, :].unsqueeze(1)).then_inc(W["hi"], 1)
        act.wait_ge(W["lo"], KT)

    @block.scalar
    def _(act):
        def split(eng, job, i, j):
            job, i, j = next_place(job, i, j)
            act.wait_ge(raw_landed[job.raw[j]], job.landed(i, j))
            act.wait_ge(panel_used, job.panel_end(i, j) - job.hl_gap[j])
            act.copy(wh[:, job.hl[j], :], raw[:, job.raw[j], :]).then_inc(hi_split, 1)

        act.dma_start(cst[:, :], const_all).then_inc(const_in, 16)
        for tt in range(2):
            act.dma_start(xin[:, tt, :], x[0, tt * P:(tt + 1) * P, :]).then_inc(x_in, 16)
        act.dma_start(cr[:, :], const_rope).then_inc(const_in, 16)

        def vec(v):
            return v.rearrange("(t p) -> t p", p=P)

        prows = [(0, 0, vec(moba_norm[0])), (0, 16, vec(rwkv_norm[0])),
                 (0, 32, rwkv_mu[0].rearrange("a (t p) -> (a t) p", p=P))]
        for k, v in enumerate((rwkv_w0, rwkv_a0, rwkv_k_k, rwkv_k_a)):
            prows.append((1, 16 * k, vec(v[0])))
        prows.append((1, 64, rwkv_r_k[0].rearrange("(t h) n -> t (h n)", h=2)))
        prows += [(1, 80, vec(rwkv_lnx_w[0])), (1, 96, vec(rwkv_lnx_b[0]))]
        prows += [(2, 0, ffn_norm.rearrange("a (t p) -> (a t) p", p=P)), (2, 32, moba_q_gain), (2, 33, moba_k_gain)]
        for layer in range(2):
            for k in range(3):
                prows.append((3 + 4 * layer + k, 0, vec(ffn_conv_w[layer, k])))
            prows.append((6 + 4 * layer, 0, vec(ffn_conv_b[layer])))
        assert len(prows) == ROW_LOADS
        for tile, r0, src in prows:
            act.dma_start(prow[r0:r0 + src.shape[0], tile, :], src).then_inc(rows_in, 16)

        split(act, J["q"], 0, 0)
        for g in range(8):
            act.wait_ge(turned, g + 1)
            act.copy(xT[:, 2 * g:2 * g + 2, :], bank(4 + g % 4)).then_inc(turned_out, 1)
            if g % 2:
                act.wait_ge(turned_out, g + 1)
                q = g // 2
                if q >= 2:
                    act.wait_ge(N["n0"]["summed"], q - 1)
                act.activation(quad((sqacc if q == 0 else sq)[:, :]), xT[:, 4 * q:4 * q + 4, :],
                               ACT.Square).then_inc(N["n0"]["squared"], 1)
        for g, tiles in enumerate(((0, 1, 2), (3, 4, 5, 6), (7, 8, 9, 10))):
            act.wait_ge(turned, 9 + g)
            cols = {0: (0, 240 + 34), 1: (PCV, 4 * 88), 2: (PCV + 4 * 88, 4 * 88)}[g]
            act.copy(prm[:, cols[0]:cols[0] + cols[1]], bank(4 + g)[:, 0:cols[1]]).then_inc(turned_out, 1)

        def norm_root(n):
            act.wait_ge(N[n]["total"], 1)
            act.activation(rstd[:, :], aux[0][:, 0:T], ACT.Sqrt, bias=C("eps", 0, 1), scale=1.0 / D)\
               .then_inc(N[n]["rooted"], 1)

        def norm_hi(n, g, before):
            act.wait_ge(N[n]["normed"], 4 * (g + 1))
            act.wait_ge(panel_used, before)
            act.copy(hH[:, 4 * g:4 * g + 4, :], quad(hf[:, g % 2, :])).then_inc(N[n]["hi"], 1)

        norm_root("n0")
        norm_hi("n0", 0, SEED)

        def take_qkv(job, part, w):
            def step(i):
                act.wait_ge(panel_used, job.panel_end(i, 4 * w + 3))
                act.copy(QKV[:, bass.ds(part * KT + i * 8 + 4 * w, 4), :], quad(acc[job.unit(0, w) % 2][:, :]))\
                   .then_inc(unit_out, 1)
            return step

        def qk_square(which, w):
            def step(i):
                n = 4 * which + 2 * i + w
                act.wait_ge(unit_out, J["qk"[which]].unit_end(i, w))
                if n >= 2:
                    act.wait_ge(qk["summed"], n - 1)
                act.activation(quad(sq2[:, w, :]), QKV[:, bass.ds(which * KT + i * 8 + 4 * w, 4), :],
                               ACT.Square).then_inc(qk["squared"], 1)
            return step

        def qk_root(which, w):
            def step(i):
                n = 4 * which + 2 * i + w
                act.wait_ge(qk["summed"], n + 1)
                if n >= 2:
                    act.wait_ge(qk["inverse"], n - 1)
                act.activation(ssr[:, w, :], aux[0][0:4, w * 512:w * 512 + T], ACT.Sqrt,
                               bias=C("eps", 0, 1, p=4), scale=1.0 / HD).then_inc(qk["rooted"], 1)
            return step

        jq, jk, jv, jo = (J[k] for k in ("q", "k", "v", "wo"))
        run(act, jq, split, first={0: [lambda: norm_hi("n0", 1, SEED)], 1: [lambda: norm_hi("n0", 2, SEED)],
                                   2: [lambda: norm_hi("n0", 3, SEED)]},
            every={3: [take_qkv(jq, 0, 0)], 7: [take_qkv(jq, 0, 1)]})
        for which, job in ((0, jk), (1, jv)):
            run(act, job, split, every={0: [qk_square(which, 0)], 1: [qk_root(which, 0), qk_square(which, 1)],
                                        2: [qk_root(which, 1)], 3: [take_qkv(job, 1 + which, 0)],
                                        7: [take_qkv(job, 1 + which, 1)]})
        act.wait_ge(qk["roped"], 9)
        act.wait_ge(unit_out, jv.unit_end(1, 1))
        with act.Fori(0, NH // 2) as i:
            for b in range(2):
                act.wait_ge(at["mixed"], 2 * i + b + 1)
                act.copy(qs[:, b, :], QKV[:, bass.ds(2 * i + b, 1), :]).then_inc(at["staged"], 1)
                act.copy(vs[:, b, :], QKV[:, bass.ds(2 * KT + 2 * i + b, 1), :]).then_inc(at["staged"], 1)
            for b in range(2):
                act.wait_ge(at["vturned"], 2 * i + b + 1)
                act.copy(vt[:, b, :], aux[b][:, 512:512 + T]).then_inc(at["vout"], 1)
            for b in range(2):
                for t, (a, e) in enumerate(((0, P), (P, 3 * P))):
                    act.wait_ge(at["neg"], 2 * i + b + 1)
                    act.activation(ex[:, b, a:e], sc[:, b, a:e], ACT.Exp, bias=st[:, b, 2 + t:3 + t],
                                   scale=HD ** -0.5, accum_out=st[:, b, 4 + t:5 + t]).then_inc(at["exped"], 1)
            for b in range(2):
                act.wait_ge(at["pturned"], 2 * i + b + 1)
                act.copy(pT[:, b, :], aux[b][:, 512:512 + 384]).then_inc(at["pout"], 1)
            for b in range(2):
                act.wait_ge(at["mixed"], 2 * i + b + 3)
                act.copy(hH[:, bass.ds(2 * i + b, 1), :], acc[b][:, 0:T]).then_inc(at["hi"], 1)

        def square(n, job, u):
            i, w = divmod(u, 2)

            def step(*_):
                act.wait_ge(unit_out, job.unit_end(i, w))
                if u >= 2:
                    act.wait_ge(N[n]["summed"], u - 1)
                act.activation(quad((sqacc if u == 0 else sq)[:, :]), xT[:, 4 * u:4 * u + 4, :],
                               ACT.Square).then_inc(N[n]["squared"], 1)
            return step

        def residual(n, job, first=None):
            a, b = job.units[0], job.m
            steps = dict(first or {})
            if n is None:
                run(act, job, split, first=steps)
                return
            steps.setdefault(a, []).append(square(n, job, 0))
            run(act, job, split, first=steps,
                late={0: [square(n, job, 1)]}, last={a: [square(n, job, 2)]})
            square(n, job, 3)()

        after = {"n1": "wo", "n3": "ro"}

        def ffn(layer):
            n = ("n1", "n3")[layer]
            ja, da, jb, db = (J[f"{k}{layer}{h}"] for k, h in (("up", "a"), ("dn", "a"), ("up", "b"), ("dn", "b")))
            norm_root(n)
            done = ja.first_panel
            norm_hi(n, 0, done)

            def steps(job, g0):
                u0 = layer * (HALF_A + HALF_B) + g0
                cw0 = PCV + layer * 4 * 88

                def take(w):
                    def step(i):
                        act.wait_ge(panel_used, job.panel_end(i, 4 * w + 3))
                        if not (u0 == 0 and w == 0 and isinstance(i, int)):
                            act.wait_ge(f["tap0"], (2 * (i + u0) + w) * 4)
                        act.copy(fu[:, :], acc[job.unit(0, w) % 2][:, :]).then_inc(unit_out, 1)
                    return step

                def init(w):
                    def step(i):
                        act.wait_ge(unit_out, job.unit_end(i, w))
                        if w:
                            act.wait_ge(f["silu"], i + u0 + 1)
                        elif not (u0 == 0 and isinstance(i, int)):
                            act.wait_ge(f["lo"], i + u0)
                        for k in range(4):
                            c = i * 4 + (g0 * 4 + w * FKT + k)
                            act.activation(fc[:, k * T:(k + 1) * T], fu[:, k * T:(k + 1) * T], ACT.Identity,
                                           bias=prm[:, bass.ds(c + (cw0 + 3 * 88), 1)],
                                           scale=prm[:, bass.ds(c + (cw0 + 2 * 88), 1)]).then_inc(f["init"], 1)
                    return step

                def silu(i):
                    act.wait_ge(f["tap0"], (2 * (i + u0)) * 4 + 4)
                    if not (u0 == 0 and isinstance(i, int)):
                        act.wait_ge(f["gated"], i + u0)
                    act.activation(sg[:, :], fc[:, :], ACT.Silu).then_inc(f["silu"], 1)

                def hi(i):
                    act.wait_ge(f["gated"], i + (u0 + 1))
                    act.copy(aH[:, bass.ds(i * 4, 4), :], quad(fc[:, :])).then_inc(f["hi"], 1)

                return ({3: [take(0)], 4: [init(0)], 5: [silu], 7: [take(1)]}, {0: [init(1)], 2: [hi]})

            for job, dn, g0 in ((ja, da, 0), (jb, db, HALF_A)):
                every, late = steps(job, g0)
                first = {}
                if g0 == 0:
                    first = {k: [lambda k=k: norm_hi(n, k + 1, done)] for k in range(3)}
                else:
                    first = {}
                run(act, job, split, first=first, every=every, late=late)
                tail = {j: [lambda g=g, job=job: g(job.n - 1) for g in fs] for j, fs in late.items()}
                residual(("n2" if layer == 0 and layers >= 3 else None) if g0 else None, dn, first=tail)

        residual("n1" if layers >= 2 else None, jo)
        if layers >= 2:
            ffn(0)

        if layers >= 3:
            norm_root("n2")
            mixes = {"rg": 5, "rv": 3, "rw": 1, "ra": 4, "rk": 2, "rr": 0}
            order_mix = list(mixes)

            def mix_hi(name, g, used):
                n = 4 * order_mix.index(name) + g

                def step(*_):
                    act.wait_ge(M["mixed"], 4 * n + 4)
                    act.wait_ge(panel_used, used)
                    act.copy(hH[:, 4 * g:4 * g + 4, :], quad(mt[:, :])).then_inc(M["hi"], 1)
                return step

            used = mix_used(J)
            for g in range(4):
                mix_hi("rg", g, used["rg"][g])()
            jg = J["rg"]
            split(act, jg, 0, 1)
            split(act, jg, 0, 2)

            def low_rank(job, panels, parts, width, func):
                k = ("rg", "rw", "ra").index(job.name)
                act.wait_ge(panel_used, job.panel_end(0, panels - 1))
                if k == 1:
                    act.wait_ge(M["v_spilled"], 64)
                if k:
                    act.wait_ge(M["low_lo"], k)
                act.activation(ru[0:parts, 0:width], acc[job.unit(0, 0) % 2][0:parts, 0:width], func)\
                   .then_inc(unit_out, 1)
                act.wait_ge(unit_out, job.unit_end(0, 0))
                act.copy(tH[0:parts, 0:width // T, :], ru[0:parts, 0:width].rearrange("p (f t) -> p f t", t=T))\
                   .then_inc(M["low_hi"], 1)

            low_rank(jg, 2, P, 2 * T, ACT.Sigmoid)
            split(act, jg, 0, 3)
            for u in range(4):
                if u == 3:
                    split(act, jg, 0, 4)
                act.wait_ge(M["low_unit"], u + 1)
                act.wait_ge(M["low_lo"], 1)
                if u:
                    act.wait_ge(M["g_spilled"], 16 * u)
                act.copy(ru[:, :], acc[jg.unit(0, 1 + u) % 2][:, :]).then_inc(unit_out, 1)

            def take_spill(job, done, before, w):
                def step(i):
                    u = 2 * i + w
                    act.wait_ge(panel_used, job.panel_end(i, 4 * w + 3))
                    if u:
                        act.wait_ge(M[done], 16 * u)
                    else:
                        act.wait_ge(before[0], before[1])
                    act.copy(ru[:, :], acc[job.unit(0, w) % 2][:, :]).then_inc(unit_out, 1)
                return step

            mix_hi("rv", 0, used["rv"][0])()
            run(act, J["rv"], split, first={k: [mix_hi("rv", k + 1, used["rv"][k + 1])] for k in range(3)},
                every={3: [take_spill(J["rv"], "v_spilled", (M["g_spilled"], 64), 0)],
                       7: [take_spill(J["rv"], "v_spilled", None, 1)]})
            for name, func, bias in (("rw", ACT.Tanh, W0), ("ra", ACT.Copy, A0)):
                job = J[name]
                for g in range(4):
                    mix_hi(name, g, used[name][g])()
                split(act, job, 0, 1)
                low_rank(job, 1, LORA, T, func)
                for u in range(4):
                    if u == 3:
                        split(act, job, 0, 2)
                    act.wait_ge(M["low_unit"], 4 + (4 if name == "ra" else 0) + u + 1)
                    for k in range(4):
                        ft = 4 * u + k
                        src = acc[job.unit(0, 1 + u) % 2][:, k * T:(k + 1) * T]
                        dst = ab[:, ft, :]
                        if name == "rw":
                            src, dst = src.rearrange("p (c t) -> p c t", c=2), cw[:, ft, :, 1:129]
                        ins = act.activation(dst, src, ACT.Sigmoid, bias=prm[:, bias + ft:bias + ft + 1])
                    ins.then_inc(unit_out, 1)

            def take_k(w):
                def step(i):
                    job = J["rk"]
                    act.wait_ge(panel_used, job.panel_end(i, 4 * w + 3))
                    act.copy(kb[:, 8 * i + 4 * w:8 * i + 4 * w + 4, :], quad(acc[job.unit(0, w) % 2][:, :]))\
                       .then_inc(unit_out, 1)
                return step

            mix_hi("rk", 0, used["rk"][0])()
            run(act, J["rk"], split, first={k: [mix_hi("rk", k + 1, used["rk"][k + 1])] for k in range(3)},
                every={3: [take_k(0)], 7: [take_k(1)]})
            mix_hi("rr", 0, used["rr"][0])()

            def kk_square(w):
                def step(i):
                    u = 2 * i + w
                    act.wait_ge(unit_out, J["rk"].unit_end(i, w))
                    act.wait_ge(M["lo"], 24)
                    if u >= 2:
                        act.wait_ge(M["kk"], u - 1)
                    for k in range(4):
                        ft = 4 * u + k
                        act.activation(kkr[:, w, k * T:(k + 1) * T], kb[:, ft, :], ACT.Copy,
                                       scale=prm[:, K_K + ft:K_K + ft + 1]).then_inc(M["kkr"], 1)
                    if u:
                        act.wait_ge(M["ksum"], u)
                    act.wait_ge(M["kkr"], 4 * u + 4)
                    act.activation(kq[:, :], kkr[:, w, :], ACT.Square).then_inc(M["ksq"], 1)
                return step

            def kk_root(w):
                def step(i):
                    u = 2 * i + w
                    act.wait_ge(M["ksum"], u + 1)
                    if u >= 2:
                        act.wait_ge(M["krec"], u - 1)
                    act.activation(kss[:, w, :], aux[0][0:8, w * 512:w * 512 + T], ACT.Sqrt)\
                       .then_inc(M["kroot"], 1)
                return step

            run(act, J["rr"], split, first={k: [mix_hi("rr", k + 1, used["rr"][k + 1])] for k in range(3)},
                every={3: [kk_square(0), take_spill(J["rr"], "r_spilled", (M["v_spilled"], 64), 0)],
                       4: [kk_root(0), kk_square(1)], 5: [kk_root(1)],
                       7: [take_spill(J["rr"], "r_spilled", None, 1)]})
            core_act(act)
            residual("n3" if layers >= 4 else None, J["ro"])
        if layers >= 4:
            ffn(1)
        for g in range(8):
            act.wait_ge(out_turned, g + 1)
            act.copy(xo[:, :, 2 * P * g:2 * P * (g + 1)].rearrange("p t (k q) -> p k t q", q=P),
                     bank(4 + g % 4).rearrange("p (k t q) -> p k t q", k=2, q=P)).then_inc(out_ready, 1)

    @block.vector
    def _(dve):
        def split(eng, job, i, j):
            job, i, j = next_place(job, i, j)
            dve.wait_ge(hi_split, job.panel_end(i, j))
            dve.tensor_tensor(wl[:, job.hl[j], :], raw[:, job.raw[j], :], wh[:, job.hl[j], :].bitcast(f32),
                              ALU.subtract).then_inc(lo_split, 1)

        def norm_rstd(n, units=4):
            dve.wait_ge(N[n]["rooted"], 1)
            dve.reciprocal(rstd[:, :], rstd[:, :]).then_inc(N[n]["rstd"], 1)

        def norm_group(n, g, gain):
            dve.wait_ge(N[n]["rstd"], 1)
            if g >= 2:
                dve.wait_ge(N[n]["lo"], g - 1)
            for k in range(4):
                kt = 4 * g + k
                dve.scalar_tensor_tensor(hf[:, g % 2, k * T:(k + 1) * T], xT[:, kt, :],
                                         prm[:, gain + kt:gain + kt + 1], rstd[:, :], ALU.mult, ALU.mult)\
                   .then_inc(N[n]["normed"], 1)
            dve.wait_ge(N[n]["hi"], g + 1)
            dve.tensor_tensor(hL[:, 4 * g:4 * g + 4, :], quad(hf[:, g % 2, :]),
                              hH[:, 4 * g:4 * g + 4, :].bitcast(f32), ALU.subtract).then_inc(N[n]["lo"], 1)

        def add_squares(n, u):
            def step(*_):
                dve.wait_ge(N[n]["squared"], u + 1)
                if u >= 2:
                    dve.wait_ge(N[n]["summed"], u - 1)
                dve.tensor_tensor(sqacc[:, :], sqacc[:, :], sq[:, :], ALU.add).then_inc(N[n]["summed"], 1)
            return step

        split(dve, J["q"], 0, 0)
        for u in range(1, 4):
            add_squares("n0", u)()
        dve.wait_ge(turned_out, 11)
        dve.tensor_scalar(prm[:, OMKA:OMKA + 16], prm[:, K_A:K_A + 16], -1.0, 1.0, ALU.mult, ALU.add)\
           .then_inc(omka_done, 1)
        norm_rstd("n0")
        norm_group("n0", 0, G_MOBA)

        def qk_inverse(which, w):
            def step(i):
                n = 4 * which + 2 * i + w
                dve.wait_ge(qk["rooted"], n + 1)
                if n >= 2:
                    dve.wait_ge(qk["spread"], n - 1)
                dve.reciprocal(rsr[:, w, :], ssr[:, w, :]).then_inc(qk["inverse"], 1)
            return step

        def qk_norm(which, w):
            def step(i):
                n = 4 * which + 2 * i + w
                dve.wait_ge(qk["spread"], n + 1)
                for k in range(4):
                    dve.scalar_tensor_tensor(nrmd[:, k * T:(k + 1) * T], QKV[:, which * KT + i * 8 + (4 * w + k), :],
                                             prm[:, (QG, KG)[which]:(QG, KG)[which] + 1],
                                             aux[1][:, k * T:(k + 1) * T], ALU.mult, ALU.mult)\
                       .then_inc(qk["normed"], 1)
            return step

        def qk_rope(which, w):
            def step(i):
                n = 4 * which + 2 * i + w
                part = QKV[:, which * KT + i * 8 + 4 * w:which * KT + i * 8 + 4 * w + 4, :]
                dve.wait_ge(qk["turned"], n + 1)
                dve.wait_ge(qk["normed"], 4 * n + 4)
                dve.wait_ge(qk["roped"], n + 1)
                dve.tensor_tensor(quad(rot[:, :]), quad(aux[0][:, :]), spread(R("sin"), 4), ALU.mult)\
                   .then_inc(qk["sined"], 1)
                dve.tensor_tensor(part, quad(nrmd[:, :]), spread(R("cos"), 4), ALU.mult).then_inc(qk["cosed"], 1)
                dve.wait_ge(qk["sined"], n + 1)
                dve.wait_ge(qk["cosed"], n + 1)
                dve.tensor_tensor(part, part, quad(rot[:, :]), ALU.add).then_inc(qk["roped"], 1)
            return step

        jq, jk, jv, jo = (J[k] for k in ("q", "k", "v", "wo"))
        run(dve, jq, split, first={g: [lambda g=g: norm_group("n0", g + 1, G_MOBA)] for g in range(3)})
        for which, job in ((0, jk), (1, jv)):
            run(dve, job, split, every={1: [qk_inverse(which, 0)], 2: [qk_inverse(which, 1)],
                                        3: [qk_norm(which, 0)], 4: [qk_rope(which, 0)],
                                        5: [qk_norm(which, 1)], 6: [qk_rope(which, 1)]})
        with dve.Fori(0, NH // 2) as i:
            for b in range(2):
                dve.wait_ge(at["scored"], 2 * i + (b + 1))
                dve.tensor_tensor(sc[:, b, :], aux[b][:, 0:384], R("cmask"), ALU.add).then_inc(at["masked"], 1)
                dve.wait_ge(at["masked"], 2 * i + (b + 1))
                for t, (a, e) in enumerate(((0, P), (P, 3 * P))):
                    dve.reduce_max(st[:, b, t:t + 1], sc[:, b, a:e], AX.X).then_inc(at["maxed"], 1)
                dve.wait_ge(at["maxed"], 4 * i + (2 * b + 2))
                dve.tensor_scalar(st[:, b, 2:4], st[:, b, 0:2], -(HD ** -0.5), None, ALU.mult)\
                   .then_inc(at["neg"], 1)
            for b in range(2):
                dve.wait_ge(at["exped"], 4 * i + (2 * b + 2))
                dve.reciprocal(st[:, b, 6:8], st[:, b, 4:6]).then_inc(at["recip"], 1)
                dve.wait_ge(at["recip"], 2 * i + (b + 1))
                for t, (a, e) in enumerate(((0, P), (P, 3 * P))):
                    dve.tensor_scalar(ex[:, b, a:e], ex[:, b, a:e], st[:, b, 6 + t:7 + t], None, ALU.mult)\
                       .then_inc(at["probs"], 1)
            for b in range(2):
                dve.wait_ge(at["hi"], 2 * i + (b + 1))
                dve.tensor_tensor(hL[:, bass.ds(2 * i + b, 1), :], acc[b][:, 0:T].unsqueeze(1),
                                  hH[:, bass.ds(2 * i + b, 1), :].bitcast(f32), ALU.subtract).then_inc(at["lo"], 1)

        def add_unit(job, n, before):
            def step(w):
                def go(i):
                    dve.wait_ge(panel_used, job.panel_end(i, job.last_panel[w]))
                    if before:
                        before()
                    u = 2 * i + w
                    part = xT[:, 4 * u:4 * u + 4, :]
                    dve.tensor_tensor(part, part, quad(acc[job.unit(0, w) % 2][:, :]), ALU.add)\
                       .then_inc(unit_out, 1)
                return go
            return step

        def residual(n, job, first=None, before=None):
            a, m = job.units[0], job.m
            add = add_unit(job, n, before)
            steps = {k: list(v) for k, v in (first or {}).items()}
            if n is None:
                run(dve, job, split, first=steps, every={a - 1: [add(0)], m - 1: [add(1)]})
                return
            run(dve, job, split, first=steps, every={a - 1: [add(0)], m - 1: [add(1)]},
                late={1: [add_squares(n, 1)]}, last={a: [add_squares(n, 2)]})
            add_squares(n, 3)()

        def ffn(layer):
            n = ("n1", "n3")[layer]
            gain = G_FFN + 16 * layer
            ja, da, jb, db = (J[f"{k}{layer}{h}"] for k, h in (("up", "a"), ("dn", "a"), ("up", "b"), ("dn", "b")))
            norm_rstd(n)
            norm_group(n, 0, gain)

            def steps(job, g0):
                u0 = layer * (HALF_A + HALF_B) + g0
                cw0 = PCV + layer * 4 * 88

                def conv(w):
                    def step(i):
                        t0 = (2 * (i + u0) + w) * 4
                        for name, tap in (("tap1", 1), ("tap0", 2)):
                            for k in range(4):
                                a, e = k * T, (k + 1) * T
                                if tap == 1:
                                    dve.wait_ge(f["init"], t0 + (k + 1))
                                else:
                                    dve.wait_ge(f["tap1"], t0 + (k + 1))
                                c = i * 4 + (g0 * 4 + w * FKT + k + cw0 + (2 - tap) * 88)
                                dve.scalar_tensor_tensor(fc[:, a + tap:e], fu[:, a:e - tap],
                                                         prm[:, bass.ds(c, 1)], fc[:, a + tap:e],
                                                         ALU.mult, ALU.add).then_inc(f[name], 1)
                    return step

                def gate(i):
                    dve.wait_ge(f["silu"], i + (u0 + 1))
                    dve.wait_ge(f["tap0"], i * 8 + (8 * u0 + 8))
                    dve.tensor_tensor(fc[:, :], fc[:, :], sg[:, :], ALU.mult).then_inc(f["gated"], 1)

                def lo(i):
                    dve.wait_ge(f["hi"], i + (u0 + 1))
                    dve.tensor_tensor(aL[:, bass.ds(i * 4, 4), :], quad(fc[:, :]),
                                      aH[:, bass.ds(i * 4, 4), :].bitcast(f32), ALU.subtract).then_inc(f["lo"], 1)

                return {4: [conv(0)]}, {0: [conv(1)], 1: [gate], 2: [lo]}

            for job, dn, g0 in ((ja, da, 0), (jb, db, HALF_A)):
                every, late = steps(job, g0)
                first = {}
                if g0 == 0:
                    first = {g: [lambda g=g: norm_group(n, g + 1, gain)] for g in range(3)}
                run(dve, job, split, first=first, every=every, late=late)
                tail = {j: [lambda g=g, job=job: g(job.n - 1) for g in fs] for j, fs in late.items()}
                residual(("n2" if layer == 0 and layers >= 3 else None) if g0 else None, dn, first=tail)

        residual("n1" if layers >= 2 else None, jo)
        if layers >= 2:
            ffn(0)

        if layers >= 3:
            norm_rstd("n2")
            dve.wait_ge(N["n2"]["rstd"], 1)
            for kt in range(KT):
                dve.scalar_tensor_tensor(hb[:, kt, :], xT[:, kt, :], prm[:, G_RWKV + kt:G_RWKV + kt + 1], rstd[:, :],
                                         ALU.mult, ALU.mult).then_inc(M["h"], 1)
            for g in range(4):
                a, e = 4 * g, 4 * g + 4
                dve.wait_ge(M["h"], e)
                dve.tensor_scalar(xx[:, a:e, 0:1], hb[:, a:e, 0:1], -1.0, None, ALU.mult).then_inc(M["xx"], 1)
                dve.tensor_tensor(xx[:, a:e, 1:T], hb[:, a:e, 0:T - 1], hb[:, a:e, 1:T], ALU.subtract)\
                   .then_inc(M["xx"], 1)
            mixes = {"rg": 5, "rv": 3, "rw": 1, "ra": 4, "rk": 2, "rr": 0}
            order_mix = list(mixes)

            def mix(name, g):
                n = 4 * order_mix.index(name) + g

                def step(*_):
                    dve.wait_ge(M["xx"], 2 * g + 2)
                    if n:
                        dve.wait_ge(M["lo"], n)
                    for k in range(4):
                        kt = 4 * g + k
                        col = MU + 16 * mixes[name] + kt
                        dve.scalar_tensor_tensor(mt[:, k * T:(k + 1) * T], xx[:, kt, :], prm[:, col:col + 1],
                                                 hb[:, kt, :], ALU.mult, ALU.add).then_inc(M["mixed"], 1)
                    dve.wait_ge(M["hi"], n + 1)
                    dve.tensor_tensor(hL[:, 4 * g:4 * g + 4, :], quad(mt[:, :]),
                                      hH[:, 4 * g:4 * g + 4, :].bitcast(f32), ALU.subtract).then_inc(M["lo"], 1)
                return step

            def low_lo(k, parts, width):
                dve.wait_ge(M["low_hi"], k + 1)
                dve.tensor_tensor(tL[0:parts, 0:width // T, :],
                                  ru[0:parts, 0:width].rearrange("p (f t) -> p f t", t=T),
                                  tH[0:parts, 0:width // T, :].bitcast(f32), ALU.subtract).then_inc(M["low_lo"], 1)

            jg = J["rg"]
            for g in range(4):
                mix("rg", g)()
            split(dve, jg, 0, 1)
            split(dve, jg, 0, 2)
            low_lo(0, P, 2 * T)
            split(dve, jg, 0, 3)
            split(dve, jg, 0, 4)
            mix("rv", 0)()
            run(dve, J["rv"], split, first={k: [mix("rv", k + 1)] for k in range(3)})
            dve.memset(cw[:, :, :, 0:1], 0.0).then_inc(M["zeroed"], 1)
            for k, name in ((1, "rw"), (2, "ra")):
                for g in range(4):
                    mix(name, g)()
                split(dve, J[name], 0, 1)
                low_lo(k, LORA, T)
                split(dve, J[name], 0, 2)

            def decay_sum(j):
                def step(i):
                    ft = 8 * i + j
                    dve.wait_ge(unit_out, J["rw"].unit_end(0, 1 + ft // 4))
                    dve.wait_ge(M["zeroed"], 1)
                    for c in range(2):
                        dve.tensor_tensor_scan(cw[:, ft, c, 1:129], C("ones"), cw[:, ft, c, 1:129], 0.0,
                                               ALU.mult, ALU.add).then_inc(M["scan"], 1)
                    dve.wait_ge(M["scan"], 2 * ft + 2)
                    if ft:
                        dve.wait_ge(M["cw"], 2 * ft)
                    dve.tensor_copy(mid[:, 0:2].unsqueeze(2), cw[:, ft, :, 64:65]).then_inc(M["mid"], 1)
                    dve.wait_ge(M["mid"], ft + 1)
                    for c in range(2):
                        dve.tensor_scalar(cw[:, ft, c, :], cw[:, ft, c, :], mid[:, c:c + 1], -EXPM05,
                                          ALU.subtract, ALU.mult).then_inc(M["cw"], 1)
                return step

            mix("rk", 0)()
            run(dve, J["rk"], split, first={k: [mix("rk", k + 1)] for k in range(3)},
                every={j: [decay_sum(j)] for j in range(8)})
            mix("rr", 0)()

            def kk_inverse(w):
                def step(i):
                    u = 2 * i + w
                    dve.wait_ge(M["kroot"], u + 1)
                    if u >= 2:
                        dve.wait_ge(M["kspread"], u - 1)
                    dve.tensor_scalar(kss[:, w, :], kss[:, w, :], 1e-12, None, ALU.max).then_inc(M["kmax"], 1)
                    dve.wait_ge(M["kmax"], u + 1)
                    dve.reciprocal(krs[:, w, :], kss[:, w, :]).then_inc(M["krec"], 1)
                return step

            def kk_finish(w):
                def step(i):
                    u = 2 * i + w
                    a, e = 4 * u, 4 * u + 4
                    dve.wait_ge(M["kspread"], u + 1)
                    dve.tensor_tensor(kkb[:, a:e, :], quad(aux[1][:, :]), quad(kkr[:, w, :]), ALU.mult)\
                       .then_inc(M["kk"], 1)
                    dve.wait_ge(M["lo"], 24)
                    if u:
                        dve.wait_ge(M["kmod"], u)
                    dve.wait_ge(unit_out, J["ra"].unit_end(0, 4))
                    for k in range(4):
                        ft = 4 * u + k
                        dve.tensor_scalar(mt[:, k * T:(k + 1) * T], ab[:, ft, :], prm[:, K_A + ft:K_A + ft + 1],
                                          prm[:, OMKA + ft:OMKA + ft + 1], ALU.mult, ALU.add).then_inc(M["kfac"], 1)
                    dve.wait_ge(M["kfac"], 4 * u + 4)
                    dve.tensor_tensor(kb[:, a:e, :], kb[:, a:e, :], quad(mt[:, :]), ALU.mult).then_inc(M["kmod"], 1)
                    dve.wait_ge(M["kk"], u + 1)
                    dve.tensor_tensor(ab[:, a:e, :], ab[:, a:e, :], kkb[:, a:e, :], ALU.mult).then_inc(M["kb"], 1)
                return step

            run(dve, J["rr"], split, first={k: [mix("rr", k + 1)] for k in range(3)},
                every={4: [kk_inverse(0)], 5: [kk_inverse(1)], 6: [kk_finish(0)], 7: [kk_finish(1)]})

            dve.wait_ge(M["x_spilled"], 16)
            dve.tensor_copy(Qb[:, :, :], spread(C("ident"), LEVELS * 4)).then_inc(W["zeroed"], 1)
            dve.wait_ge(M["kb"], 4)
            dve.wait_ge(M["r_spilled"], 64)
            dve.memset(ar[:, :, :, :, :].rearrange("p h c a t -> p (h c a t)"), 0.0).then_inc(W["zeroed"], 1)
            dve.wait_ge(W["zeroed"], 2)
            with dve.Fori(0, KT) as p:
                dve.wait_ge(W["exps"], p * 3 + 3)
                for h, r in heads:
                    dve.scalar_tensor_tensor(ar[r, h, :, 0, :], kkp(p, rows=r).rearrange("p (c t) -> p c t", c=2),
                                             -1.0, e1[r, :, 0:P], ALU.mult, ALU.mult).then_inc(W["scaled"], 1)
                dve.tensor_tensor(bt[:, :, :], abp(p).rearrange("p (c t) -> p c t", c=2), e2[:, :, :], ALU.mult)\
                   .then_inc(W["scaled"], 1)
                dve.tensor_tensor(kt_[:, :, :], kbp(p).rearrange("p (c t) -> p c t", c=2), e2[:, :, :], ALU.mult)\
                   .then_inc(W["scaled"], 1)
                dve.wait_ge(W["r_in"], p * 16 + 16)
                for h, r in heads:
                    dve.tensor_tensor(ar[r, h, :, 1, :], rb[r, :].rearrange("p (c t) -> p c t", c=2),
                                      e1[r, :, 1:129], ALU.mult).then_inc(W["scaled"], 1)
                dve.wait_ge(W["scaled"], p * 6 + 6)
                for h, r in heads:
                    dve.scalar_tensor_tensor(bp[r, :].rearrange("p (c t) -> p c t", c=2), ar[r, h, :, 1, :],
                                             prm[r, bass.ds(p + R_K, 1)], kt_[r, :, :], ALU.mult, ALU.mult)\
                       .then_inc(W["bonusp"], 1)
                for c in range(2):
                    dve.wait_ge(W["gram"], p * 2 + (c + 1))
                    dve.tensor_tensor(mB[:, c], bank(1 + c).rearrange("p (h n) -> p h n", h=2), spread(C("mb"), 2),
                                      ALU.mult).then_inc(W["gmask"], 1)
                    dve.tensor_tensor(mK[:, c], bank(3 + c).rearrange("p (h n) -> p h n", h=2), spread(C("mk"), 2),
                                      ALU.mult).then_inc(W["gmask"], 1)
                for c in range(2):
                    dve.wait_ge(W["gmask"], p * 4 + (2 * c + 1))
                    dve.tensor_tensor(mB[:, c, :, 0:P], mB[:, c, :, 0:P], spread(C("ident"), 2), ALU.add)\
                       .then_inc(W["geye"], 1)
                for c in range(2):
                    dve.wait_ge(W["geye"], p * 2 + (c + 1))
                    dve.tensor_tensor(XT[:, c], mB[:, c, :, 0:P], spread(C("mx1t"), 2), ALU.mult)\
                       .then_inc(W["xt0"], 1)
                for c in range(2):
                    dve.wait_ge(W["lev0"], p * 2 + (c + 1))
                    dve.tensor_tensor(X[:, c], bank(5 + c)[:, 0:T].rearrange("p (h n) -> p h n", h=2),
                                      spread(C("mx1"), 2), ALU.mult).then_inc(W["x0"], 1)
                for level in range(1, LEVELS + 1):
                    s = 1 << level
                    lv = C("lv", P * (level - 1), P * level)
                    for c in range(2):
                        dve.wait_ge(W["lp"], p * 12 + (2 * (level - 1) + c + 1))
                        dve.tensor_tensor(blocks(Ql(level, c), s, 0), compact(bank(c)[:, 0:P], s), compact(lv, s),
                                          ALU.mult).then_inc(W["lq"], 1)
                    if level < LEVELS:
                        for c in range(2):
                            dve.wait_ge(W["lx"], p * 10 + (2 * (level - 1) + c + 1))
                            dve.tensor_copy(blocks(X[:, c], s, 0), compact(bank(2 + c)[:, 0:P], s))\
                               .then_inc(W["lxo"], 1)
                dve.wait_ge(W["smm"], p + 1)
                dve.tensor_scalar(s0[:, :], bank(5)[:, 0:RH], scl[:, 0:1], None, ALU.mult).then_inc(W["sout"], 1)
                dve.wait_ge(W["mean"], p + 1)
                dve.scalar_tensor_tensor(y2[:, :], bank(1)[:, 0:T], -1.0 / RH, ys[:, :], ALU.mult, ALU.add)\
                   .then_inc(W["cent"], 1)
                dve.wait_ge(W["std"], p + 1)
                dve.reciprocal(y3[:, :], y3[:, :]).then_inc(W["rec"], 1)
                dve.wait_ge(W["rec"], p + 1)
                dve.wait_ge(W["cent"], p + 1)
                dve.tensor_tensor(y2[:, :], y2[:, :], y3[:, :], ALU.mult).then_inc(W["norm"], 1)
                dve.wait_ge(W["norm"], p + 1)
                dve.tensor_scalar(y2[:, :], y2[:, :], prm[:, bass.ds(p + LNW, 1)], prm[:, bass.ds(p + LNB, 1)],
                                  ALU.mult, ALU.add).then_inc(W["aff"], 1)
                dve.wait_ge(W["bmm"], p + 1)
                dve.wait_ge(W["v_in"], p * 16 + 16)
                dve.tensor_tensor(y3[:, :], bank(3)[:, 0:T], vb[:, :], ALU.mult).then_inc(W["bon"], 1)
                dve.wait_ge(W["bon"], p + 1)
                dve.wait_ge(W["aff"], p + 1)
                dve.tensor_tensor(y2[:, :], y2[:, :], y3[:, :], ALU.add).then_inc(W["ysum"], 1)
                dve.wait_ge(W["ysum"], p + 1)
                dve.wait_ge(W["g_in"], p * 16 + 16)
                dve.tensor_tensor(y2[:, :], y2[:, :], gb[:, :], ALU.mult).then_inc(W["gate"], 1)
                dve.wait_ge(W["hi"], p + 2)
                dve.tensor_tensor(hL[:, bass.ds(p, 1), :], y2[:, :].unsqueeze(1),
                                  hH[:, bass.ds(p, 1), :].bitcast(f32), ALU.subtract).then_inc(W["lo"], 1)

            residual("n3" if layers >= 4 else None, J["ro"], before=lambda: dve.wait_ge(M["x_back"], 16))
        if layers >= 4:
            ffn(1)

    @block.gpsimd
    def _(pool):
        if layers < 3:
            return
        xs, rs, vs_, gs = x_spill, r_spill, v_spill, g_spill
        pool.wait_ge(M["h"], KT)
        pool.dma_start(xs, xT[:, :, :]).then_inc(M["x_spilled"], 16)
        for u in range(4):
            pool.wait_ge(unit_out, J["rg"].unit_end(0, 1 + u))
            pool.dma_start(gs[:, 4 * u:4 * u + 4, :], quad(ru[:, :])).then_inc(M["g_spilled"], 16)
        for name, dst, done in (("rv", vs_, "v_spilled"), ("rr", rs, "r_spilled")):
            for u in range(4):
                pool.wait_ge(unit_out, J[name].unit_end(*divmod(u, 2)))
                pool.dma_start(dst[:, 4 * u:4 * u + 4, :], quad(ru[:, :])).then_inc(M[done], 16)
        for done, n in (("g_spilled", 64), ("v_spilled", 64), ("r_spilled", 64)):
            pool.wait_ge(M[done], n)
        pool.wait_ge(M["kb"], 4)
        with pool.Fori(0, KT) as p:
            pool.wait_ge(W["hi"], p + 1)
            pool.dma_start(rb[:, :].unsqueeze(1), rs[:, bass.ds(p, 1), :]).then_inc(W["r_in"], 16)
            pool.dma_start(vb[:, :].unsqueeze(1), vs_[:, bass.ds(p, 1), :]).then_inc(W["v_in"], 16)
            pool.dma_start(gb[:, :].unsqueeze(1), gs[:, bass.ds(p, 1), :]).then_inc(W["g_in"], 16)
        pool.wait_ge(W["lo"], KT)
        pool.wait_ge(W["hi"], KT + 1)
        pool.dma_start(xT[:, :, :], xs).then_inc(M["x_back"], 16)
        for s, n in ((M["x_back"], 16), (W["r_in"], 16 * KT), (W["v_in"], 16 * KT), (W["g_in"], 16 * KT)):
            pool.wait_ge(s, n)

    @block.tensor
    def _(pe):
        def products(job, src, ready, every=None):
            every = every or {}

            def body(i):
                j = 0
                for w, panels in enumerate(job.units):
                    a = acc[job.unit(0, w) % 2]
                    for p in range(panels):
                        pe.wait_ge(lo_split, job.panel_end(i, j))
                        if p == 0:
                            pe.wait_ge(unit_out, job.unit_end(i, w) - 2)
                        ready(p)
                        s = job.hl[j]
                        for q in range(4):
                            hi, lo = src(4 * p + q)
                            for ft in range(4):
                                at_ = q * UNIT + ft * P
                                for n, (wt, h) in enumerate(((wh, hi), (wh, lo), (wl, hi))):
                                    mm = pe.matmul(a[:, ft * T:(ft + 1) * T], wt[:, s, at_:at_ + P], h,
                                                   start=(p == 0 and q == 0 and n == 0 and ft % 2 == 0),
                                                   stop=(p == panels - 1 and q == 3 and n == 2),
                                                   skip_group_check=True)
                        mm.then_inc(panel_used, 1)
                        for f in every.get(j, ()):
                            f(i)
                        j += 1

            if job.n == 1:
                body(0)
            else:
                with pe.Fori(0, job.n) as i:
                    body(i)

        def h_in(kt):
            return hH[:, kt, :], hL[:, kt, :]

        def a_in(kt):
            return aH[:, kt, :], aL[:, kt, :]

        pe.sem_inc(panel_used, SEED)
        pe.sem_inc(hi_split, SEED)
        pe.sem_inc(lo_split, SEED)
        pe.sem_inc(unit_out, 2)
        pe.sem_inc(at["mixed"], 2)
        pe.sem_inc(qk["roped"], 1)
        if layers >= 3:
            pe.sem_inc(W["hi"], 1)
        pe.wait_ge(const_in, 32)
        pe.wait_ge(x_in, 32)
        for g in range(8):
            if g >= 4:
                pe.wait_ge(turned_out, g - 3)
            for k in range(2):
                for tt in range(2):
                    mm = pe.transpose(bank(4 + g % 4)[:, (2 * k + tt) * P:(2 * k + tt + 1) * P],
                                      xin[:, tt, (2 * g + k) * P:(2 * g + k + 1) * P], C("ident"))
            mm.then_inc(turned, 1)
        pe.wait_ge(rows_in, 16 * ROW_LOADS)
        for g, tiles in enumerate(((0, 1, 2), (3, 4, 5, 6), (7, 8, 9, 10))):
            pe.wait_ge(turned_out, 5 + g)
            at_ = 0
            for tile in tiles:
                n = {0: 128, 1: 112, 2: 34}.get(tile, 88)
                mm = pe.transpose(bank(4 + g)[:, at_:at_ + n], prow[0:n, tile, :], C("ident", 0, n, p=n))
                at_ += n
            mm.then_inc(turned, 1)

        def norm_total(n, sq_from=3):
            pe.wait_ge(N[n]["summed"], sq_from)
            for k in range(4):
                mm = pe.matmul(aux[0][:, 0:T], C("ones"), sqacc[:, k * T:(k + 1) * T], start=(k == 0), stop=(k == 3))
            mm.then_inc(N[n]["total"], 1)

        pe.wait_ge(turned_out, 9)
        norm_total("n0")

        def qk_sum(which, w):
            def step(i):
                n = i * 2 + (4 * which + w)
                pe.wait_ge(qk["squared"], n + 1)
                pe.wait_ge(qk["roped"], n - (w - 1))
                for k in range(4):
                    mm = pe.matmul(aux[0][0:4, w * 512:w * 512 + T], R("ssum", 4 * k, 4 * k + 4),
                                   sq2[:, w, k * T:(k + 1) * T], start=(k == 0), stop=(k == 3))
                mm.then_inc(qk["summed"], 1)
            return step

        def qk_spread(which, w):
            def step(i):
                n = i * 2 + (4 * which + w)
                pe.wait_ge(qk["inverse"], n + 1)
                if which or w:
                    pe.wait_ge(qk["normed"], 4 * n)
                for k in range(4):
                    mm = pe.matmul(aux[1][:, k * T:(k + 1) * T], R("sbc", k * P, (k + 1) * P, p=4), rsr[:, w, :],
                                   start=True, stop=True)
                mm.then_inc(qk["spread"], 1)
            return step

        def qk_turn(which, w):
            def step(i):
                n = i * 2 + (4 * which + w)
                pe.wait_ge(qk["normed"], 4 * n + 4)
                for k in range(2):
                    mm = pe.matmul(aux[0][:, k * 512:(k + 1) * 512], R("perm"), nrmd[:, k * 512:(k + 1) * 512],
                                   start=True, stop=True)
                mm.then_inc(qk["turned"], 1)
            return step

        def normed(n):
            return lambda p: pe.wait_ge(N[n]["lo"], p + 1)

        jq, jk, jv, jo = (J[k] for k in ("q", "k", "v", "wo"))
        products(jq, h_in, normed("n0"))
        for which, job in ((0, jk), (1, jv)):
            products(job, h_in, normed("n0"),
                     every={0: [qk_sum(which, 0)], 1: [qk_sum(which, 1)], 2: [qk_spread(which, 0)],
                            3: [qk_turn(which, 0)], 4: [qk_spread(which, 1)], 5: [qk_turn(which, 1)]})
        pe.wait_ge(qk["roped"], 9)
        with pe.Fori(0, NH // 2) as i:
            for b in range(2):
                pe.wait_ge(at["staged"], 4 * i + (2 * b + 2))
                for (a, e), qa in (((0, P), 0), ((P, 3 * P), P)):
                    k = QKV[:, bass.ds(i * 2 + (KT + b), 1), 0:e - a].rearrange("p a t -> p (a t)")
                    mm = pe.matmul(aux[b][:, a:e], qs[:, b, qa:qa + P], k, start=True, stop=True)
                mm.then_inc(at["scored"], 1)
                for t in range(2):
                    mm = pe.transpose(aux[b][:, 512 + t * P:512 + (t + 1) * P], vs[:, b, t * P:(t + 1) * P],
                                      C("ident"))
                mm.then_inc(at["vturned"], 1)
            for b in range(2):
                pe.wait_ge(at["probs"], 4 * i + (2 * b + 2))
                pe.wait_ge(at["vout"], 2 * i + (b + 1))
                for n, a in enumerate((0, P, 2 * P)):
                    mm = pe.transpose(aux[b][:, 512 + n * P:512 + (n + 1) * P], ex[:, b, a:a + P], C("ident"))
                mm.then_inc(at["pturned"], 1)
            for b in range(2):
                pe.wait_ge(at["pout"], 2 * i + (b + 1))
                pe.matmul(acc[b][:, 0:T], vt[:, b, 0:P], pT[:, b, 0:T], start=True, stop=True,
                          skip_group_check=True)
                pe.matmul(acc[b][:, P:T], vt[:, b, P:T], pT[:, b, T:T + P], start=False, stop=True,
                          skip_group_check=True).then_inc(at["mixed"], 1)

        products(jo, h_in, lambda p: pe.wait_ge(at["lo"], NH))

        def ffn(layer):
            n = ("n1", "n3")[layer]
            norm_total(n)
            for h, g0 in (("a", 0), ("b", HALF_A)):
                products(J[f"up{layer}{h}"], h_in, normed(n))
                u0 = layer * (HALF_A + HALF_B) + g0
                products(J[f"dn{layer}{h}"], a_in, lambda p, u0=u0: pe.wait_ge(f["lo"], u0 + p + 1))

        if layers >= 2:
            ffn(0)
        if layers >= 3:
            norm_total("n2")
            mixed = {name: (lambda p, k=k: pe.wait_ge(M["lo"], 4 * k + p + 1))
                     for k, name in enumerate(("rg", "rv", "rw", "ra", "rk", "rr"))}

            def triple(out_, col, lhs, kt_hi, kt_lo, parts, first, last, clear):
                for n, (wt, h) in enumerate(((wh, kt_hi), (wh, kt_lo), (wl, kt_hi))):
                    mm = pe.matmul(out_, lhs(wt), h, start=(first and clear and n == 0), stop=(last and n == 2),
                                   skip_group_check=True)
                return mm

            def low_units(job, k, slots, parts):
                pe.wait_ge(M["low_lo"], k + 1)
                for u in range(4):
                    a = acc[job.unit(0, 1 + u) % 2]
                    pe.wait_ge(unit_out, job.unit_end(0, 1 + u) - 2)
                    for ft in range(4):
                        col = (4 * u + ft) * P
                        for q, s in enumerate(slots):
                            mm = triple(a[:, ft * T:(ft + 1) * T], col, lambda wt, s=s: wt[0:parts, s, col:col + P],
                                        tH[0:parts, q, :], tL[0:parts, q, :], parts, q == 0, q == len(slots) - 1,
                                        ft % 2 == 0)
                    mm.then_inc(M["low_unit"], 1)

            jg = J["rg"]
            pe.wait_ge(unit_out, jg.unit_end(0, 0) - 2)
            for j in range(2):
                pe.wait_ge(lo_split, jg.panel_end(0, j))
                for q in range(8):
                    kt = 8 * j + q
                    if kt % 4 == 0:
                        mixed["rg"](kt // 4)
                    for ft in range(2):
                        at_ = q * T + ft * P
                        mm = triple(acc[jg.unit(0, 0) % 2][:, ft * T:(ft + 1) * T], 0,
                                    lambda wt: wt[:, jg.hl[j], at_:at_ + P], hH[:, kt, :], hL[:, kt, :], P,
                                    kt == 0, kt == KT - 1, ft == 0)
                mm.then_inc(panel_used, 1)
            pe.wait_ge(lo_split, jg.panel_end(0, 3))
            low_units(jg, 0, jg.hl[2:4], P)
            pe.drain().then_inc(panel_used, 2)
            products(J["rv"], h_in, mixed["rv"])
            for k, name in ((1, "rw"), (2, "ra")):
                job = J[name]
                pe.wait_ge(lo_split, job.panel_end(0, 0))
                pe.wait_ge(unit_out, job.unit_end(0, 0) - 2)
                for kt in range(KT):
                    if kt % 4 == 0:
                        mixed[name](kt // 4)
                    mm = triple(acc[job.unit(0, 0) % 2][0:LORA, 0:T], 0,
                                lambda wt: wt[:, job.hl[0], kt * LORA:(kt + 1) * LORA], hH[:, kt, :], hL[:, kt, :],
                                P, kt == 0, kt == KT - 1, True)
                mm.then_inc(panel_used, 1)
                pe.wait_ge(lo_split, job.panel_end(0, 1))
                low_units(job, k, job.hl[1:2], LORA)
                pe.drain().then_inc(panel_used, 1)
            products(J["rk"], h_in, mixed["rk"])

            def kk_sum(w):
                def step(i):
                    pe.wait_ge(M["ksq"], i * 2 + (w + 1))
                    for k in range(4):
                        mm = pe.matmul(aux[0][0:8, w * 512:w * 512 + T], C("ksum", 8 * k, 8 * k + 8),
                                       kq[:, k * T:(k + 1) * T], start=(k == 0), stop=(k == 3))
                    mm.then_inc(M["ksum"], 1)
                return step

            def kk_spread(w):
                def step(i):
                    pe.wait_ge(M["krec"], i * 2 + (w + 1))
                    if w:
                        pe.wait_ge(M["kk"], i * 2 + w)
                    for k in range(4):
                        mm = pe.matmul(aux[1][:, k * T:(k + 1) * T], C("kbc", k * P, (k + 1) * P, p=8),
                                       krs[:, w, :], start=True, stop=True)
                    mm.then_inc(M["kspread"], 1)
                return step

            products(J["rr"], h_in, mixed["rr"],
                     every={3: [kk_sum(0)], 4: [kk_sum(1)], 5: [kk_spread(0)], 6: [kk_spread(1)]})
            core_pe(pe)
            products(J["ro"], h_in, lambda p: pe.wait_ge(W["lo"], KT))
        if layers >= 4:
            ffn(1)
        pe.wait_ge(unit_out, final_job.unit_end(final_job.n - 1, 1))
        for g in range(8):
            if g >= 4:
                pe.wait_ge(out_ready, g - 3)
            for k in range(2):
                for tt in range(2):
                    mm = pe.transpose(bank(4 + g % 4)[:, (2 * k + tt) * P:(2 * k + tt + 1) * P],
                                      xT[:, 2 * g + k, tt * P:(tt + 1) * P], C("ident"))
            mm.then_inc(out_turned, 1)

    block_ctx.__exit__(None, None, None)


def constants():
    import numpy as np
    r, c = np.arange(P)[:, None], np.arange(P)[None, :]
    parts = {
        "ident": np.eye(P), "ones": np.ones((P, P)), "blk": r // RH == c // RH,
        "mb": np.hstack([-1.0 * (r < c), r <= c]), "mk": np.hstack([r < c, r <= c]),
        "mx1": 1.0 * (r == c) - ((r == c + 1) & (c % 2 == 0)), "mx1t": 1.0 * (r == c) - ((c == r + 1) & (r % 2 == 0)),
        "ksum": np.hstack([np.stack([r[:, 0] // RH + 2 * k == j for j in range(8)], 1) for k in range(4)]),
        "eps": np.array([[NORM_EPS, GN_EPS, 0, 0]] * P),
    }
    kbc = np.zeros((P, 4 * P))
    for k in range(4):
        for j in range(8):
            kbc[j, k * P:(k + 1) * P] = np.arange(P) // RH + 2 * k == j
    parts["kbc"] = kbc
    levels = []
    for level in range(1, LEVELS + 1):
        s = 1 << level
        cols = np.array([q for q in range(P) if q % (2 * s) < s])[None, :]
        one = 1.0 * (r == cols) - ((r // (2 * s) == cols // (2 * s)) & (r % (2 * s) >= s))
        levels += [one, one]
    parts["lv"] = np.hstack(levels)
    a = np.zeros((P, NCONST), np.float32)
    for name, (lo, hi) in CONST.items():
        a[:, lo:hi] = parts[name]
    half = HD // 8
    freq = np.float32(500000.0) ** (-np.arange(0, 2 * half, 2, dtype=np.float32) / np.float32(2 * half))
    ang = np.arange(T, dtype=np.float32)[None, :] * freq.astype(np.float32)[:, None]
    cos, sin = np.ones((P, T), np.float32), np.zeros((P, T), np.float32)
    cos[0:half], cos[half:2 * half] = np.cos(ang), np.cos(ang)
    sin[0:half], sin[half:2 * half] = -np.sin(ang), np.sin(ang)
    perm = np.zeros((P, P))
    for d in range(half):
        perm[d + half, d] = perm[d, d + half] = 1.0
    causal = np.where(c <= r, 0.0, -1e30)
    ssum, sbc = np.zeros((P, 16)), np.zeros((P, 4 * P))
    for k in range(4):
        ssum[:, 4 * k + k] = 1.0
        sbc[k, k * P:(k + 1) * P] = 1.0
    rope = {"perm": perm, "cos": cos, "sin": sin, "cmask": np.hstack([causal, np.zeros((P, P)), causal]),
            "ssum": ssum, "sbc": sbc}
    b = np.zeros((P, NROPE), np.float32)
    for name, (lo, hi) in ROPE.items():
        b[:, lo:hi] = rope[name]
    return a, b


_INS = ["x", "moba_norm", "moba_wqkv", "moba_q_gain", "moba_k_gain", "moba_wo",
        "rwkv_norm", "rwkv_mu", "rwkv_w_r", "rwkv_w_k", "rwkv_w_v", "rwkv_w_o",
        "rwkv_w0", "rwkv_w1", "rwkv_w2", "rwkv_a0", "rwkv_a1", "rwkv_a2", "rwkv_g1", "rwkv_g2",
        "rwkv_k_k", "rwkv_k_a", "rwkv_r_k", "rwkv_lnx_w", "rwkv_lnx_b",
        "ffn_norm", "ffn_w_up", "ffn_conv_w", "ffn_conv_b", "ffn_w_down"]
LAYERS = 4


def kernel(**inputs):
    import numpy as _np
    import concourse.bacc as _bacc
    from concourse import mybir as _mybir
    from concourse.bass_utils import run_bass_kernel_spmd as _run

    nc = _bacc.Bacc("TRN2", target_bir_lowering=False, num_devices=1)
    arrays, args = {}, []
    const_all, const_rope = constants()
    for name, a in [(n, inputs[n]) for n in _INS] + [("const_all", const_all), ("const_rope", const_rope)]:
        a = _np.ascontiguousarray(a)
        arrays[f"in_{name}_dram"] = a
        args.append(nc.dram_tensor(f"in_{name}_dram", a.shape, _mybir.dt.from_np(a.dtype), kind="ExternalInput").ap())
    args.append(nc.dram_tensor("out_0_dram", (1, T, D), _mybir.dt.float32, kind="ExternalOutput").ap())
    for name in ("x", "r", "v", "g"):
        args.append(nc.dram_tensor(f"{name}_spill", (P, KT, T), _mybir.dt.float32, kind="Internal").ap())
    hybrid_trunk(nc, *args, layers=LAYERS)
    r = _run(nc, [arrays], core_ids=[0])
    return r.results[0]["out_0_dram"]
```

```python
import concourse.bass as bass
from concourse import mybir

P = 128
T = 256
D = 2048
KT = D // P
FF = 5632
FKT = FF // P
NORM_EPS = 1e-6
GN_EPS = 64e-5
HD = 128
NH = D // HD
RH = 64
LORA = 96
UNIT = 512
RAW = 3
SPLIT = 2
PAN = 2048
HALF_A = 6
HALF_B = 5
LEVELS = 6
EXPM05 = 0.6065306597126334
SEED = 8
QT = 4 * T


def columns(*specs):
    at, got = 0, {}
    for name, w in specs:
        got[name] = (at, at + w)
        at += w
    return got, at


CONST, NCONST = columns(("ident", P), ("ones", P), ("blk", P), ("mb", 2 * P), ("mk", 2 * P), ("mx1", P), ("mx1t", P),
                        ("lv", P * LEVELS), ("ksum", 32), ("kbc", 4 * P), ("eps", 4))
ROPE, NROPE = columns(("perm", P), ("cos", T), ("sin", T), ("cmask", 384), ("ssum", 16), ("sbc", 4 * P))
PA, PB, PC, PCV = 0, 128, 240, 274
PRM_COLS = PCV + 8 * 88
G_MOBA, G_RWKV, MU = 0, 16, 32
W0, A0, K_K, K_A, R_K, LNW, LNB = (PB + 16 * i for i in range(7))
G_FFN, QG, KG = PC, PC + 32, PC + 33
OMKA = PRM_COLS
ROW_LOADS = 3 + 7 + 3 + 2 * 4


class Job:

    def __init__(self, name, n, units, accs):
        self.name, self.n, self.units, self.accs = name, n, units, accs
        self.m = sum(units)
        self.last_panel = [sum(units[:k + 1]) - 1 for k in range(len(units))]

    def panel(self, i, j):
        return self.first_panel + i * self.m + j

    def unit(self, i, w):
        return self.first_unit + i * self.accs + w

    def panel_end(self, i, j):
        return self.first_panel + i * self.m + (j + 1)

    def unit_end(self, i, w):
        return self.first_unit + i * self.accs + (w + 1)

    def landed(self, i, j):
        s = self.raw[j]
        return i * (16 * self.uses[s]) + 16 * (self.landed0[s] + self.raw[:j + 1].count(s))


def gaps(job, idx, slots, last):
    got = []
    for j, s in enumerate(slots):
        earlier = [q for q in range(j) if slots[q] == s]
        if earlier:
            got.append(j - earlier[-1])
            continue
        back = [idx + j - last[s]]
        if job.n > 1:
            back.append(job.m - max(q for q in range(job.m) if slots[q] == s) + j)
        got.append(min(back))
    for s in set(slots):
        last[s] = idx + (job.n - 1) * job.m + max(q for q in range(job.m) if slots[q] == s)
    return got


def plan(jobs):
    idx, unit = SEED, 2
    landed = [0] * RAW
    last_raw, last_split = [SEED - 1] * RAW, [SEED - 1] * SPLIT
    for job in jobs:
        job.first_panel, job.first_unit = idx, unit
        job.raw = [j % RAW for j in range(job.m)]
        job.hl = [j % SPLIT for j in range(job.m)]
        job.landed0 = list(landed)
        job.uses = [job.raw.count(s) for s in range(RAW)]
        job.raw_gap = gaps(job, idx, job.raw, last_raw)
        job.hl_gap = gaps(job, idx, job.hl, last_split)
        for s in range(RAW):
            landed[s] += job.n * job.uses[s]
        idx += job.n * job.m
        unit += job.n * job.accs


def hybrid_trunk(nc, x, moba_norm, moba_wqkv, moba_q_gain, moba_k_gain, moba_wo,
                 rwkv_norm, rwkv_mu, rwkv_w_r, rwkv_w_k, rwkv_w_v, rwkv_w_o,
                 rwkv_w0, rwkv_w1, rwkv_w2, rwkv_a0, rwkv_a1, rwkv_a2, rwkv_g1, rwkv_g2,
                 rwkv_k_k, rwkv_k_a, rwkv_r_k, rwkv_lnx_w, rwkv_lnx_b,
                 ffn_norm, ffn_w_up, ffn_conv_w, ffn_conv_b, ffn_w_down, const_all, const_rope, out,
                 x_spill, r_spill, v_spill, g_spill, layers=4):
    f32, f32r = mybir.dt.float32, mybir.dt.float32r
    ALU, ACT, AX = mybir.AluOpType, mybir.ActivationFunctionType, mybir.AxisListType

    J = {}
    stages = ((1, "q", 2, [4, 4], 2), (1, "k", 2, [4, 4], 2), (1, "v", 2, [4, 4], 2), (1, "wo", 2, [4, 4], 2),
              (2, "up0a", HALF_A, [4, 4], 2), (2, "dn0a", 2, [6, 6], 2),
              (2, "up0b", HALF_B, [4, 4], 2), (2, "dn0b", 2, [5, 5], 2),
              (3, "rg", 1, [4], 5), (3, "rv", 2, [4, 4], 2), (3, "rw", 1, [2], 5), (3, "ra", 1, [2], 5),
              (3, "rk", 2, [4, 4], 2), (3, "rr", 2, [4, 4], 2), (3, "ro", 2, [4, 4], 2),
              (4, "up1a", HALF_A, [4, 4], 2), (4, "dn1a", 2, [6, 6], 2),
              (4, "up1b", HALF_B, [4, 4], 2), (4, "dn1b", 2, [5, 5], 2))
    for layer, name, n, units, accs in stages:
        if layer <= layers:
            J[name] = Job(name, n, units, accs)
    order = list(J)
    plan([J[n] for n in order])
    final_job = J[order[-1]]

    def rows(w):
        return w.rearrange("(t p) n -> p t n", p=P)

    top = [(nc.sbuf_base + 31) // 32 * 32]
    limit = nc.sbuf_usable_end

    def place(at, *specs):
        fixed = at is None
        at = top[0] if fixed else at
        got = []
        for name, shape, dt in specs:
            size = 4
            for s in shape[1:]:
                size *= s
            assert at + size <= limit, (name, at + size - limit)
            got.append(nc.alloc_sbuf_tensor_at(name, shape, dt, offset=at))
            at += (size + 31) // 32 * 32
        if fixed:
            top[0] = at
        return got

    xT_at = top[0]
    (xT, hH, hL, raw, wh, wl, cst, prm, rstd, rt) = place(
        None, ("xT", [P, KT, T], f32), ("hH", [P, KT, T], f32r), ("hL", [P, KT, T], f32r),
        ("raw", [P, RAW, PAN], f32), ("wh", [P, SPLIT, PAN], f32r), ("wl", [P, SPLIT, PAN], f32r),
        ("cst", [P, NCONST], f32), ("prm", [P, PRM_COLS + 16], f32), ("rstd", [P, T], f32), ("mid", [P, 8], f32))
    mid = rt
    area = top[0]
    K16 = KT * T * 4
    xin, prow = place(area, ("xin", [P, 2, D], f32), ("prow", [P, 11, P], f32))
    norm_at = area + 3 * K16
    sq, sqacc, hf = place(norm_at, ("sq", [P, QT], f32), ("sqacc", [P, QT], f32), ("hf", [P, 2, QT], f32))
    rest_at = norm_at + 4 * QT * 4
    QKV, = place(area, ("QKV", [P, 3 * KT, T], f32))
    rot, nrmd, ssr, rsr, cr = place(rest_at, ("rot", [P, QT], f32), ("nrmd", [P, QT], f32), ("ssr", [4, 2, T], f32),
                                    ("rsr", [4, 2, T], f32), ("cr", [P, NROPE], f32))
    sq2, = place(norm_at + 2 * QT * 4, ("sq2", [P, 2, QT], f32))
    qs, vs, vt, sc, ex, pT, st = place(
        norm_at, ("qs", [P, 2, T], f32), ("vs", [P, 2, T], f32), ("vt", [P, 2, T], f32), ("sc", [P, 2, 384], f32),
        ("ex", [P, 2, 384], f32), ("pT", [P, 2, 384], f32), ("st", [P, 2, 8], f32))
    aH, aL = place(area, ("aH", [P, 4 * HALF_A, T], f32r), ("aL", [P, 4 * HALF_A, T], f32r))
    sg, fu, fc = place(rest_at, ("sg", [P, QT], f32), ("fu", [P, QT], f32), ("fc", [P, QT], f32))
    hb, xx, cw, kb, ab, ru, mt = place(
        area, ("hb", [P, KT, T], f32), ("xx", [P, KT, T], f32), ("cw", [P, KT, 2, 129], f32),
        ("kb", [P, KT, T], f32), ("ab", [P, KT, T], f32), ("ru", [P, QT], f32), ("mt", [P, QT], f32))
    xx_at = area + K16
    kb_at = xx_at + K16 + KT * 258 * 4
    ru_at = kb_at + 2 * K16
    tH, tL = place(kb_at, ("tH", [P, 2, T], f32r), ("tL", [P, 2, T], f32r))
    kkr, kq, kss, krs = place(xx_at, ("kkr", [P, 2, QT], f32), ("kq", [P, QT], f32),
                              ("kss", [8, 2, T], f32), ("krs", [8, 2, T], f32))
    kkb, = place(area, ("kkb", [P, KT, T], f32))
    slot1_at = xT_at + 3 * K16 + RAW * PAN * 4 + PAN * 4
    Qb, X, XT0 = place(xT_at, ("Qb", [P, LEVELS * 4, P], f32), ("Xb", [P, 2, 2, P], f32), ("XT0", [P, 2, 2, P], f32))
    mB0, mK0, tok0, tok1, vb0, vb1, bp0, bp1 = place(
        xx_at, ("mB0", [P, 2, 2, 2 * P], f32), ("mK0", [P, 2, 2, 2 * P], f32), ("tok0", [P, 4, P], f32),
        ("tok1", [P, 4, P], f32), ("vb0", [P, T], f32), ("vb1", [P, T], f32), ("bp0", [P, T], f32),
        ("bp1", [P, T], f32))
    ar0, gb, e1, zb, ub, s0, scl = place(
        ru_at, ("ar0", [P, 2, 2, 2, P], f32), ("gb", [P, T], f32), ("e1", [P, 2, 129], f32),
        ("zb", [P, 2, 2, RH], f32), ("ub", [P, 2, 2, RH], f32), ("s0", [P, RH], f32), ("scl", [P, 2], f32))
    hH_last, hL_last = xT_at + K16 + (KT - 2) * T * 4, xT_at + 2 * K16 + (KT - 2) * T * 4
    rb, bt = place(hH_last, ("rb", [P, T], f32), ("bt", [P, 2, P], f32))
    e2, kt_ = place(hL_last, ("e2", [P, 2, P], f32), ("ktl", [P, 2, P], f32))
    ar1, XT1, ys, y2 = place(slot1_at, ("ar1", [P, 2, 2, 2, P], f32), ("XT1", [P, 2, 2, P], f32),
                             ("ys", [P, T], f32), ("y2", [P, T], f32))
    mB1, mK1 = place(slot1_at + SPLIT * PAN * 4, ("mB1", [P, 2, 2, 2 * P], f32), ("mK1", [P, 2, 2, 2 * P], f32))
    y3 = rstd
    ars, mBs, mKs, toks, XTs, vbs, bps = (ar0, ar1), (mB0, mB1), (mK0, mK1), (tok0, tok1), (XT0, XT1), (vb0, vb1), \
        (bp0, bp1)
    xo, = place(area, ("xo", [P, 2, D], f32))

    acc = [nc.alloc_psum_tensor(f"acc{k}", [P, QT], f32) for k in range(2)]
    aux = [nc.alloc_psum_tensor(f"aux{k}", [P, QT], f32) for k in range(2)]

    def bank(k):
        return (acc + aux)[k // 2][:, (k % 2) * 512:(k % 2) * 512 + 512]

    def C(name, a=0, b=None, p=P):
        lo, hi = CONST[name]
        return cst[0:p, lo + a:hi if b is None else lo + b]

    def R(name, a=0, b=None, p=P):
        lo, hi = ROPE[name]
        return cr[0:p, lo + a:hi if b is None else lo + b]

    def quad(ap):
        return ap.rearrange("p (f t) -> p f t", f=4)

    def sem(name):
        return nc.alloc_semaphore(name)

    raw_landed = [sem(f"raw_landed{k}") for k in range(RAW)]
    hi_split, lo_split = sem("hi_split"), sem("lo_split")
    panel_used = sem("panel_used")
    unit_out = sem("unit_out")
    const_in, x_in, rows_in = sem("const_in"), sem("x_in"), sem("rows_in")
    turned, turned_out = sem("turned"), sem("turned_out")
    omka_done = sem("omka_done")

    class Names:

        def __init__(self, phase, *names):
            self.sems = {n: sem(f"{phase}_{n}") for n in names}

        def __getitem__(self, n):
            return self.sems[n]

    norm_names = ("squared", "summed", "total", "rooted", "rstd", "normed", "hi", "lo")
    N = {k: Names(k, *norm_names) for k in ("n0", "n1", "n2", "n3")[:layers]}
    qk = Names("qk", "squared", "summed", "rooted", "inverse", "spread", "normed", "turned", "cosed", "sined", "roped")
    at = Names("at", "staged", "vturned", "vout", "scored", "masked", "maxed", "neg", "exped", "recip", "probs",
               "pturned", "pout", "mixed", "hi", "lo")
    f = Names("ffn", "init", "tap1", "tap0", "silu", "gated", "hi", "lo")
    M = Names("mix", "h", "xx", "mixed", "hi", "lo", "low_hi", "low_lo", "zeroed", "scan", "mid", "cw",
              "kkr", "ksq", "ksum", "kroot", "kmax", "krec", "kspread", "kk", "kfac", "kmod", "kb",
              "x_spilled", "r_spilled", "v_spilled", "g_spilled", "x_back", "low_unit")
    W = Names("core", "zeroed", "exps", "scaled", "bonusp", "turned", "tok", "gram", "gmask", "geye", "xt0",
              "lev0", "x0", "lp", "lq", "lt", "lxo", "lto", "zmm", "zout", "umm", "uout", "smm", "sout",
              "ymm", "yout", "mean", "cent", "csq", "var", "std", "rec", "norm", "aff", "bmm", "bon", "ysum", "gate",
              "hi", "lo")
    W.sems.update({n: sem(f"core_{n}") for n in ("r_in", "v_in", "g_in")})
    out_turned, out_ready, out_done = sem("out_turned"), sem("out_ready"), sem("out_done")

    block_ctx = nc.Block()
    block = block_ctx.__enter__()

    def run(eng, job, split, first=None, every=None, late=None, last=None):
        first, every, late, last = first or {}, every or {}, late or {}, last or {}

        def body(i, is_first, is_last):
            for j in range(job.m):
                if j + 1 < job.m or not (job is final_job and is_last):
                    split(eng, job, i, j + 1)
                if is_first:
                    for f in first.get(j, ()):
                        f()
                else:
                    for f in late.get(j, ()):
                        f(i - 1)
                for f in every.get(j, ()):
                    f(i)
                if is_last:
                    for f in last.get(j, ()):
                        f()

        body(0, True, job.n == 1)
        if job.n == 2:
            body(1, False, True)
        elif job.n > 2:
            with eng.Fori(1, job.n) as i:
                body(i, False, False)

    following = {order[k]: order[k + 1] for k in range(len(order) - 1)}

    def next_place(job, i, j):
        if j < job.m:
            return job, i, j
        return job, i + 1, 0

    def mix_used(J):
        used = {"rg": [J["rg"].first_panel] * 4}
        jg = J["rg"]
        used["rv"] = [jg.panel_end(0, g // 2) for g in range(4)]
        for name, before in (("rw", "rv"), ("rr", "rk")):
            used[name] = [J[before].panel_end(1, 4 + g) for g in range(4)]
        for name, before in (("ra", "rw"), ("rk", "ra")):
            used[name] = [J[before].panel_end(0, 0)] * 4
        return used

    def flat(t, per):
        dims = len(t.shape) - 1
        v = {2: lambda: t[:, :, :].rearrange("p a b -> p (a b)"),
             3: lambda: t[:, :, :, :].rearrange("p a b c -> p (a b c)")}[dims]()
        return lambda p, a=0, n=per, rows=slice(0, P): v[rows, bass.ds(p * per + a, n)]

    cwp, kbp, abp, kkp = flat(cw, 258), flat(kb, T), flat(ab, T), flat(kkb, T)

    def spread(ap, n):
        return ap.unsqueeze(1).to_broadcast([ap.shape[0], n, ap.shape[1]])

    def blocks(ap, s, half):
        return ap.rearrange("p h (b u s) -> p (h b) u s", u=2, s=s)[:, :, half, :]

    def compact(ap, s):
        return ap.rearrange("p (b s) -> p b s", s=s)

    heads = [(h, slice(h * RH, (h + 1) * RH)) for h in range(2)]

    def Ql(level, c):
        at_ = 4 * (level - 1) + 2 * c
        return Qb[:, at_:at_ + 2, :]

    def core(body, eng):
        body(None, None, (0, 0))
        body(None, (0, 0), (1, 1))
        with eng.Fori(0, KT // 2 - 1) as i:
            body((i * 2, 0), (i * 2 + 1, 1), (i * 2 + 2, 0))
            body((i * 2 + 1, 1), (i * 2 + 2, 0), (i * 2 + 3, 1))
        body((KT - 2, 0), (KT - 1, 1), None)
        body((KT - 1, 1), None, None)

    def has(p, n):
        return not isinstance(p, int) or p >= n

    def pairs_before(p, n, count):
        return p * count + (1 - n) * count

    def core_loads(sp):
        def tile(src, at_):
            return src.rearrange("p k t -> p (k t)")[:, bass.ds(at_, T)]

        def load(p, k):
            if has(p, 1):
                sp.wait_ge(W["scaled"], p * 6)
            sp.dma_start(rb[:, :], tile(r_spill, p * T)).then_inc(W["r_in"], 16)
            if has(p, 2):
                sp.wait_ge(W["bon"], pairs_before(p, 2, 1))
            elif has(p, 1):
                sp.wait_ge(W["turned"], p)
            sp.dma_start(vbs[k][:, :], tile(v_spill, p * T)).then_inc(W["v_in"], 16)

        def load_gate(p):
            if has(p, 1):
                sp.wait_ge(W["gate"], p)
            sp.dma_start(gb[:, :], tile(g_spill, p * T)).then_inc(W["g_in"], 16)

        for done in ("g_spilled", "v_spilled", "r_spilled"):
            sp.wait_ge(M[done], 64)
        sp.wait_ge(M["kb"], 4)
        load(0, 0)
        load(1, 1)
        load_gate(0)
        with sp.Fori(1, KT // 2) as i:
            load(i * 2, 0)
            load_gate(i * 2 - 1)
            load(i * 2 + 1, 1)
            load_gate(i * 2)
        load_gate(KT - 1)

    def core_pe(pe):
        def body(b, f, _):
            def turn():
                p, k = f
                pe.wait_ge(W["v_in"], p * 16 + 16)
                pe.wait_ge(W["scaled"], p * 6 + 6)
                if has(p, 1):
                    pe.wait_ge(W["tok"], p)
                for n, src in enumerate((vbs[k][:, 0:P], vbs[k][:, P:T], bt[:, 0, :], kt_[:, 0, :])):
                    mm = pe.transpose(bank(4)[:, n * P:(n + 1) * P], src, C("ident"))
                mm.then_inc(W["turned"], 1)

            def gram(c):
                p, k = f
                if has(p, 1):
                    pe.wait_ge(W["lto"], pairs_before(p, 1, 12))
                    pe.wait_ge(W["lq"], pairs_before(p, 1, 12))
                for h, r in heads:
                    rhs = ars[k][:, h, c, :, :].rearrange("p a t -> p (a t)")
                    pe.matmul(bank(c)[:, h * T:(h + 1) * T], bt[:, c, :], rhs, start=True, stop=True)
                    mm = pe.matmul(bank(2 + c)[:, h * T:(h + 1) * T], kt_[:, c, :], rhs, start=True, stop=True)
                mm.then_inc(W["gram"], 1)

            def lev0(c):
                p, k = f
                pe.wait_ge(W["geye"], p * 2 + (c + 1))
                for h, r in heads:
                    mm = pe.matmul(bank(c)[:, h * P:(h + 1) * P], mBs[k][:, c, h, 0:P], C("ident"),
                                   start=True, stop=True)
                mm.then_inc(W["lev0"], 1)

            def level_g(level):
                p, k = f
                for c in range(2):
                    if level == 1:
                        pe.wait_ge(W["x0"], p * 2 + (c + 1))
                    else:
                        pe.wait_ge(W["lxo"], p * 10 + (2 * (level - 2) + c + 1))
                    for h, r in heads:
                        low = blocks(X[:, c, h:h + 1, :], 1 << level, 0)
                        mm = pe.matmul(bank(c)[:, h * RH:(h + 1) * RH], mBs[k][:, c, h, 0:P], low,
                                       start=True, stop=True)
                    mm.then_inc(W["lp"], 1)

            def level_x(level):
                p, k = f
                s = 1 << level
                for c in range(2):
                    pe.wait_ge(W["lq"], p * 12 + (2 * (level - 1) + c + 1))
                    if level == 1:
                        pe.wait_ge(W["xt0"], p * 2 + (c + 1))
                        pe.wait_ge(W["gmask"], p * 4 + (2 * c + 2))
                    else:
                        pe.wait_ge(W["lto"], p * 12 + (2 * (level - 2) + c + 1))
                    q = Ql(level, c)
                    if level < LEVELS:
                        for h, r in heads:
                            mm = pe.matmul(bank(2 + c)[:, h * RH:(h + 1) * RH], XTs[k][:, c, h, :],
                                           blocks(q[:, h:h + 1, :], s, 0), start=True, stop=True)
                    for h, r in heads:
                        mm = pe.matmul(bank(2 + c)[:, P + h * RH:P + (h + 1) * RH], q[:, h, :],
                                       blocks(XTs[k][:, c, h:h + 1, :], s, 1), start=True, stop=True)
                    mm.then_inc(W["lt"], 1)

            def z(c):
                p, k = b
                if c:
                    pe.wait_ge(W["sout"], p + 1)
                else:
                    pe.wait_ge(W["lto"], p * 12 + 12)
                    pe.wait_ge(W["gmask"], p * 4 + 4)
                    pe.wait_ge(W["tok"], p + 1)
                    if has(p, 1):
                        pe.wait_ge(W["cent"], p)
                for h, r in heads:
                    z_ = bank(5)[:, h * RH:(h + 1) * RH]
                    mm = pe.matmul(z_, mKs[k][:, c, h, 0:P], toks[k][:, c, r], start=True, stop=(c == 0))
                    if c:
                        mm = pe.matmul(z_, ars[k][:, h, 1, 0, :], s0[:, :], start=False, stop=True)
                mm.then_inc(W["zmm"], 1)

            def u(c):
                p, k = b
                pe.wait_ge(W["zout"], p * 2 + (c + 1))
                for h, r in heads:
                    mm = pe.matmul(bank(5)[:, P + h * RH:P + (h + 1) * RH], XTs[k][:, c, h, :], zb[:, c, h, :],
                                   start=True, stop=True)
                mm.then_inc(W["umm"], 1)

            def state():
                p, k = b
                pe.wait_ge(W["uout"], p * 2 + 1)
                if has(p, 1):
                    pe.wait_ge(W["bon"], p)
                for h, r in heads:
                    pe.matmul(bank(6)[r, 0:RH], toks[k][:, 2, r], ub[:, 0, h, :], start=True, stop=False)
                    mm = pe.matmul(bank(6)[r, 0:RH], toks[k][:, 3, r], toks[k][:, 0, r], start=False, stop=True)
                mm.then_inc(W["smm"], 1)

            def outputs():
                p, k = b
                pe.wait_ge(W["uout"], p * 2 + 2)
                if has(p, 1):
                    pe.wait_ge(W["std"], p)
                for c in range(2):
                    for h, r in heads:
                        y = bank(7)[r, c * P:(c + 1) * P]
                        pe.matmul(y, ub[:, c, h, :], mBs[k][:, c, h, P:2 * P], start=True, stop=False)
                        mm = pe.matmul(y, toks[k][:, c, r], mKs[k][:, c, h, P:2 * P], start=False, stop=(c == 0))
                        if c:
                            mm = pe.matmul(y, s0[:, :], ars[k][:, h, 1, 1, :], start=False, stop=True)
                mm.then_inc(W["ymm"], 1)

            def head_sum(at_, src, done):
                pe.matmul(at_[:, 0:T], C("blk"), src[:, :], start=True, stop=True).then_inc(W[done], 1)

            if b:
                z(0)
            if f:
                turn()
                gram(0)
            if b:
                u(0)
            if f:
                gram(1)
            if b:
                state()
            if f:
                lev0(0)
                lev0(1)
            if b:
                z(1)
            if f:
                level_g(1)
            if b:
                u(1)
            if f:
                level_x(1)
                level_g(2)
            if b:
                outputs()
            if f:
                level_x(2)
            if b:
                pe.wait_ge(W["bonusp"], b[0] * 2 + 2)
                head_sum(bank(6), bps[b[1]], "bmm")
                pe.wait_ge(W["yout"], b[0] + 1)
                head_sum(bank(5), ys, "mean")
            if f:
                level_g(3)
                level_x(3)
            if b:
                pe.wait_ge(W["csq"], b[0] + 1)
                head_sum(bank(7), ys, "var")
            if f:
                for level in range(4, LEVELS + 1):
                    level_g(level)
                    level_x(level)

        core(body, pe)

    def core_act(act):
        act.wait_ge(M["cw"], 2 * KT)
        act.wait_ge(M["kb"], 4)
        act.wait_ge(M["r_spilled"], 64)

        def body(b, f, n):
            def level(lev):
                p, k = f
                for c in range(2):
                    act.wait_ge(W["lt"], p * 12 + (2 * (lev - 1) + c + 1))
                    if lev < LEVELS:
                        act.copy(blocks(X[:, c], 1 << lev, 0), compact(bank(2 + c)[:, 0:P], 1 << lev))\
                           .then_inc(W["lxo"], 1)
                    act.copy(blocks(XTs[k][:, c], 1 << lev, 1), compact(bank(2 + c)[:, P:2 * P], 1 << lev))\
                       .then_inc(W["lto"], 1)

            def zout(c):
                act.wait_ge(W["zmm"], b[0] * 2 + (c + 1))
                act.copy(zb[:, c].rearrange("p h v -> p (h v)"), bank(5)[:, 0:P]).then_inc(W["zout"], 1)

            def uout(c):
                act.wait_ge(W["umm"], b[0] * 2 + (c + 1))
                act.copy(ub[:, c].rearrange("p h v -> p (h v)"), bank(5)[:, P:2 * P]).then_inc(W["uout"], 1)

            if b:
                zout(0)
            if f:
                p, k = f
                act.wait_ge(W["turned"], p + 1)
                act.copy(toks[k][:, :, :].rearrange("p a n -> p (a n)"), bank(4)).then_inc(W["tok"], 1)
            if b:
                uout(0)
                zout(1)
                uout(1)
            if f:
                level(1)
            if b:
                act.wait_ge(W["ymm"], b[0] + 1)
                act.copy(ys[:, :], bank(7)[:, 0:T]).then_inc(W["yout"], 1)
            if f:
                level(2)
            if b:
                act.wait_ge(W["cent"], b[0] + 1)
                act.activation(ys[:, :], y2[:, :], ACT.Square).then_inc(W["csq"], 1)
            if f:
                level(3)
            if b:
                act.wait_ge(W["var"], b[0] + 1)
                if has(b[0], 1):
                    act.wait_ge(W["ysum"], b[0])
                act.activation(y3[:, :], bank(7)[:, 0:T], ACT.Sqrt, bias=C("eps", 1, 2), scale=1.0 / RH)\
                   .then_inc(W["std"], 1)
            if f:
                level(4)
            if n:
                p, k = n
                if has(p, 1):
                    act.wait_ge(W["scaled"], p * 6)
                act.activation(e1[:, :, :].rearrange("p c t -> p (c t)"), cwp(p), ACT.Exp).then_inc(W["exps"], 1)
                act.activation(e2[:, :, :], cwp(p).rearrange("p (c t) -> p c t", c=2)[:, :, 1:129], ACT.Exp,
                               scale=-1.0).then_inc(W["exps"], 1)
                act.activation(scl[:, k:k + 1], cwp(p, 129, 1), ACT.Exp, bias=cwp(p, 128, 1), scale=-1.0)\
                   .then_inc(W["exps"], 1)
            if f:
                level(5)
            if b:
                act.wait_ge(W["gate"], b[0] + 1)
                act.copy(hH[:, bass.ds(b[0], 1), :], y2[:, :].unsqueeze(1)).then_inc(W["hi"], 1)
            if f:
                level(6)

        core(body, act)
        act.wait_ge(W["lo"], KT)

    @block.sync
    def _(sp):
        def load(job, src, ahead=0, between=None):
            def body(i, panels=range(job.m)):
                base = src(i)
                for j in panels:
                    sp.wait_ge(lo_split, job.panel_end(i, j) - job.raw_gap[j])
                    view = base(j)
                    a, b = view.shape[1], view.shape[2]
                    dst = raw[0:view.shape[0], job.raw[j], 0:a * b].rearrange("p (a b) -> p a b", a=a)
                    sp.dma_start(dst, view).then_inc(raw_landed[job.raw[j]], 16)
            if between:
                body(0, range(ahead))
                between()
                body(0, range(ahead, job.m))
                for i in range(1, job.n):
                    body(i)
            elif job.n == 1:
                body(0)
            else:
                with sp.Fori(0, job.n) as i:
                    body(i)

        def plain(w, k0=0, c0=0, per=4):
            def src(i):
                col = i * (2 * UNIT) if isinstance(i, int) else sp.snap(i * (2 * UNIT))

                def view(j):
                    u, p = divmod(j, per)
                    cut = w[:, k0 + 4 * p:k0 + 4 * p + 4, c0 + u * UNIT:]
                    return cut[:, :, bass.ds(col, UNIT)]
                return view
            return src

        def gate_up(w, g0):
            def src(i):
                col = sp.snap(i * UNIT)

                def view(j):
                    u, p = divmod(j, 4)
                    cut = w[:, 4 * p:4 * p + 4, u * FF + g0 * UNIT:]
                    return cut[:, :, bass.ds(col, UNIT)]
                return view
            return src

        def fixed(*views):
            return lambda i: lambda j: views[j]

        wqkv = rows(moba_wqkv[0])
        load(J["q"], plain(wqkv))
        load(J["k"], plain(wqkv, c0=D))
        load(J["v"], plain(wqkv, c0=2 * D))
        load(J["wo"], plain(rows(moba_wo[0])))

        def ffn(layer):
            up, down = rows(ffn_w_up[layer]), rows(ffn_w_down[layer])
            load(J[f"up{layer}a"], gate_up(up, 0))
            load(J[f"dn{layer}a"], plain(down, k0=0, per=HALF_A))
            load(J[f"up{layer}b"], gate_up(up, HALF_A))
            load(J[f"dn{layer}b"], plain(down, k0=4 * HALF_A, per=HALF_B))

        if layers >= 2:
            ffn(0)
        if layers >= 3:
            g1 = rows(rwkv_g1[0])
            g2 = rwkv_g2[0].rearrange("(a p) n -> a p n", p=P)
            load(J["rg"], fixed(g1[:, 0:8, :], g1[:, 8:16, :], g2[0:1].rearrange("a p n -> p a n"),
                                g2[1:2].rearrange("a p n -> p a n")))
            load(J["rv"], plain(rows(rwkv_w_v[0])))
            load(J["rw"], fixed(rows(rwkv_w1[0]), rwkv_w2.rearrange("a p n -> p a n")))
            load(J["ra"], fixed(rows(rwkv_a1[0]), rwkv_a2.rearrange("a p n -> p a n")))
            load(J["rk"], plain(rows(rwkv_w_k[0])))
            load(J["rr"], plain(rows(rwkv_w_r[0])))
            load(J["ro"], plain(rows(rwkv_w_o[0])), ahead=RAW, between=lambda: core_loads(sp))
        if layers >= 4:
            ffn(1)
        for tt in range(2):
            sp.wait_ge(out_ready, 8)
            sp.dma_start(out[0, tt * P:(tt + 1) * P, :], xo[:, tt, :]).then_inc(out_done, 16)
        sp.wait_ge(out_done, 32)

    @block.scalar
    def _(act):
        def split(eng, job, i, j):
            job, i, j = next_place(job, i, j)
            act.wait_ge(raw_landed[job.raw[j]], job.landed(i, j))
            act.wait_ge(panel_used, job.panel_end(i, j) - job.hl_gap[j])
            act.copy(wh[:, job.hl[j], :], raw[:, job.raw[j], :]).then_inc(hi_split, 1)

        act.dma_start(cst[:, :], const_all).then_inc(const_in, 16)
        for tt in range(2):
            act.dma_start(xin[:, tt, :], x[0, tt * P:(tt + 1) * P, :]).then_inc(x_in, 16)
        act.dma_start(cr[:, :], const_rope).then_inc(const_in, 16)

        def vec(v):
            return v.rearrange("(t p) -> t p", p=P)

        prows = [(0, 0, vec(moba_norm[0])), (0, 16, vec(rwkv_norm[0])),
                 (0, 32, rwkv_mu[0].rearrange("a (t p) -> (a t) p", p=P))]
        for k, v in enumerate((rwkv_w0, rwkv_a0, rwkv_k_k, rwkv_k_a)):
            prows.append((1, 16 * k, vec(v[0])))
        prows.append((1, 64, rwkv_r_k[0].rearrange("(t h) n -> t (h n)", h=2)))
        prows += [(1, 80, vec(rwkv_lnx_w[0])), (1, 96, vec(rwkv_lnx_b[0]))]
        prows += [(2, 0, ffn_norm.rearrange("a (t p) -> (a t) p", p=P)), (2, 32, moba_q_gain), (2, 33, moba_k_gain)]
        for layer in range(2):
            for k in range(3):
                prows.append((3 + 4 * layer + k, 0, vec(ffn_conv_w[layer, k])))
            prows.append((6 + 4 * layer, 0, vec(ffn_conv_b[layer])))
        assert len(prows) == ROW_LOADS
        for tile, r0, src in prows:
            act.dma_start(prow[r0:r0 + src.shape[0], tile, :], src).then_inc(rows_in, 16)

        split(act, J["q"], 0, 0)
        for g in range(8):
            act.wait_ge(turned, g + 1)
            act.copy(xT[:, 2 * g:2 * g + 2, :], bank(4 + g % 4)).then_inc(turned_out, 1)
            if g % 2:
                act.wait_ge(turned_out, g + 1)
                q = g // 2
                if q >= 2:
                    act.wait_ge(N["n0"]["summed"], q - 1)
                act.activation(quad((sqacc if q == 0 else sq)[:, :]), xT[:, 4 * q:4 * q + 4, :],
                               ACT.Square).then_inc(N["n0"]["squared"], 1)
        for g, tiles in enumerate(((0, 1, 2), (3, 4, 5, 6), (7, 8, 9, 10))):
            act.wait_ge(turned, 9 + g)
            cols = {0: (0, 240 + 34), 1: (PCV, 4 * 88), 2: (PCV + 4 * 88, 4 * 88)}[g]
            act.copy(prm[:, cols[0]:cols[0] + cols[1]], bank(4 + g)[:, 0:cols[1]]).then_inc(turned_out, 1)

        def norm_root(n):
            act.wait_ge(N[n]["total"], 1)
            act.activation(rstd[:, :], aux[0][:, 0:T], ACT.Sqrt, bias=C("eps", 0, 1), scale=1.0 / D)\
               .then_inc(N[n]["rooted"], 1)

        def norm_hi(n, g, before):
            act.wait_ge(N[n]["normed"], 4 * (g + 1))
            act.wait_ge(panel_used, before)
            act.copy(hH[:, 4 * g:4 * g + 4, :], quad(hf[:, g % 2, :])).then_inc(N[n]["hi"], 1)

        norm_root("n0")
        norm_hi("n0", 0, SEED)

        def take_qkv(job, part, w):
            def step(i):
                act.wait_ge(panel_used, job.panel_end(i, 4 * w + 3))
                act.copy(QKV[:, bass.ds(part * KT + i * 8 + 4 * w, 4), :], quad(acc[job.unit(0, w) % 2][:, :]))\
                   .then_inc(unit_out, 1)
            return step

        def qk_square(which, w):
            def step(i):
                n = 4 * which + 2 * i + w
                act.wait_ge(unit_out, J["qk"[which]].unit_end(i, w))
                if n >= 2:
                    act.wait_ge(qk["summed"], n - 1)
                act.activation(quad(sq2[:, w, :]), QKV[:, bass.ds(which * KT + i * 8 + 4 * w, 4), :],
                               ACT.Square).then_inc(qk["squared"], 1)
            return step

        def qk_root(which, w):
            def step(i):
                n = 4 * which + 2 * i + w
                act.wait_ge(qk["summed"], n + 1)
                if n >= 2:
                    act.wait_ge(qk["inverse"], n - 1)
                act.activation(ssr[:, w, :], aux[0][0:4, w * 512:w * 512 + T], ACT.Sqrt,
                               bias=C("eps", 0, 1, p=4), scale=1.0 / HD).then_inc(qk["rooted"], 1)
            return step

        jq, jk, jv, jo = (J[k] for k in ("q", "k", "v", "wo"))
        run(act, jq, split, first={0: [lambda: norm_hi("n0", 1, SEED)], 1: [lambda: norm_hi("n0", 2, SEED)],
                                   2: [lambda: norm_hi("n0", 3, SEED)]},
            every={3: [take_qkv(jq, 0, 0)], 7: [take_qkv(jq, 0, 1)]})
        for which, job in ((0, jk), (1, jv)):
            run(act, job, split, every={0: [qk_square(which, 0)], 1: [qk_root(which, 0), qk_square(which, 1)],
                                        2: [qk_root(which, 1)], 3: [take_qkv(job, 1 + which, 0)],
                                        7: [take_qkv(job, 1 + which, 1)]})
        act.wait_ge(qk["roped"], 9)
        act.wait_ge(unit_out, jv.unit_end(1, 1))
        with act.Fori(0, NH // 2) as i:
            for b in range(2):
                act.wait_ge(at["mixed"], 2 * i + b + 1)
                act.copy(qs[:, b, :], QKV[:, bass.ds(2 * i + b, 1), :]).then_inc(at["staged"], 1)
                act.copy(vs[:, b, :], QKV[:, bass.ds(2 * KT + 2 * i + b, 1), :]).then_inc(at["staged"], 1)
            for b in range(2):
                act.wait_ge(at["vturned"], 2 * i + b + 1)
                act.copy(vt[:, b, :], aux[b][:, 512:512 + T]).then_inc(at["vout"], 1)
            for b in range(2):
                for t, (a, e) in enumerate(((0, P), (P, 3 * P))):
                    act.wait_ge(at["neg"], 2 * i + b + 1)
                    act.activation(ex[:, b, a:e], sc[:, b, a:e], ACT.Exp, bias=st[:, b, 2 + t:3 + t],
                                   scale=HD ** -0.5, accum_out=st[:, b, 4 + t:5 + t]).then_inc(at["exped"], 1)
            for b in range(2):
                act.wait_ge(at["pturned"], 2 * i + b + 1)
                act.copy(pT[:, b, :], aux[b][:, 512:512 + 384]).then_inc(at["pout"], 1)
            for b in range(2):
                act.wait_ge(at["mixed"], 2 * i + b + 3)
                act.copy(hH[:, bass.ds(2 * i + b, 1), :], acc[b][:, 0:T]).then_inc(at["hi"], 1)

        def square(n, job, u):
            i, w = divmod(u, 2)

            def step(*_):
                act.wait_ge(unit_out, job.unit_end(i, w))
                if u >= 2:
                    act.wait_ge(N[n]["summed"], u - 1)
                act.activation(quad((sqacc if u == 0 else sq)[:, :]), xT[:, 4 * u:4 * u + 4, :],
                               ACT.Square).then_inc(N[n]["squared"], 1)
            return step

        def residual(n, job, first=None):
            a, b = job.units[0], job.m
            steps = dict(first or {})
            if n is None:
                run(act, job, split, first=steps)
                return
            steps.setdefault(a, []).append(square(n, job, 0))
            run(act, job, split, first=steps,
                late={0: [square(n, job, 1)]}, last={a: [square(n, job, 2)]})
            square(n, job, 3)()

        after = {"n1": "wo", "n3": "ro"}

        def ffn(layer):
            n = ("n1", "n3")[layer]
            ja, da, jb, db = (J[f"{k}{layer}{h}"] for k, h in (("up", "a"), ("dn", "a"), ("up", "b"), ("dn", "b")))
            norm_root(n)
            done = ja.first_panel
            norm_hi(n, 0, done)

            def steps(job, g0):
                u0 = layer * (HALF_A + HALF_B) + g0
                cw0 = PCV + layer * 4 * 88

                def take(w):
                    def step(i):
                        act.wait_ge(panel_used, job.panel_end(i, 4 * w + 3))
                        if not (u0 == 0 and w == 0 and isinstance(i, int)):
                            act.wait_ge(f["tap0"], (2 * (i + u0) + w) * 4)
                        act.copy(fu[:, :], acc[job.unit(0, w) % 2][:, :]).then_inc(unit_out, 1)
                    return step

                def init(w):
                    def step(i):
                        act.wait_ge(unit_out, job.unit_end(i, w))
                        if w:
                            act.wait_ge(f["silu"], i + u0 + 1)
                        elif not (u0 == 0 and isinstance(i, int)):
                            act.wait_ge(f["lo"], i + u0)
                        for k in range(4):
                            c = i * 4 + (g0 * 4 + w * FKT + k)
                            act.activation(fc[:, k * T:(k + 1) * T], fu[:, k * T:(k + 1) * T], ACT.Identity,
                                           bias=prm[:, bass.ds(c + (cw0 + 3 * 88), 1)],
                                           scale=prm[:, bass.ds(c + (cw0 + 2 * 88), 1)]).then_inc(f["init"], 1)
                    return step

                def silu(i):
                    act.wait_ge(f["tap0"], (2 * (i + u0)) * 4 + 4)
                    if not (u0 == 0 and isinstance(i, int)):
                        act.wait_ge(f["gated"], i + u0)
                    act.activation(sg[:, :], fc[:, :], ACT.Silu).then_inc(f["silu"], 1)

                def hi(i):
                    act.wait_ge(f["gated"], i + (u0 + 1))
                    act.copy(aH[:, bass.ds(i * 4, 4), :], quad(fc[:, :])).then_inc(f["hi"], 1)

                return ({3: [take(0)], 4: [init(0)], 5: [silu], 7: [take(1)]}, {0: [init(1)], 2: [hi]})

            for job, dn, g0 in ((ja, da, 0), (jb, db, HALF_A)):
                every, late = steps(job, g0)
                first = {}
                if g0 == 0:
                    first = {k: [lambda k=k: norm_hi(n, k + 1, done)] for k in range(3)}
                else:
                    first = {}
                run(act, job, split, first=first, every=every, late=late)
                tail = {j: [lambda g=g, job=job: g(job.n - 1) for g in fs] for j, fs in late.items()}
                residual(("n2" if layer == 0 and layers >= 3 else None) if g0 else None, dn, first=tail)

        residual("n1" if layers >= 2 else None, jo)
        if layers >= 2:
            ffn(0)

        if layers >= 3:
            norm_root("n2")
            mixes = {"rg": 5, "rv": 3, "rw": 1, "ra": 4, "rk": 2, "rr": 0}
            order_mix = list(mixes)

            def mix_hi(name, g, used):
                n = 4 * order_mix.index(name) + g

                def step(*_):
                    act.wait_ge(M["mixed"], 4 * n + 4)
                    act.wait_ge(panel_used, used)
                    act.copy(hH[:, 4 * g:4 * g + 4, :], quad(mt[:, :])).then_inc(M["hi"], 1)
                return step

            used = mix_used(J)
            for g in range(4):
                mix_hi("rg", g, used["rg"][g])()
            jg = J["rg"]
            split(act, jg, 0, 1)
            split(act, jg, 0, 2)

            def low_rank(job, panels, parts, width, func):
                k = ("rg", "rw", "ra").index(job.name)
                act.wait_ge(panel_used, job.panel_end(0, panels - 1))
                if k == 1:
                    act.wait_ge(M["v_spilled"], 64)
                if k:
                    act.wait_ge(M["low_lo"], k)
                act.activation(ru[0:parts, 0:width], acc[job.unit(0, 0) % 2][0:parts, 0:width], func)\
                   .then_inc(unit_out, 1)
                act.wait_ge(unit_out, job.unit_end(0, 0))
                act.copy(tH[0:parts, 0:width // T, :], ru[0:parts, 0:width].rearrange("p (f t) -> p f t", t=T))\
                   .then_inc(M["low_hi"], 1)

            low_rank(jg, 2, P, 2 * T, ACT.Sigmoid)
            split(act, jg, 0, 3)
            for u in range(4):
                if u == 3:
                    split(act, jg, 0, 4)
                act.wait_ge(M["low_unit"], u + 1)
                act.wait_ge(M["low_lo"], 1)
                if u:
                    act.wait_ge(M["g_spilled"], 16 * u)
                act.copy(ru[:, :], acc[jg.unit(0, 1 + u) % 2][:, :]).then_inc(unit_out, 1)

            def take_spill(job, done, before, w):
                def step(i):
                    u = 2 * i + w
                    act.wait_ge(panel_used, job.panel_end(i, 4 * w + 3))
                    if u:
                        act.wait_ge(M[done], 16 * u)
                    else:
                        act.wait_ge(before[0], before[1])
                    act.copy(ru[:, :], acc[job.unit(0, w) % 2][:, :]).then_inc(unit_out, 1)
                return step

            mix_hi("rv", 0, used["rv"][0])()
            run(act, J["rv"], split, first={k: [mix_hi("rv", k + 1, used["rv"][k + 1])] for k in range(3)},
                every={3: [take_spill(J["rv"], "v_spilled", (M["g_spilled"], 64), 0)],
                       7: [take_spill(J["rv"], "v_spilled", None, 1)]})
            for name, func, bias in (("rw", ACT.Tanh, W0), ("ra", ACT.Copy, A0)):
                job = J[name]
                for g in range(4):
                    mix_hi(name, g, used[name][g])()
                split(act, job, 0, 1)
                low_rank(job, 1, LORA, T, func)
                for u in range(4):
                    if u == 3:
                        split(act, job, 0, 2)
                    act.wait_ge(M["low_unit"], 4 + (4 if name == "ra" else 0) + u + 1)
                    for k in range(4):
                        ft = 4 * u + k
                        src = acc[job.unit(0, 1 + u) % 2][:, k * T:(k + 1) * T]
                        dst = ab[:, ft, :]
                        if name == "rw":
                            src, dst = src.rearrange("p (c t) -> p c t", c=2), cw[:, ft, :, 1:129]
                        ins = act.activation(dst, src, ACT.Sigmoid, bias=prm[:, bias + ft:bias + ft + 1])
                    ins.then_inc(unit_out, 1)

            def take_k(w):
                def step(i):
                    job = J["rk"]
                    act.wait_ge(panel_used, job.panel_end(i, 4 * w + 3))
                    act.copy(kb[:, 8 * i + 4 * w:8 * i + 4 * w + 4, :], quad(acc[job.unit(0, w) % 2][:, :]))\
                       .then_inc(unit_out, 1)
                return step

            mix_hi("rk", 0, used["rk"][0])()
            run(act, J["rk"], split, first={k: [mix_hi("rk", k + 1, used["rk"][k + 1])] for k in range(3)},
                every={3: [take_k(0)], 7: [take_k(1)]})
            mix_hi("rr", 0, used["rr"][0])()

            def kk_square(w):
                def step(i):
                    u = 2 * i + w
                    act.wait_ge(unit_out, J["rk"].unit_end(i, w))
                    act.wait_ge(M["lo"], 24)
                    if u >= 2:
                        act.wait_ge(M["kk"], u - 1)
                    for k in range(4):
                        ft = 4 * u + k
                        act.activation(kkr[:, w, k * T:(k + 1) * T], kb[:, ft, :], ACT.Copy,
                                       scale=prm[:, K_K + ft:K_K + ft + 1]).then_inc(M["kkr"], 1)
                    if u:
                        act.wait_ge(M["ksum"], u)
                    act.wait_ge(M["kkr"], 4 * u + 4)
                    act.activation(kq[:, :], kkr[:, w, :], ACT.Square).then_inc(M["ksq"], 1)
                return step

            def kk_root(w):
                def step(i):
                    u = 2 * i + w
                    act.wait_ge(M["ksum"], u + 1)
                    if u >= 2:
                        act.wait_ge(M["krec"], u - 1)
                    act.activation(kss[:, w, :], aux[0][0:8, w * 512:w * 512 + T], ACT.Sqrt)\
                       .then_inc(M["kroot"], 1)
                return step

            run(act, J["rr"], split, first={k: [mix_hi("rr", k + 1, used["rr"][k + 1])] for k in range(3)},
                every={3: [kk_square(0), take_spill(J["rr"], "r_spilled", (M["v_spilled"], 64), 0)],
                       4: [kk_root(0), kk_square(1)], 5: [kk_root(1)],
                       7: [take_spill(J["rr"], "r_spilled", None, 1)]})
            core_act(act)
            residual("n3" if layers >= 4 else None, J["ro"])
        if layers >= 4:
            ffn(1)
        for g in range(8):
            act.wait_ge(out_turned, g + 1)
            act.copy(xo[:, :, 2 * P * g:2 * P * (g + 1)].rearrange("p t (k q) -> p k t q", q=P),
                     bank(4 + g % 4).rearrange("p (k t q) -> p k t q", k=2, q=P)).then_inc(out_ready, 1)

    @block.vector
    def _(dve):
        def split(eng, job, i, j):
            job, i, j = next_place(job, i, j)
            dve.wait_ge(hi_split, job.panel_end(i, j))
            dve.tensor_tensor(wl[:, job.hl[j], :], raw[:, job.raw[j], :], wh[:, job.hl[j], :].bitcast(f32),
                              ALU.subtract).then_inc(lo_split, 1)

        def norm_rstd(n, units=4):
            dve.wait_ge(N[n]["rooted"], 1)
            dve.reciprocal(rstd[:, :], rstd[:, :]).then_inc(N[n]["rstd"], 1)

        def norm_group(n, g, gain):
            dve.wait_ge(N[n]["rstd"], 1)
            if g >= 2:
                dve.wait_ge(N[n]["lo"], g - 1)
            for k in range(4):
                kt = 4 * g + k
                dve.scalar_tensor_tensor(hf[:, g % 2, k * T:(k + 1) * T], xT[:, kt, :],
                                         prm[:, gain + kt:gain + kt + 1], rstd[:, :], ALU.mult, ALU.mult)\
                   .then_inc(N[n]["normed"], 1)
            dve.wait_ge(N[n]["hi"], g + 1)
            dve.tensor_tensor(hL[:, 4 * g:4 * g + 4, :], quad(hf[:, g % 2, :]),
                              hH[:, 4 * g:4 * g + 4, :].bitcast(f32), ALU.subtract).then_inc(N[n]["lo"], 1)

        def add_squares(n, u):
            def step(*_):
                dve.wait_ge(N[n]["squared"], u + 1)
                if u >= 2:
                    dve.wait_ge(N[n]["summed"], u - 1)
                dve.tensor_tensor(sqacc[:, :], sqacc[:, :], sq[:, :], ALU.add).then_inc(N[n]["summed"], 1)
            return step

        split(dve, J["q"], 0, 0)
        for u in range(1, 4):
            add_squares("n0", u)()
        dve.wait_ge(turned_out, 11)
        dve.tensor_scalar(prm[:, OMKA:OMKA + 16], prm[:, K_A:K_A + 16], -1.0, 1.0, ALU.mult, ALU.add)\
           .then_inc(omka_done, 1)
        norm_rstd("n0")
        norm_group("n0", 0, G_MOBA)

        def qk_inverse(which, w):
            def step(i):
                n = 4 * which + 2 * i + w
                dve.wait_ge(qk["rooted"], n + 1)
                if n >= 2:
                    dve.wait_ge(qk["spread"], n - 1)
                dve.reciprocal(rsr[:, w, :], ssr[:, w, :]).then_inc(qk["inverse"], 1)
            return step

        def qk_norm(which, w):
            def step(i):
                n = 4 * which + 2 * i + w
                dve.wait_ge(qk["spread"], n + 1)
                for k in range(4):
                    dve.scalar_tensor_tensor(nrmd[:, k * T:(k + 1) * T], QKV[:, which * KT + i * 8 + (4 * w + k), :],
                                             prm[:, (QG, KG)[which]:(QG, KG)[which] + 1],
                                             aux[1][:, k * T:(k + 1) * T], ALU.mult, ALU.mult)\
                       .then_inc(qk["normed"], 1)
            return step

        def qk_rope(which, w):
            def step(i):
                n = 4 * which + 2 * i + w
                part = QKV[:, which * KT + i * 8 + 4 * w:which * KT + i * 8 + 4 * w + 4, :]
                dve.wait_ge(qk["turned"], n + 1)
                dve.wait_ge(qk["normed"], 4 * n + 4)
                dve.wait_ge(qk["roped"], n + 1)
                dve.tensor_tensor(quad(rot[:, :]), quad(aux[0][:, :]), spread(R("sin"), 4), ALU.mult)\
                   .then_inc(qk["sined"], 1)
                dve.tensor_tensor(part, quad(nrmd[:, :]), spread(R("cos"), 4), ALU.mult).then_inc(qk["cosed"], 1)
                dve.wait_ge(qk["sined"], n + 1)
                dve.wait_ge(qk["cosed"], n + 1)
                dve.tensor_tensor(part, part, quad(rot[:, :]), ALU.add).then_inc(qk["roped"], 1)
            return step

        jq, jk, jv, jo = (J[k] for k in ("q", "k", "v", "wo"))
        run(dve, jq, split, first={g: [lambda g=g: norm_group("n0", g + 1, G_MOBA)] for g in range(3)})
        for which, job in ((0, jk), (1, jv)):
            run(dve, job, split, every={1: [qk_inverse(which, 0)], 2: [qk_inverse(which, 1)],
                                        3: [qk_norm(which, 0)], 4: [qk_rope(which, 0)],
                                        5: [qk_norm(which, 1)], 6: [qk_rope(which, 1)]})
        with dve.Fori(0, NH // 2) as i:
            for b in range(2):
                dve.wait_ge(at["scored"], 2 * i + (b + 1))
                dve.tensor_tensor(sc[:, b, :], aux[b][:, 0:384], R("cmask"), ALU.add).then_inc(at["masked"], 1)
                dve.wait_ge(at["masked"], 2 * i + (b + 1))
                for t, (a, e) in enumerate(((0, P), (P, 3 * P))):
                    dve.reduce_max(st[:, b, t:t + 1], sc[:, b, a:e], AX.X).then_inc(at["maxed"], 1)
                dve.wait_ge(at["maxed"], 4 * i + (2 * b + 2))
                dve.tensor_scalar(st[:, b, 2:4], st[:, b, 0:2], -(HD ** -0.5), None, ALU.mult)\
                   .then_inc(at["neg"], 1)
            for b in range(2):
                dve.wait_ge(at["exped"], 4 * i + (2 * b + 2))
                dve.reciprocal(st[:, b, 6:8], st[:, b, 4:6]).then_inc(at["recip"], 1)
                dve.wait_ge(at["recip"], 2 * i + (b + 1))
                for t, (a, e) in enumerate(((0, P), (P, 3 * P))):
                    dve.tensor_scalar(ex[:, b, a:e], ex[:, b, a:e], st[:, b, 6 + t:7 + t], None, ALU.mult)\
                       .then_inc(at["probs"], 1)
            for b in range(2):
                dve.wait_ge(at["hi"], 2 * i + (b + 1))
                dve.tensor_tensor(hL[:, bass.ds(2 * i + b, 1), :], acc[b][:, 0:T].unsqueeze(1),
                                  hH[:, bass.ds(2 * i + b, 1), :].bitcast(f32), ALU.subtract).then_inc(at["lo"], 1)

        def add_unit(job, n, before):
            def step(w):
                def go(i):
                    dve.wait_ge(panel_used, job.panel_end(i, job.last_panel[w]))
                    if before:
                        before()
                    u = 2 * i + w
                    part = xT[:, 4 * u:4 * u + 4, :]
                    dve.tensor_tensor(part, part, quad(acc[job.unit(0, w) % 2][:, :]), ALU.add)\
                       .then_inc(unit_out, 1)
                return go
            return step

        def residual(n, job, first=None, before=None):
            a, m = job.units[0], job.m
            add = add_unit(job, n, before)
            steps = {k: list(v) for k, v in (first or {}).items()}
            if n is None:
                run(dve, job, split, first=steps, every={a - 1: [add(0)], m - 1: [add(1)]})
                return
            run(dve, job, split, first=steps, every={a - 1: [add(0)], m - 1: [add(1)]},
                late={1: [add_squares(n, 1)]}, last={a: [add_squares(n, 2)]})
            add_squares(n, 3)()

        def ffn(layer):
            n = ("n1", "n3")[layer]
            gain = G_FFN + 16 * layer
            ja, da, jb, db = (J[f"{k}{layer}{h}"] for k, h in (("up", "a"), ("dn", "a"), ("up", "b"), ("dn", "b")))
            norm_rstd(n)
            norm_group(n, 0, gain)

            def steps(job, g0):
                u0 = layer * (HALF_A + HALF_B) + g0
                cw0 = PCV + layer * 4 * 88

                def conv(w):
                    def step(i):
                        t0 = (2 * (i + u0) + w) * 4
                        for name, tap in (("tap1", 1), ("tap0", 2)):
                            for k in range(4):
                                a, e = k * T, (k + 1) * T
                                if tap == 1:
                                    dve.wait_ge(f["init"], t0 + (k + 1))
                                else:
                                    dve.wait_ge(f["tap1"], t0 + (k + 1))
                                c = i * 4 + (g0 * 4 + w * FKT + k + cw0 + (2 - tap) * 88)
                                dve.scalar_tensor_tensor(fc[:, a + tap:e], fu[:, a:e - tap],
                                                         prm[:, bass.ds(c, 1)], fc[:, a + tap:e],
                                                         ALU.mult, ALU.add).then_inc(f[name], 1)
                    return step

                def gate(i):
                    dve.wait_ge(f["silu"], i + (u0 + 1))
                    dve.wait_ge(f["tap0"], i * 8 + (8 * u0 + 8))
                    dve.tensor_tensor(fc[:, :], fc[:, :], sg[:, :], ALU.mult).then_inc(f["gated"], 1)

                def lo(i):
                    dve.wait_ge(f["hi"], i + (u0 + 1))
                    dve.tensor_tensor(aL[:, bass.ds(i * 4, 4), :], quad(fc[:, :]),
                                      aH[:, bass.ds(i * 4, 4), :].bitcast(f32), ALU.subtract).then_inc(f["lo"], 1)

                return {4: [conv(0)]}, {0: [conv(1)], 1: [gate], 2: [lo]}

            for job, dn, g0 in ((ja, da, 0), (jb, db, HALF_A)):
                every, late = steps(job, g0)
                first = {}
                if g0 == 0:
                    first = {g: [lambda g=g: norm_group(n, g + 1, gain)] for g in range(3)}
                run(dve, job, split, first=first, every=every, late=late)
                tail = {j: [lambda g=g, job=job: g(job.n - 1) for g in fs] for j, fs in late.items()}
                residual(("n2" if layer == 0 and layers >= 3 else None) if g0 else None, dn, first=tail)

        residual("n1" if layers >= 2 else None, jo)
        if layers >= 2:
            ffn(0)

        if layers >= 3:
            norm_rstd("n2")
            dve.wait_ge(N["n2"]["rstd"], 1)
            for kt in range(KT):
                dve.scalar_tensor_tensor(hb[:, kt, :], xT[:, kt, :], prm[:, G_RWKV + kt:G_RWKV + kt + 1], rstd[:, :],
                                         ALU.mult, ALU.mult).then_inc(M["h"], 1)
            for g in range(4):
                a, e = 4 * g, 4 * g + 4
                dve.wait_ge(M["h"], e)
                dve.tensor_scalar(xx[:, a:e, 0:1], hb[:, a:e, 0:1], -1.0, None, ALU.mult).then_inc(M["xx"], 1)
                dve.tensor_tensor(xx[:, a:e, 1:T], hb[:, a:e, 0:T - 1], hb[:, a:e, 1:T], ALU.subtract)\
                   .then_inc(M["xx"], 1)
            mixes = {"rg": 5, "rv": 3, "rw": 1, "ra": 4, "rk": 2, "rr": 0}
            order_mix = list(mixes)

            def mix(name, g):
                n = 4 * order_mix.index(name) + g

                def step(*_):
                    dve.wait_ge(M["xx"], 2 * g + 2)
                    if n:
                        dve.wait_ge(M["lo"], n)
                    for k in range(4):
                        kt = 4 * g + k
                        col = MU + 16 * mixes[name] + kt
                        dve.scalar_tensor_tensor(mt[:, k * T:(k + 1) * T], xx[:, kt, :], prm[:, col:col + 1],
                                                 hb[:, kt, :], ALU.mult, ALU.add).then_inc(M["mixed"], 1)
                    dve.wait_ge(M["hi"], n + 1)
                    dve.tensor_tensor(hL[:, 4 * g:4 * g + 4, :], quad(mt[:, :]),
                                      hH[:, 4 * g:4 * g + 4, :].bitcast(f32), ALU.subtract).then_inc(M["lo"], 1)
                return step

            def low_lo(k, parts, width):
                dve.wait_ge(M["low_hi"], k + 1)
                dve.tensor_tensor(tL[0:parts, 0:width // T, :],
                                  ru[0:parts, 0:width].rearrange("p (f t) -> p f t", t=T),
                                  tH[0:parts, 0:width // T, :].bitcast(f32), ALU.subtract).then_inc(M["low_lo"], 1)

            jg = J["rg"]
            for g in range(4):
                mix("rg", g)()
            split(dve, jg, 0, 1)
            split(dve, jg, 0, 2)
            low_lo(0, P, 2 * T)
            split(dve, jg, 0, 3)
            split(dve, jg, 0, 4)
            mix("rv", 0)()
            run(dve, J["rv"], split, first={k: [mix("rv", k + 1)] for k in range(3)})
            dve.memset(cw[:, :, :, 0:1], 0.0).then_inc(M["zeroed"], 1)
            for k, name in ((1, "rw"), (2, "ra")):
                for g in range(4):
                    mix(name, g)()
                split(dve, J[name], 0, 1)
                low_lo(k, LORA, T)
                split(dve, J[name], 0, 2)

            def decay_sum(j):
                def step(i):
                    ft = 8 * i + j
                    dve.wait_ge(unit_out, J["rw"].unit_end(0, 1 + ft // 4))
                    dve.wait_ge(M["zeroed"], 1)
                    for c in range(2):
                        dve.tensor_tensor_scan(cw[:, ft, c, 1:129], C("ones"), cw[:, ft, c, 1:129], 0.0,
                                               ALU.mult, ALU.add).then_inc(M["scan"], 1)
                    dve.wait_ge(M["scan"], 2 * ft + 2)
                    if ft:
                        dve.wait_ge(M["cw"], 2 * ft)
                    dve.tensor_copy(mid[:, 0:2].unsqueeze(2), cw[:, ft, :, 64:65]).then_inc(M["mid"], 1)
                    dve.wait_ge(M["mid"], ft + 1)
                    for c in range(2):
                        dve.tensor_scalar(cw[:, ft, c, :], cw[:, ft, c, :], mid[:, c:c + 1], -EXPM05,
                                          ALU.subtract, ALU.mult).then_inc(M["cw"], 1)
                return step

            mix("rk", 0)()
            run(dve, J["rk"], split, first={k: [mix("rk", k + 1)] for k in range(3)},
                every={j: [decay_sum(j)] for j in range(8)})
            mix("rr", 0)()

            def kk_inverse(w):
                def step(i):
                    u = 2 * i + w
                    dve.wait_ge(M["kroot"], u + 1)
                    if u >= 2:
                        dve.wait_ge(M["kspread"], u - 1)
                    dve.tensor_scalar(kss[:, w, :], kss[:, w, :], 1e-12, None, ALU.max).then_inc(M["kmax"], 1)
                    dve.wait_ge(M["kmax"], u + 1)
                    dve.reciprocal(krs[:, w, :], kss[:, w, :]).then_inc(M["krec"], 1)
                return step

            def kk_finish(w):
                def step(i):
                    u = 2 * i + w
                    a, e = 4 * u, 4 * u + 4
                    dve.wait_ge(M["kspread"], u + 1)
                    dve.tensor_tensor(kkb[:, a:e, :], quad(aux[1][:, :]), quad(kkr[:, w, :]), ALU.mult)\
                       .then_inc(M["kk"], 1)
                    dve.wait_ge(M["lo"], 24)
                    if u:
                        dve.wait_ge(M["kmod"], u)
                    dve.wait_ge(unit_out, J["ra"].unit_end(0, 4))
                    for k in range(4):
                        ft = 4 * u + k
                        dve.tensor_scalar(mt[:, k * T:(k + 1) * T], ab[:, ft, :], prm[:, K_A + ft:K_A + ft + 1],
                                          prm[:, OMKA + ft:OMKA + ft + 1], ALU.mult, ALU.add).then_inc(M["kfac"], 1)
                    dve.wait_ge(M["kfac"], 4 * u + 4)
                    dve.tensor_tensor(kb[:, a:e, :], kb[:, a:e, :], quad(mt[:, :]), ALU.mult).then_inc(M["kmod"], 1)
                    dve.wait_ge(M["kk"], u + 1)
                    dve.tensor_tensor(ab[:, a:e, :], ab[:, a:e, :], kkb[:, a:e, :], ALU.mult).then_inc(M["kb"], 1)
                return step

            run(dve, J["rr"], split, first={k: [mix("rr", k + 1)] for k in range(3)},
                every={4: [kk_inverse(0)], 5: [kk_inverse(1)], 6: [kk_finish(0)], 7: [kk_finish(1)]})

            dve.wait_ge(M["x_spilled"], 16)
            dve.tensor_copy(Qb[:, :, :], spread(C("ident"), LEVELS * 4)).then_inc(W["zeroed"], 1)
            dve.wait_ge(M["kb"], 4)
            dve.wait_ge(M["r_spilled"], 64)
            for k in range(2):
                dve.memset(ars[k][:, :, :, :, :].rearrange("p h c a t -> p (h c a t)"), 0.0)\
                   .then_inc(W["zeroed"], 1)
            dve.wait_ge(W["zeroed"], 3)

            def body(b, f, n):
                def gram(c):
                    p, k = f
                    dve.wait_ge(W["gram"], p * 2 + (c + 1))
                    if has(p, 2):
                        dve.wait_ge(W["ymm"], pairs_before(p, 2, 1))
                    dve.tensor_tensor(mBs[k][:, c], bank(c).rearrange("p (h n) -> p h n", h=2),
                                      spread(C("mb"), 2), ALU.mult).then_inc(W["gmask"], 1)
                    dve.tensor_tensor(mKs[k][:, c], bank(2 + c).rearrange("p (h n) -> p h n", h=2),
                                      spread(C("mk"), 2), ALU.mult).then_inc(W["gmask"], 1)
                    dve.wait_ge(W["gmask"], p * 4 + (2 * c + 1))
                    dve.tensor_tensor(mBs[k][:, c, :, 0:P], mBs[k][:, c, :, 0:P], spread(C("ident"), 2), ALU.add)\
                       .then_inc(W["geye"], 1)

                def xt0(c):
                    p, k = f
                    dve.wait_ge(W["geye"], p * 2 + (c + 1))
                    dve.tensor_tensor(XTs[k][:, c], mBs[k][:, c, :, 0:P], spread(C("mx1t"), 2), ALU.mult)\
                       .then_inc(W["xt0"], 1)

                def x0(c):
                    p, k = f
                    dve.wait_ge(W["lev0"], p * 2 + (c + 1))
                    dve.tensor_tensor(X[:, c], bank(c)[:, 0:T].rearrange("p (h n) -> p h n", h=2),
                                      spread(C("mx1"), 2), ALU.mult).then_inc(W["x0"], 1)

                def level(lev):
                    p, k = f
                    s = 1 << lev
                    lv = C("lv", P * (lev - 1), P * lev)
                    for c in range(2):
                        dve.wait_ge(W["lp"], p * 12 + (2 * (lev - 1) + c + 1))
                        dve.tensor_tensor(blocks(Ql(lev, c), s, 0), compact(bank(c)[:, 0:P], s), compact(lv, s),
                                          ALU.mult).then_inc(W["lq"], 1)

                if f:
                    gram(0)
                    gram(1)
                    xt0(0)
                    xt0(1)
                if b:
                    p, k = b
                    dve.wait_ge(W["smm"], p + 1)
                    dve.tensor_scalar(s0[:, :], bank(6)[:, 0:RH], scl[:, k:k + 1], None, ALU.mult)\
                       .then_inc(W["sout"], 1)
                if f:
                    x0(0)
                    x0(1)
                    level(1)
                    level(2)
                if b:
                    p, k = b
                    dve.wait_ge(W["mean"], p + 1)
                    if has(p, 1):
                        dve.wait_ge(W["hi"], p)
                        dve.wait_ge(W["lo"], p)
                    dve.scalar_tensor_tensor(y2[:, :], bank(5)[:, 0:T], -1.0 / RH, ys[:, :], ALU.mult, ALU.add)\
                       .then_inc(W["cent"], 1)
                if f:
                    level(3)
                    level(4)
                if b:
                    p, k = b
                    dve.wait_ge(W["std"], p + 1)
                    dve.reciprocal(y3[:, :], y3[:, :]).then_inc(W["rec"], 1)
                    dve.wait_ge(W["rec"], p + 1)
                    dve.wait_ge(W["cent"], p + 1)
                    dve.tensor_tensor(y2[:, :], y2[:, :], y3[:, :], ALU.mult).then_inc(W["norm"], 1)
                if f:
                    level(5)
                if b:
                    p, k = b
                    dve.wait_ge(W["norm"], p + 1)
                    dve.tensor_scalar(y2[:, :], y2[:, :], prm[:, bass.ds(p + LNW, 1)], prm[:, bass.ds(p + LNB, 1)],
                                      ALU.mult, ALU.add).then_inc(W["aff"], 1)
                    dve.wait_ge(W["bmm"], p + 1)
                    dve.tensor_tensor(y3[:, :], bank(6)[:, 0:T], vbs[k][:, :], ALU.mult).then_inc(W["bon"], 1)
                    dve.wait_ge(W["bon"], p + 1)
                    dve.wait_ge(W["aff"], p + 1)
                    dve.tensor_tensor(y2[:, :], y2[:, :], y3[:, :], ALU.add).then_inc(W["ysum"], 1)
                    dve.wait_ge(W["ysum"], p + 1)
                    dve.wait_ge(W["g_in"], p * 16 + 16)
                    dve.tensor_tensor(y2[:, :], y2[:, :], gb[:, :], ALU.mult).then_inc(W["gate"], 1)
                if f:
                    level(6)
                if b:
                    p, k = b
                    dve.wait_ge(W["hi"], p + 1)
                    dve.tensor_tensor(hL[:, bass.ds(p, 1), :], y2[:, :].unsqueeze(1),
                                      hH[:, bass.ds(p, 1), :].bitcast(f32), ALU.subtract).then_inc(W["lo"], 1)
                if n:
                    p, k = n
                    dve.wait_ge(W["exps"], p * 3 + 3)
                    if has(p, 2):
                        dve.wait_ge(W["bmm"], pairs_before(p, 2, 1))
                    if has(p, 1):
                        dve.wait_ge(W["gram"], p * 2)
                    for h, r in heads:
                        dve.scalar_tensor_tensor(ars[k][r, h, :, 0, :],
                                                 kkp(p, rows=r).rearrange("p (c t) -> p c t", c=2),
                                                 -1.0, e1[r, :, 0:P], ALU.mult, ALU.mult).then_inc(W["scaled"], 1)
                    dve.tensor_tensor(bt[:, :, :], abp(p).rearrange("p (c t) -> p c t", c=2), e2[:, :, :], ALU.mult)\
                       .then_inc(W["scaled"], 1)
                    dve.tensor_tensor(kt_[:, :, :], kbp(p).rearrange("p (c t) -> p c t", c=2), e2[:, :, :], ALU.mult)\
                       .then_inc(W["scaled"], 1)
                    dve.wait_ge(W["r_in"], p * 16 + 16)
                    for h, r in heads:
                        dve.tensor_tensor(ars[k][r, h, :, 1, :], rb[r, :].rearrange("p (c t) -> p c t", c=2),
                                          e1[r, :, 1:129], ALU.mult).then_inc(W["scaled"], 1)
                    dve.wait_ge(W["scaled"], p * 6 + 6)
                    for h, r in heads:
                        dve.scalar_tensor_tensor(bps[k][r, :].rearrange("p (c t) -> p c t", c=2),
                                                 ars[k][r, h, :, 1, :], prm[r, bass.ds(p + R_K, 1)],
                                                 kt_[r, :, :], ALU.mult, ALU.mult).then_inc(W["bonusp"], 1)

            core(body, dve)

            residual("n3" if layers >= 4 else None, J["ro"], before=lambda: dve.wait_ge(M["x_back"], 16))
        if layers >= 4:
            ffn(1)

    @block.gpsimd
    def _(pool):
        if layers < 3:
            return
        xs = x_spill
        pool.wait_ge(M["h"], KT)
        pool.dma_start(xs, xT[:, :, :]).then_inc(M["x_spilled"], 16)
        for u in range(4):
            pool.wait_ge(unit_out, J["rg"].unit_end(0, 1 + u))
            pool.dma_start(g_spill[:, 4 * u:4 * u + 4, :], quad(ru[:, :])).then_inc(M["g_spilled"], 16)
        for name, dst, done in (("rv", v_spill, "v_spilled"), ("rr", r_spill, "r_spilled")):
            for u in range(4):
                pool.wait_ge(unit_out, J[name].unit_end(*divmod(u, 2)))
                pool.dma_start(dst[:, 4 * u:4 * u + 4, :], quad(ru[:, :])).then_inc(M[done], 16)
        pool.wait_ge(W["lo"], KT)
        pool.dma_start(xT[:, :, :], xs).then_inc(M["x_back"], 16)
        for s, n in ((M["x_spilled"], 16), (M["g_spilled"], 64), (M["v_spilled"], 64), (M["r_spilled"], 64),
                     (M["x_back"], 16)):
            pool.wait_ge(s, n)

    @block.tensor
    def _(pe):
        def products(job, src, ready, every=None):
            every = every or {}

            def body(i):
                j = 0
                for w, panels in enumerate(job.units):
                    a = acc[job.unit(0, w) % 2]
                    for p in range(panels):
                        pe.wait_ge(lo_split, job.panel_end(i, j))
                        if p == 0:
                            pe.wait_ge(unit_out, job.unit_end(i, w) - 2)
                        ready(p)
                        s = job.hl[j]
                        for q in range(4):
                            hi, lo = src(4 * p + q)
                            for ft in range(4):
                                at_ = q * UNIT + ft * P
                                for n, (wt, h) in enumerate(((wh, hi), (wh, lo), (wl, hi))):
                                    mm = pe.matmul(a[:, ft * T:(ft + 1) * T], wt[:, s, at_:at_ + P], h,
                                                   start=(p == 0 and q == 0 and n == 0 and ft % 2 == 0),
                                                   stop=(p == panels - 1 and q == 3 and n == 2),
                                                   skip_group_check=True)
                        mm.then_inc(panel_used, 1)
                        for f in every.get(j, ()):
                            f(i)
                        j += 1

            if job.n == 1:
                body(0)
            else:
                with pe.Fori(0, job.n) as i:
                    body(i)

        def h_in(kt):
            return hH[:, kt, :], hL[:, kt, :]

        def a_in(kt):
            return aH[:, kt, :], aL[:, kt, :]

        pe.sem_inc(panel_used, SEED)
        pe.sem_inc(hi_split, SEED)
        pe.sem_inc(lo_split, SEED)
        pe.sem_inc(unit_out, 2)
        pe.sem_inc(at["mixed"], 2)
        pe.sem_inc(qk["roped"], 1)
        pe.wait_ge(const_in, 32)
        pe.wait_ge(x_in, 32)
        for g in range(8):
            if g >= 4:
                pe.wait_ge(turned_out, g - 3)
            for k in range(2):
                for tt in range(2):
                    mm = pe.transpose(bank(4 + g % 4)[:, (2 * k + tt) * P:(2 * k + tt + 1) * P],
                                      xin[:, tt, (2 * g + k) * P:(2 * g + k + 1) * P], C("ident"))
            mm.then_inc(turned, 1)
        pe.wait_ge(rows_in, 16 * ROW_LOADS)
        for g, tiles in enumerate(((0, 1, 2), (3, 4, 5, 6), (7, 8, 9, 10))):
            pe.wait_ge(turned_out, 5 + g)
            at_ = 0
            for tile in tiles:
                n = {0: 128, 1: 112, 2: 34}.get(tile, 88)
                mm = pe.transpose(bank(4 + g)[:, at_:at_ + n], prow[0:n, tile, :], C("ident", 0, n, p=n))
                at_ += n
            mm.then_inc(turned, 1)

        def norm_total(n, sq_from=3):
            pe.wait_ge(N[n]["summed"], sq_from)
            for k in range(4):
                mm = pe.matmul(aux[0][:, 0:T], C("ones"), sqacc[:, k * T:(k + 1) * T], start=(k == 0), stop=(k == 3))
            mm.then_inc(N[n]["total"], 1)

        pe.wait_ge(turned_out, 9)
        norm_total("n0")

        def qk_sum(which, w):
            def step(i):
                n = i * 2 + (4 * which + w)
                pe.wait_ge(qk["squared"], n + 1)
                pe.wait_ge(qk["roped"], n - (w - 1))
                for k in range(4):
                    mm = pe.matmul(aux[0][0:4, w * 512:w * 512 + T], R("ssum", 4 * k, 4 * k + 4),
                                   sq2[:, w, k * T:(k + 1) * T], start=(k == 0), stop=(k == 3))
                mm.then_inc(qk["summed"], 1)
            return step

        def qk_spread(which, w):
            def step(i):
                n = i * 2 + (4 * which + w)
                pe.wait_ge(qk["inverse"], n + 1)
                if which or w:
                    pe.wait_ge(qk["normed"], 4 * n)
                for k in range(4):
                    mm = pe.matmul(aux[1][:, k * T:(k + 1) * T], R("sbc", k * P, (k + 1) * P, p=4), rsr[:, w, :],
                                   start=True, stop=True)
                mm.then_inc(qk["spread"], 1)
            return step

        def qk_turn(which, w):
            def step(i):
                n = i * 2 + (4 * which + w)
                pe.wait_ge(qk["normed"], 4 * n + 4)
                for k in range(2):
                    mm = pe.matmul(aux[0][:, k * 512:(k + 1) * 512], R("perm"), nrmd[:, k * 512:(k + 1) * 512],
                                   start=True, stop=True)
                mm.then_inc(qk["turned"], 1)
            return step

        def normed(n):
            return lambda p: pe.wait_ge(N[n]["lo"], p + 1)

        jq, jk, jv, jo = (J[k] for k in ("q", "k", "v", "wo"))
        products(jq, h_in, normed("n0"))
        for which, job in ((0, jk), (1, jv)):
            products(job, h_in, normed("n0"),
                     every={0: [qk_sum(which, 0)], 1: [qk_sum(which, 1)], 2: [qk_spread(which, 0)],
                            3: [qk_turn(which, 0)], 4: [qk_spread(which, 1)], 5: [qk_turn(which, 1)]})
        pe.wait_ge(qk["roped"], 9)
        with pe.Fori(0, NH // 2) as i:
            for b in range(2):
                pe.wait_ge(at["staged"], 4 * i + (2 * b + 2))
                for (a, e), qa in (((0, P), 0), ((P, 3 * P), P)):
                    k = QKV[:, bass.ds(i * 2 + (KT + b), 1), 0:e - a].rearrange("p a t -> p (a t)")
                    mm = pe.matmul(aux[b][:, a:e], qs[:, b, qa:qa + P], k, start=True, stop=True)
                mm.then_inc(at["scored"], 1)
                for t in range(2):
                    mm = pe.transpose(aux[b][:, 512 + t * P:512 + (t + 1) * P], vs[:, b, t * P:(t + 1) * P],
                                      C("ident"))
                mm.then_inc(at["vturned"], 1)
            for b in range(2):
                pe.wait_ge(at["probs"], 4 * i + (2 * b + 2))
                pe.wait_ge(at["vout"], 2 * i + (b + 1))
                for n, a in enumerate((0, P, 2 * P)):
                    mm = pe.transpose(aux[b][:, 512 + n * P:512 + (n + 1) * P], ex[:, b, a:a + P], C("ident"))
                mm.then_inc(at["pturned"], 1)
            for b in range(2):
                pe.wait_ge(at["pout"], 2 * i + (b + 1))
                pe.matmul(acc[b][:, 0:T], vt[:, b, 0:P], pT[:, b, 0:T], start=True, stop=True,
                          skip_group_check=True)
                pe.matmul(acc[b][:, P:T], vt[:, b, P:T], pT[:, b, T:T + P], start=False, stop=True,
                          skip_group_check=True).then_inc(at["mixed"], 1)

        products(jo, h_in, lambda p: pe.wait_ge(at["lo"], NH))

        def ffn(layer):
            n = ("n1", "n3")[layer]
            norm_total(n)
            for h, g0 in (("a", 0), ("b", HALF_A)):
                products(J[f"up{layer}{h}"], h_in, normed(n))
                u0 = layer * (HALF_A + HALF_B) + g0
                products(J[f"dn{layer}{h}"], a_in, lambda p, u0=u0: pe.wait_ge(f["lo"], u0 + p + 1))

        if layers >= 2:
            ffn(0)
        if layers >= 3:
            norm_total("n2")
            mixed = {name: (lambda p, k=k: pe.wait_ge(M["lo"], 4 * k + p + 1))
                     for k, name in enumerate(("rg", "rv", "rw", "ra", "rk", "rr"))}

            def triple(out_, col, lhs, kt_hi, kt_lo, parts, first, last, clear):
                for n, (wt, h) in enumerate(((wh, kt_hi), (wh, kt_lo), (wl, kt_hi))):
                    mm = pe.matmul(out_, lhs(wt), h, start=(first and clear and n == 0), stop=(last and n == 2),
                                   skip_group_check=True)
                return mm

            def low_units(job, k, slots, parts):
                pe.wait_ge(M["low_lo"], k + 1)
                for u in range(4):
                    a = acc[job.unit(0, 1 + u) % 2]
                    pe.wait_ge(unit_out, job.unit_end(0, 1 + u) - 2)
                    for ft in range(4):
                        col = (4 * u + ft) * P
                        for q, s in enumerate(slots):
                            mm = triple(a[:, ft * T:(ft + 1) * T], col, lambda wt, s=s: wt[0:parts, s, col:col + P],
                                        tH[0:parts, q, :], tL[0:parts, q, :], parts, q == 0, q == len(slots) - 1,
                                        ft % 2 == 0)
                    mm.then_inc(M["low_unit"], 1)

            jg = J["rg"]
            pe.wait_ge(unit_out, jg.unit_end(0, 0) - 2)
            for j in range(2):
                pe.wait_ge(lo_split, jg.panel_end(0, j))
                for q in range(8):
                    kt = 8 * j + q
                    if kt % 4 == 0:
                        mixed["rg"](kt // 4)
                    for ft in range(2):
                        at_ = q * T + ft * P
                        mm = triple(acc[jg.unit(0, 0) % 2][:, ft * T:(ft + 1) * T], 0,
                                    lambda wt: wt[:, jg.hl[j], at_:at_ + P], hH[:, kt, :], hL[:, kt, :], P,
                                    kt == 0, kt == KT - 1, ft == 0)
                mm.then_inc(panel_used, 1)
            pe.wait_ge(lo_split, jg.panel_end(0, 3))
            low_units(jg, 0, jg.hl[2:4], P)
            pe.drain().then_inc(panel_used, 2)
            products(J["rv"], h_in, mixed["rv"])
            for k, name in ((1, "rw"), (2, "ra")):
                job = J[name]
                pe.wait_ge(lo_split, job.panel_end(0, 0))
                pe.wait_ge(unit_out, job.unit_end(0, 0) - 2)
                for kt in range(KT):
                    if kt % 4 == 0:
                        mixed[name](kt // 4)
                    mm = triple(acc[job.unit(0, 0) % 2][0:LORA, 0:T], 0,
                                lambda wt: wt[:, job.hl[0], kt * LORA:(kt + 1) * LORA], hH[:, kt, :], hL[:, kt, :],
                                P, kt == 0, kt == KT - 1, True)
                mm.then_inc(panel_used, 1)
                pe.wait_ge(lo_split, job.panel_end(0, 1))
                low_units(job, k, job.hl[1:2], LORA)
                pe.drain().then_inc(panel_used, 1)
            products(J["rk"], h_in, mixed["rk"])

            def kk_sum(w):
                def step(i):
                    pe.wait_ge(M["ksq"], i * 2 + (w + 1))
                    for k in range(4):
                        mm = pe.matmul(aux[0][0:8, w * 512:w * 512 + T], C("ksum", 8 * k, 8 * k + 8),
                                       kq[:, k * T:(k + 1) * T], start=(k == 0), stop=(k == 3))
                    mm.then_inc(M["ksum"], 1)
                return step

            def kk_spread(w):
                def step(i):
                    pe.wait_ge(M["krec"], i * 2 + (w + 1))
                    if w:
                        pe.wait_ge(M["kk"], i * 2 + w)
                    for k in range(4):
                        mm = pe.matmul(aux[1][:, k * T:(k + 1) * T], C("kbc", k * P, (k + 1) * P, p=8),
                                       krs[:, w, :], start=True, stop=True)
                    mm.then_inc(M["kspread"], 1)
                return step

            products(J["rr"], h_in, mixed["rr"],
                     every={3: [kk_sum(0)], 4: [kk_sum(1)], 5: [kk_spread(0)], 6: [kk_spread(1)]})
            core_pe(pe)
            products(J["ro"], h_in, lambda p: pe.wait_ge(W["lo"], KT))
        if layers >= 4:
            ffn(1)
        pe.wait_ge(unit_out, final_job.unit_end(final_job.n - 1, 1))
        for g in range(8):
            if g >= 4:
                pe.wait_ge(out_ready, g - 3)
            for k in range(2):
                for tt in range(2):
                    mm = pe.transpose(bank(4 + g % 4)[:, (2 * k + tt) * P:(2 * k + tt + 1) * P],
                                      xT[:, 2 * g + k, tt * P:(tt + 1) * P], C("ident"))
            mm.then_inc(out_turned, 1)

    block_ctx.__exit__(None, None, None)


def constants():
    import numpy as np
    r, c = np.arange(P)[:, None], np.arange(P)[None, :]
    parts = {
        "ident": np.eye(P), "ones": np.ones((P, P)), "blk": r // RH == c // RH,
        "mb": np.hstack([-1.0 * (r < c), r <= c]), "mk": np.hstack([r < c, r <= c]),
        "mx1": 1.0 * (r == c) - ((r == c + 1) & (c % 2 == 0)), "mx1t": 1.0 * (r == c) - ((c == r + 1) & (r % 2 == 0)),
        "ksum": np.hstack([np.stack([r[:, 0] // RH + 2 * k == j for j in range(8)], 1) for k in range(4)]),
        "eps": np.array([[NORM_EPS, GN_EPS, 0, 0]] * P),
    }
    kbc = np.zeros((P, 4 * P))
    for k in range(4):
        for j in range(8):
            kbc[j, k * P:(k + 1) * P] = np.arange(P) // RH + 2 * k == j
    parts["kbc"] = kbc
    levels = []
    for level in range(1, LEVELS + 1):
        s = 1 << level
        cols = np.array([q for q in range(P) if q % (2 * s) < s])[None, :]
        one = 1.0 * (r == cols) - ((r // (2 * s) == cols // (2 * s)) & (r % (2 * s) >= s))
        levels += [one, one]
    parts["lv"] = np.hstack(levels)
    a = np.zeros((P, NCONST), np.float32)
    for name, (lo, hi) in CONST.items():
        a[:, lo:hi] = parts[name]
    half = HD // 8
    freq = np.float32(500000.0) ** (-np.arange(0, 2 * half, 2, dtype=np.float32) / np.float32(2 * half))
    ang = np.arange(T, dtype=np.float32)[None, :] * freq.astype(np.float32)[:, None]
    cos, sin = np.ones((P, T), np.float32), np.zeros((P, T), np.float32)
    cos[0:half], cos[half:2 * half] = np.cos(ang), np.cos(ang)
    sin[0:half], sin[half:2 * half] = -np.sin(ang), np.sin(ang)
    perm = np.zeros((P, P))
    for d in range(half):
        perm[d + half, d] = perm[d, d + half] = 1.0
    causal = np.where(c <= r, 0.0, -1e30)
    ssum, sbc = np.zeros((P, 16)), np.zeros((P, 4 * P))
    for k in range(4):
        ssum[:, 4 * k + k] = 1.0
        sbc[k, k * P:(k + 1) * P] = 1.0
    rope = {"perm": perm, "cos": cos, "sin": sin, "cmask": np.hstack([causal, np.zeros((P, P)), causal]),
            "ssum": ssum, "sbc": sbc}
    b = np.zeros((P, NROPE), np.float32)
    for name, (lo, hi) in ROPE.items():
        b[:, lo:hi] = rope[name]
    return a, b


_INS = ["x", "moba_norm", "moba_wqkv", "moba_q_gain", "moba_k_gain", "moba_wo",
        "rwkv_norm", "rwkv_mu", "rwkv_w_r", "rwkv_w_k", "rwkv_w_v", "rwkv_w_o",
        "rwkv_w0", "rwkv_w1", "rwkv_w2", "rwkv_a0", "rwkv_a1", "rwkv_a2", "rwkv_g1", "rwkv_g2",
        "rwkv_k_k", "rwkv_k_a", "rwkv_r_k", "rwkv_lnx_w", "rwkv_lnx_b",
        "ffn_norm", "ffn_w_up", "ffn_conv_w", "ffn_conv_b", "ffn_w_down"]
LAYERS = 4


def kernel(**inputs):
    import numpy as _np
    import concourse.bacc as _bacc
    from concourse import mybir as _mybir
    from concourse.bass_utils import run_bass_kernel_spmd as _run

    nc = _bacc.Bacc("TRN2", target_bir_lowering=False, num_devices=1)
    arrays, args = {}, []
    const_all, const_rope = constants()
    for name, a in [(n, inputs[n]) for n in _INS] + [("const_all", const_all), ("const_rope", const_rope)]:
        a = _np.ascontiguousarray(a)
        arrays[f"in_{name}_dram"] = a
        args.append(nc.dram_tensor(f"in_{name}_dram", a.shape, _mybir.dt.from_np(a.dtype), kind="ExternalInput").ap())
    args.append(nc.dram_tensor("out_0_dram", (1, T, D), _mybir.dt.float32, kind="ExternalOutput").ap())
    for name in ("x", "r", "v", "g"):
        args.append(nc.dram_tensor(f"{name}_spill", (P, KT, T), _mybir.dt.float32, kind="Internal").ap())
    hybrid_trunk(nc, *args, layers=LAYERS)
    r = _run(nc, [arrays], core_ids=[0])
    return r.results[0]["out_0_dram"]
```

```python
import concourse.bass as bass
from concourse import mybir

P = 128
T = 256
D = 2048
KT = D // P
FF = 5632
FKT = FF // P
NORM_EPS = 1e-6
GN_EPS = 64e-5
HD = 128
NH = D // HD
RH = 64
LORA = 96
UNIT = 512
RAW = 3
SPLIT = 2
PAN = 2048
HALF_A = 6
HALF_B = 5
LEVELS = 6
EXPM05 = 0.6065306597126334
SEED = 8
QT = 4 * T


def columns(*specs):
    at, got = 0, {}
    for name, w in specs:
        got[name] = (at, at + w)
        at += w
    return got, at


CONST, NCONST = columns(("ident", P), ("ones", P), ("blk", P), ("mb", 2 * P), ("mk", 2 * P), ("mx1", P), ("mx1t", P),
                        ("lv", P * LEVELS), ("ksum", 32), ("kbc", 4 * P), ("eps", 4))
ROPE, NROPE = columns(("perm", P), ("cos", T), ("sin", T), ("cmask", 384), ("ssum", 16), ("sbc", 4 * P))
PA, PB, PC, PCV = 0, 128, 240, 274
PRM_COLS = PCV + 8 * 88
G_MOBA, G_RWKV, MU = 0, 16, 32
W0, A0, K_K, K_A, R_K, LNW, LNB = (PB + 16 * i for i in range(7))
G_FFN, QG, KG = PC, PC + 32, PC + 33
OMKA = PRM_COLS
ROW_LOADS = 3 + 7 + 3 + 2 * 4


class Job:

    def __init__(self, name, n, units, accs):
        self.name, self.n, self.units, self.accs = name, n, units, accs
        self.m = sum(units)
        self.last_panel = [sum(units[:k + 1]) - 1 for k in range(len(units))]

    def unit(self, i, w):
        return self.first_unit + i * self.accs + w

    def panel_end(self, i, j):
        return self.first_panel + i * self.m + (j + 1)

    def unit_end(self, i, w):
        return self.first_unit + i * self.accs + (w + 1)

    def landed(self, i, j):
        s = self.raw[j]
        return i * (16 * self.uses[s]) + 16 * (self.landed0[s] + self.raw[:j + 1].count(s))


def gaps(job, idx, slots, last):
    got = []
    for j, s in enumerate(slots):
        earlier = [q for q in range(j) if slots[q] == s]
        if earlier:
            got.append(j - earlier[-1])
            continue
        back = [idx + j - last[s]]
        if job.n > 1:
            back.append(job.m - max(q for q in range(job.m) if slots[q] == s) + j)
        got.append(min(back))
    for s in set(slots):
        last[s] = idx + (job.n - 1) * job.m + max(q for q in range(job.m) if slots[q] == s)
    return got


def plan(jobs):
    idx, unit = SEED, 2
    landed = [0] * RAW
    last_raw, last_split = list(range(SEED - RAW, SEED)), list(range(SEED - SPLIT, SEED))
    for job in jobs:
        job.first_panel, job.first_unit = idx, unit
        job.raw = [j % RAW for j in range(job.m)]
        if job.raw[-1] == 0:
            job.raw[-1] = 1
        job.hl = [j % SPLIT for j in range(job.m)]
        job.landed0 = list(landed)
        job.uses = [job.raw.count(s) for s in range(RAW)]
        job.raw_gap = gaps(job, idx, job.raw, last_raw)
        job.hl_gap = gaps(job, idx, job.hl, last_split)
        for s in range(RAW):
            landed[s] += job.n * job.uses[s]
        idx += job.n * job.m
        unit += job.n * job.accs


def hybrid_trunk(nc, x, moba_norm, moba_wqkv, moba_q_gain, moba_k_gain, moba_wo,
                 rwkv_norm, rwkv_mu, rwkv_w_r, rwkv_w_k, rwkv_w_v, rwkv_w_o,
                 rwkv_w0, rwkv_w1, rwkv_w2, rwkv_a0, rwkv_a1, rwkv_a2, rwkv_g1, rwkv_g2,
                 rwkv_k_k, rwkv_k_a, rwkv_r_k, rwkv_lnx_w, rwkv_lnx_b,
                 ffn_norm, ffn_w_up, ffn_conv_w, ffn_conv_b, ffn_w_down, const_all, const_rope, out,
                 x_spill, r_spill, v_spill, g_spill):
    f32, f32r = mybir.dt.float32, mybir.dt.float32r
    ALU, ACT, AX = mybir.AluOpType, mybir.ActivationFunctionType, mybir.AxisListType

    J = {}
    stages = (("q", 2, [4, 4], 2), ("k", 2, [4, 4], 2), ("v", 2, [4, 4], 2), ("wo", 2, [4, 4], 2),
              ("up0a", HALF_A, [4, 4], 2), ("dn0a", 2, [6, 6], 2),
              ("up0b", HALF_B, [4, 4], 2), ("dn0b", 2, [5, 5], 2),
              ("rg", 1, [4], 5), ("rv", 2, [4, 4], 2), ("rw", 1, [2], 5), ("ra", 1, [2], 5),
              ("rk", 2, [4, 4], 2), ("rr", 2, [4, 4], 2), ("ro", 2, [4, 4], 2),
              ("up1a", HALF_A, [4, 4], 2), ("dn1a", 2, [6, 6], 2),
              ("up1b", HALF_B, [4, 4], 2), ("dn1b", 2, [5, 5], 2))
    for name, n, units, accs in stages:
        J[name] = Job(name, n, units, accs)
    order = list(J)
    plan([J[n] for n in order])
    final_job = J[order[-1]]

    def rows(w):
        return w.rearrange("(t p) n -> p t n", p=P)

    top = [(nc.sbuf_base + 31) // 32 * 32]
    limit = nc.sbuf_usable_end

    def place(at, *specs):
        fixed = at is None
        at = top[0] if fixed else at
        got = []
        for name, shape, dt in specs:
            size = 4
            for s in shape[1:]:
                size *= s
            assert at + size <= limit, (name, at + size - limit)
            got.append(nc.alloc_sbuf_tensor_at(name, shape, dt, offset=at))
            at += (size + 31) // 32 * 32
        if fixed:
            top[0] = at
        return got

    xT_at = top[0]
    (xT, hH, hL, raw, wh, wl, cst, prm, rstd, rt) = place(
        None, ("xT", [P, KT, T], f32), ("hH", [P, KT, T], f32r), ("hL", [P, KT, T], f32r),
        ("raw", [P, RAW, PAN], f32), ("wh", [P, SPLIT, PAN], f32r), ("wl", [P, SPLIT, PAN], f32r),
        ("cst", [P, NCONST], f32), ("prm", [P, PRM_COLS + 16], f32), ("rstd", [P, T], f32), ("mid", [P, 8], f32))
    mid = rt
    area = top[0]
    K16 = KT * T * 4
    xin, prow = place(area, ("xin", [P, 2, D], f32), ("prow", [P, 11, P], f32))
    norm_at = area + 3 * K16
    sq, sqacc, hf = place(norm_at, ("sq", [P, QT], f32), ("sqacc", [P, QT], f32), ("hf", [P, 2, QT], f32))
    rest_at = norm_at + 4 * QT * 4
    QKV, = place(area, ("QKV", [P, 3 * KT, T], f32))
    rot, nrmd, ssr, rsr, cr = place(rest_at, ("rot", [P, QT], f32), ("nrmd", [P, QT], f32), ("ssr", [4, 2, T], f32),
                                    ("rsr", [4, 2, T], f32), ("cr", [P, NROPE], f32))
    sq2, = place(norm_at + 2 * QT * 4, ("sq2", [P, 2, QT], f32))
    qs, vs, vt, sc, ex, pT, st = place(
        norm_at, ("qs", [P, 2, T], f32), ("vs", [P, 2, T], f32), ("vt", [P, 2, T], f32), ("sc", [P, 2, 384], f32),
        ("ex", [P, 2, 384], f32), ("pT", [P, 2, 384], f32), ("st", [P, 2, 8], f32))
    aH, aL = place(area, ("aH", [P, 4 * HALF_A, T], f32r), ("aL", [P, 4 * HALF_A, T], f32r))
    sg, fu, fc = place(rest_at, ("sg", [P, QT], f32), ("fu", [P, QT], f32), ("fc", [P, QT], f32))
    hb, xx, cw, kb, ab, ru, mt = place(
        area, ("hb", [P, KT, T], f32), ("xx", [P, KT, T], f32), ("cw", [P, KT, 2, 129], f32),
        ("kb", [P, KT, T], f32), ("ab", [P, KT, T], f32), ("ru", [P, QT], f32), ("mt", [P, QT], f32))
    xx_at = area + K16
    kb_at = xx_at + K16 + KT * 258 * 4
    ru_at = kb_at + 2 * K16
    tH, tL = place(kb_at, ("tH", [P, 2, T], f32r), ("tL", [P, 2, T], f32r))
    mt2, = place(kb_at + 4 * T * 4, ("mt2", [P, QT], f32))
    kkr, kq, kss, krs = place(xx_at, ("kkr", [P, 2, QT], f32), ("kq", [P, QT], f32),
                              ("kss", [8, 2, T], f32), ("krs", [8, 2, T], f32))
    kkb, = place(area, ("kkb", [P, KT, T], f32))
    slot1_at = xT_at + 3 * K16 + RAW * PAN * 4 + PAN * 4
    Qb, X, XT0 = place(xT_at, ("Qb", [P, LEVELS * 4, P], f32), ("Xb", [P, 2, 2, P], f32), ("XT0", [P, 2, 2, P], f32))
    mB0, mK0, tok0, tok1, vb0, vb1, bp0, bp1 = place(
        xx_at, ("mB0", [P, 2, 2, 2 * P], f32), ("mK0", [P, 2, 2, 2 * P], f32), ("tok0", [P, 4, P], f32),
        ("tok1", [P, 4, P], f32), ("vb0", [P, T], f32), ("vb1", [P, T], f32), ("bp0", [P, T], f32),
        ("bp1", [P, T], f32))
    ar0, gb, e1, zb, ub, s0, scl = place(
        ru_at, ("ar0", [P, 2, 2, 2, P], f32), ("gb", [P, T], f32), ("e1", [P, 2, 129], f32),
        ("zb", [P, 2, 2, RH], f32), ("ub", [P, 2, 2, RH], f32), ("s0", [P, RH], f32), ("scl", [P, 2], f32))
    hH_last, hL_last = xT_at + K16 + (KT - 2) * T * 4, xT_at + 2 * K16 + (KT - 2) * T * 4
    rb, bt = place(hH_last, ("rb", [P, T], f32), ("bt", [P, 2, P], f32))
    e2, kt_ = place(hL_last, ("e2", [P, 2, P], f32), ("ktl", [P, 2, P], f32))
    ar1, XT1, ys, y2 = place(slot1_at, ("ar1", [P, 2, 2, 2, P], f32), ("XT1", [P, 2, 2, P], f32),
                             ("ys", [P, T], f32), ("y2", [P, T], f32))
    mB1, mK1 = place(slot1_at + SPLIT * PAN * 4, ("mB1", [P, 2, 2, 2 * P], f32), ("mK1", [P, 2, 2, 2 * P], f32))
    y3 = rstd
    ars, mBs, mKs, toks, XTs, vbs, bps = (ar0, ar1), (mB0, mB1), (mK0, mK1), (tok0, tok1), (XT0, XT1), (vb0, vb1), \
        (bp0, bp1)
    xo, = place(area, ("xo", [P, 2, D], f32))

    acc = [nc.alloc_psum_tensor(f"acc{k}", [P, QT], f32) for k in range(2)]
    aux = [nc.alloc_psum_tensor(f"aux{k}", [P, QT], f32) for k in range(2)]

    def bank(k):
        return (acc + aux)[k // 2][:, (k % 2) * 512:(k % 2) * 512 + 512]

    def C(name, a=0, b=None, p=P):
        lo, hi = CONST[name]
        return cst[0:p, lo + a:hi if b is None else lo + b]

    def R(name, a=0, b=None, p=P):
        lo, hi = ROPE[name]
        return cr[0:p, lo + a:hi if b is None else lo + b]

    def quad(ap):
        return ap.rearrange("p (f t) -> p f t", f=4)

    def sem(name):
        return nc.alloc_semaphore(name)

    raw_landed = [sem(f"raw_landed{k}") for k in range(RAW)]
    hi_split, lo_split = sem("hi_split"), sem("lo_split")
    panel_used = sem("panel_used")
    unit_out = sem("unit_out")
    const_in, x_in, rows_in = sem("const_in"), sem("x_in"), sem("rows_in")
    turned, turned_out = sem("turned"), sem("turned_out")
    omka_done = sem("omka_done")

    class Names:

        def __init__(self, phase, *names):
            self.sems = {n: sem(f"{phase}_{n}") for n in names}

        def __getitem__(self, n):
            return self.sems[n]

    norm_names = ("squared", "summed", "total", "rooted", "rstd", "normed", "hi", "lo")
    N = {k: Names(k, *norm_names) for k in ("n0", "n1", "n2", "n3")}
    qk = Names("qk", "squared", "summed", "rooted", "inverse", "spread", "normed", "turned", "cosed", "sined", "roped")
    at = Names("at", "staged", "vturned", "vout", "scored", "masked", "maxed", "neg", "exped", "recip", "probs",
               "pturned", "pout", "mixed", "hi", "lo")
    f = Names("ffn", "init", "tap1", "tap0", "silu", "gated", "hi", "lo")
    M = Names("mix", "h", "xx", "mixed", "hi", "lo", "low_hi", "low_lo", "zeroed", "scan", "mid", "cw",
              "kkr", "ksq", "ksum", "kroot", "kmax", "krec", "kspread", "kk", "kfac", "kmod", "kb",
              "x_spilled", "r_spilled", "v_spilled", "g_spilled", "x_back", "low_unit")
    W = Names("core", "zeroed", "exps", "scaled", "bonusp", "turned", "tok", "gram", "gmask", "geye", "xt0",
              "lev0", "x0", "lp", "lq", "lt", "lxo", "lto", "zmm", "zout", "umm", "uout", "smm", "sout",
              "ymm", "yout", "mean", "cent", "csq", "var", "std", "rec", "norm", "aff", "bmm", "bon", "ysum", "gate",
              "hi", "lo")
    W.sems.update({n: sem(f"core_{n}") for n in ("r_in", "v_in", "g_in")})
    out_turned, out_ready, out_done = sem("out_turned"), sem("out_ready"), sem("out_done")

    block_ctx = nc.Block()
    block = block_ctx.__enter__()

    def run(eng, job, split, first=None, every=None, late=None, last=None):
        first, every, late, last = first or {}, every or {}, late or {}, last or {}

        def body(i, is_first, is_last):
            for j in range(job.m):
                if j + 1 < job.m or not (job is final_job and is_last):
                    split(eng, job, i, j + 1)
                if is_first:
                    for f in first.get(j, ()):
                        f()
                else:
                    for f in late.get(j, ()):
                        f(i - 1)
                for f in every.get(j, ()):
                    f(i)
                if is_last:
                    for f in last.get(j, ()):
                        f()

        body(0, True, job.n == 1)
        if job.n == 2:
            body(1, False, True)
        elif job.n > 2:
            with eng.Fori(1, job.n) as i:
                body(i, False, False)

    def next_place(job, i, j):
        if j < job.m:
            return job, i, j
        return job, i + 1, 0

    def mix_used(J):
        used = {"rg": [J["rg"].first_panel] * 4}
        jg = J["rg"]
        used["rv"] = [jg.panel_end(0, g // 2) for g in range(4)]
        for name, before in (("rw", "rv"), ("rr", "rk")):
            used[name] = [J[before].panel_end(1, 4 + g) for g in range(4)]
        for name, before in (("ra", "rw"), ("rk", "ra")):
            used[name] = [J[before].panel_end(0, 0)] * 4
        return used

    def mix_buffer(name, g):
        return mt2[:, :] if g % 2 and name not in ("rk", "rr") else mt[:, :]

    def flat(t, per):
        dims = len(t.shape) - 1
        v = {2: lambda: t[:, :, :].rearrange("p a b -> p (a b)"),
             3: lambda: t[:, :, :, :].rearrange("p a b c -> p (a b c)")}[dims]()
        return lambda p, a=0, n=per, rows=slice(0, P): v[rows, bass.ds(p * per + a, n)]

    cwp, kbp, abp, kkp = flat(cw, 258), flat(kb, T), flat(ab, T), flat(kkb, T)

    def spread(ap, n):
        return ap.unsqueeze(1).to_broadcast([ap.shape[0], n, ap.shape[1]])

    def blocks(ap, s, half):
        return ap.rearrange("p h (b u s) -> p (h b) u s", u=2, s=s)[:, :, half, :]

    def compact(ap, s):
        return ap.rearrange("p (b s) -> p b s", s=s)

    heads = [(h, slice(h * RH, (h + 1) * RH)) for h in range(2)]

    def Ql(level, c):
        at_ = 4 * (level - 1) + 2 * c
        return Qb[:, at_:at_ + 2, :]

    def attention(body, eng):
        last = NH // 2 - 1
        body(None, 0)
        body(0, 1)
        with eng.Fori(1, last) as i:
            body(i, i + 1)
        body(last, None)

    def core(body, eng):
        body(None, None, (0, 0))
        body(None, (0, 0), (1, 1))
        body((0, 0), (1, 1), (2, 0))
        body((1, 1), (2, 0), (3, 1))
        with eng.Fori(1, KT // 2 - 1) as i:
            body((i * 2, 0), (i * 2 + 1, 1), (i * 2 + 2, 0))
            body((i * 2 + 1, 1), (i * 2 + 2, 0), (i * 2 + 3, 1))
        body((KT - 2, 0), (KT - 1, 1), None)
        body((KT - 1, 1), None, None)

    def has(p, n):
        return not isinstance(p, int) or p >= n

    def pairs_before(p, n, count):
        return p * count + (1 - n) * count

    def core_loads(sp):
        def tile(src, at_):
            return src.rearrange("p k t -> p (k t)")[:, bass.ds(at_, T)]

        def load(p, k):
            if has(p, 1):
                sp.wait_ge(W["scaled"], p * 6)
            sp.dma_start(rb[:, :], tile(r_spill, p * T)).then_inc(W["r_in"], 16)
            if has(p, 2):
                sp.wait_ge(W["bon"], pairs_before(p, 2, 1))
            elif has(p, 1):
                sp.wait_ge(W["turned"], p)
            sp.dma_start(vbs[k][:, :], tile(v_spill, p * T)).then_inc(W["v_in"], 16)

        def load_gate(p):
            if has(p, 1):
                sp.wait_ge(W["gate"], p)
            sp.dma_start(gb[:, :], tile(g_spill, p * T)).then_inc(W["g_in"], 16)

        for done in ("g_spilled", "v_spilled", "r_spilled"):
            sp.wait_ge(M[done], 64)
        sp.wait_ge(M["kb"], 4)
        load(0, 0)
        load(1, 1)
        load_gate(0)
        with sp.Fori(1, KT // 2) as i:
            load(i * 2, 0)
            load_gate(i * 2 - 1)
            load(i * 2 + 1, 1)
            load_gate(i * 2)
        load_gate(KT - 1)

    def core_pe(pe):
        def body(b, f, _):
            def turn():
                p, k = f
                pe.wait_ge(W["v_in"], p * 16 + 16)
                pe.wait_ge(W["scaled"], p * 6 + 6)
                if has(p, 1):
                    pe.wait_ge(W["tok"], p)
                for n, src in enumerate((vbs[k][:, 0:P], vbs[k][:, P:T], bt[:, 0, :], kt_[:, 0, :])):
                    mm = pe.transpose(bank(4)[:, n * P:(n + 1) * P], src, C("ident"))
                mm.then_inc(W["turned"], 1)

            def gram(c):
                p, k = f
                if has(p, 1):
                    pe.wait_ge(W["lto"], pairs_before(p, 1, 12))
                    pe.wait_ge(W["lq"], pairs_before(p, 1, 12))
                for h, r in heads:
                    rhs = ars[k][:, h, c, :, :].rearrange("p a t -> p (a t)")
                    pe.matmul(bank(c)[:, h * T:(h + 1) * T], bt[:, c, :], rhs, start=True, stop=True)
                    mm = pe.matmul(bank(2 + c)[:, h * T:(h + 1) * T], kt_[:, c, :], rhs, start=True, stop=True)
                mm.then_inc(W["gram"], 1)

            def lev0(c):
                p, k = f
                pe.wait_ge(W["geye"], p * 2 + (c + 1))
                for h, r in heads:
                    mm = pe.matmul(bank(c)[:, h * P:(h + 1) * P], mBs[k][:, c, h, 0:P], C("ident"),
                                   start=True, stop=True)
                mm.then_inc(W["lev0"], 1)

            def level_g(level):
                p, k = f
                for c in range(2):
                    if level == 1:
                        pe.wait_ge(W["x0"], p * 2 + (c + 1))
                    else:
                        pe.wait_ge(W["lxo"], p * 10 + (2 * (level - 2) + c + 1))
                    for h, r in heads:
                        low = blocks(X[:, c, h:h + 1, :], 1 << level, 0)
                        mm = pe.matmul(bank(c)[:, h * RH:(h + 1) * RH], mBs[k][:, c, h, 0:P], low,
                                       start=True, stop=True)
                    mm.then_inc(W["lp"], 1)

            def level_x(level):
                p, k = f
                s = 1 << level
                for c in range(2):
                    pe.wait_ge(W["lq"], p * 12 + (2 * (level - 1) + c + 1))
                    if level == 1:
                        pe.wait_ge(W["xt0"], p * 2 + (c + 1))
                        pe.wait_ge(W["gmask"], p * 4 + (c + 3))
                    else:
                        pe.wait_ge(W["lto"], p * 12 + (2 * (level - 2) + c + 1))
                    q = Ql(level, c)
                    if level < LEVELS:
                        for h, r in heads:
                            mm = pe.matmul(bank(2 + c)[:, h * RH:(h + 1) * RH], XTs[k][:, c, h, :],
                                           blocks(q[:, h:h + 1, :], s, 0), start=True, stop=True)
                    for h, r in heads:
                        mm = pe.matmul(bank(2 + c)[:, P + h * RH:P + (h + 1) * RH], q[:, h, :],
                                       blocks(XTs[k][:, c, h:h + 1, :], s, 1), start=True, stop=True)
                    mm.then_inc(W["lt"], 1)

            def z(c):
                p, k = b
                if c:
                    pe.wait_ge(W["sout"], p + 1)
                else:
                    pe.wait_ge(W["lto"], p * 12 + 12)
                    pe.wait_ge(W["gmask"], p * 4 + 4)
                    pe.wait_ge(W["tok"], p + 1)
                    if has(p, 1):
                        pe.wait_ge(W["cent"], p)
                for h, r in heads:
                    z_ = bank(5)[:, h * RH:(h + 1) * RH]
                    mm = pe.matmul(z_, mKs[k][:, c, h, 0:P], toks[k][:, c, r], start=True, stop=(c == 0))
                    if c:
                        mm = pe.matmul(z_, ars[k][:, h, 1, 0, :], s0[:, :], start=False, stop=True)
                mm.then_inc(W["zmm"], 1)

            def u(c):
                p, k = b
                pe.wait_ge(W["zout"], p * 2 + (c + 1))
                for h, r in heads:
                    mm = pe.matmul(bank(5)[:, P + h * RH:P + (h + 1) * RH], XTs[k][:, c, h, :], zb[:, c, h, :],
                                   start=True, stop=True)
                mm.then_inc(W["umm"], 1)

            def state():
                p, k = b
                pe.wait_ge(W["uout"], p * 2 + 1)
                if has(p, 1):
                    pe.wait_ge(W["bon"], p)
                for h, r in heads:
                    pe.matmul(bank(6)[r, 0:RH], toks[k][:, 2, r], ub[:, 0, h, :], start=True, stop=False)
                    mm = pe.matmul(bank(6)[r, 0:RH], toks[k][:, 3, r], toks[k][:, 0, r], start=False, stop=True)
                mm.then_inc(W["smm"], 1)

            def outputs():
                p, k = b
                pe.wait_ge(W["uout"], p * 2 + 2)
                if has(p, 1):
                    pe.wait_ge(W["std"], p)
                for c in range(2):
                    for h, r in heads:
                        y = bank(7)[r, c * P:(c + 1) * P]
                        pe.matmul(y, ub[:, c, h, :], mBs[k][:, c, h, P:2 * P], start=True, stop=False)
                        mm = pe.matmul(y, toks[k][:, c, r], mKs[k][:, c, h, P:2 * P], start=False, stop=(c == 0))
                        if c:
                            mm = pe.matmul(y, s0[:, :], ars[k][:, h, 1, 1, :], start=False, stop=True)
                mm.then_inc(W["ymm"], 1)

            def head_sum(at_, src, done):
                pe.matmul(at_[:, 0:T], C("blk"), src[:, :], start=True, stop=True).then_inc(W[done], 1)

            if f:
                turn()
            if b:
                z(0)
            if f:
                gram(0)
                gram(1)
            if b:
                u(0)
                state()
            if f:
                lev0(0)
                lev0(1)
            if b:
                z(1)
            if f:
                level_g(1)
            if b:
                u(1)
            if f:
                level_x(1)
                level_g(2)
            if b:
                outputs()
            if f:
                level_x(2)
            if b:
                pe.wait_ge(W["bonusp"], b[0] * 2 + 2)
                head_sum(bank(6), bps[b[1]], "bmm")
                pe.wait_ge(W["yout"], b[0] + 1)
                head_sum(bank(5), ys, "mean")
            if f:
                level_g(3)
                level_x(3)
            if b:
                pe.wait_ge(W["csq"], b[0] + 1)
                head_sum(bank(7), ys, "var")
            if f:
                for level in range(4, LEVELS + 1):
                    level_g(level)
                    level_x(level)

        core(body, pe)

    def core_act(act):
        act.wait_ge(M["cw"], 2 * KT)
        act.wait_ge(M["kb"], 4)
        act.wait_ge(M["r_spilled"], 64)

        def gain(p):
            act.wait_ge(W["norm"], p + 1)
            act.activation(y2[:, :], y2[:, :], ACT.Identity, bias=prm[:, bass.ds(p + LNB, 1)],
                           scale=prm[:, bass.ds(p + LNW, 1)]).then_inc(W["aff"], 1)

        def core_hi(p):
            act.wait_ge(W["gate"], p + 1)
            act.copy(hH[:, bass.ds(p, 1), :], y2[:, :].unsqueeze(1)).then_inc(W["hi"], 1)

        def body(b, f, n):
            def level(lev):
                p, k = f
                for c in range(2):
                    act.wait_ge(W["lt"], p * 12 + (2 * (lev - 1) + c + 1))
                    if lev < LEVELS:
                        act.copy(blocks(X[:, c], 1 << lev, 0), compact(bank(2 + c)[:, 0:P], 1 << lev))\
                           .then_inc(W["lxo"], 1)
                    act.copy(blocks(XTs[k][:, c], 1 << lev, 1), compact(bank(2 + c)[:, P:2 * P], 1 << lev))\
                       .then_inc(W["lto"], 1)

            def zout(c):
                act.wait_ge(W["zmm"], b[0] * 2 + (c + 1))
                act.copy(zb[:, c].rearrange("p h v -> p (h v)"), bank(5)[:, 0:P]).then_inc(W["zout"], 1)

            def uout(c):
                act.wait_ge(W["umm"], b[0] * 2 + (c + 1))
                act.copy(ub[:, c].rearrange("p h v -> p (h v)"), bank(5)[:, P:2 * P]).then_inc(W["uout"], 1)

            if f:
                p, k = f
                act.wait_ge(W["turned"], p + 1)
                act.copy(toks[k][:, :, :].rearrange("p a n -> p (a n)"), bank(4)).then_inc(W["tok"], 1)
            if b:
                zout(0)
                if has(b[0], 1):
                    gain(b[0] - 1)
                uout(0)
                zout(1)
                uout(1)
            if f:
                level(1)
            if b:
                act.wait_ge(W["ymm"], b[0] + 1)
                act.copy(ys[:, :], bank(7)[:, 0:T]).then_inc(W["yout"], 1)
            if f:
                level(2)
            if b:
                if has(b[0], 1):
                    core_hi(b[0] - 1)
                act.wait_ge(W["cent"], b[0] + 1)
                act.activation(ys[:, :], y2[:, :], ACT.Square).then_inc(W["csq"], 1)
            if n:
                p, k = n
                if has(p, 1):
                    act.wait_ge(W["scaled"], p * 6)
                act.activation(e1[:, :, :].rearrange("p c t -> p (c t)"), cwp(p), ACT.Exp).then_inc(W["exps"], 1)
                act.activation(e2[:, :, :], cwp(p).rearrange("p (c t) -> p c t", c=2)[:, :, 1:129], ACT.Exp,
                               scale=-1.0).then_inc(W["exps"], 1)
                act.activation(scl[:, k:k + 1], cwp(p, 129, 1), ACT.Exp, bias=cwp(p, 128, 1), scale=-1.0)\
                   .then_inc(W["exps"], 1)
            if f:
                level(3)
            if b:
                act.wait_ge(W["var"], b[0] + 1)
                if has(b[0], 1):
                    act.wait_ge(W["norm"], b[0])
                act.activation(y3[:, :], bank(7)[:, 0:T], ACT.Sqrt, bias=C("eps", 1, 2), scale=1.0 / RH)\
                   .then_inc(W["std"], 1)
            if f:
                level(4)
            if f:
                level(5)
            if f:
                level(6)

        core(body, act)
        gain(KT - 1)
        core_hi(KT - 1)
        act.wait_ge(W["lo"], KT)

    @block.sync
    def _(sp):
        def load(job, src, ahead=0, between=None):
            def body(i, panels=range(job.m)):
                base = src(i)
                for j in panels:
                    sp.wait_ge(lo_split, job.panel_end(i, j) - job.raw_gap[j])
                    view = base(j)
                    a, b = view.shape[1], view.shape[2]
                    dst = raw[0:view.shape[0], job.raw[j], 0:a * b].rearrange("p (a b) -> p a b", a=a)
                    sp.dma_start(dst, view).then_inc(raw_landed[job.raw[j]], 16)
            if between:
                body(0, range(ahead))
                between()
                body(0, range(ahead, job.m))
                for i in range(1, job.n):
                    body(i)
            elif job.n == 1:
                body(0)
            else:
                with sp.Fori(0, job.n) as i:
                    body(i)

        def plain(w, k0=0, c0=0, per=4):
            def src(i):
                col = i * (2 * UNIT) if isinstance(i, int) else sp.snap(i * (2 * UNIT))

                def view(j):
                    u, p = divmod(j, per)
                    cut = w[:, k0 + 4 * p:k0 + 4 * p + 4, c0 + u * UNIT:]
                    return cut[:, :, bass.ds(col, UNIT)]
                return view
            return src

        def gate_up(w, g0):
            def src(i):
                col = sp.snap(i * UNIT)

                def view(j):
                    u, p = divmod(j, 4)
                    cut = w[:, 4 * p:4 * p + 4, u * FF + g0 * UNIT:]
                    return cut[:, :, bass.ds(col, UNIT)]
                return view
            return src

        def fixed(*views):
            return lambda i: lambda j: views[j]

        sp.dma_start(cst[:, 0:P], const_all[:, 0:P]).then_inc(const_in, 16)
        for tt in range(2):
            sp.dma_start(xin[:, tt, :], x[0, tt * P:(tt + 1) * P, :]).then_inc(x_in, 16)
        wqkv = rows(moba_wqkv[0])
        load(J["q"], plain(wqkv))
        load(J["k"], plain(wqkv, c0=D))
        load(J["v"], plain(wqkv, c0=2 * D))
        load(J["wo"], plain(rows(moba_wo[0])))

        def ffn(layer):
            up, down = rows(ffn_w_up[layer]), rows(ffn_w_down[layer])
            load(J[f"up{layer}a"], gate_up(up, 0))
            load(J[f"dn{layer}a"], plain(down, k0=0, per=HALF_A))
            load(J[f"up{layer}b"], gate_up(up, HALF_A))
            load(J[f"dn{layer}b"], plain(down, k0=4 * HALF_A, per=HALF_B))

        ffn(0)
        g1 = rows(rwkv_g1[0])
        g2 = rwkv_g2[0].rearrange("(a p) n -> a p n", p=P)
        load(J["rg"], fixed(g1[:, 0:8, :], g1[:, 8:16, :], g2[0:1].rearrange("a p n -> p a n"),
                            g2[1:2].rearrange("a p n -> p a n")))
        load(J["rv"], plain(rows(rwkv_w_v[0])))
        load(J["rw"], fixed(rows(rwkv_w1[0]), rwkv_w2.rearrange("a p n -> p a n")))
        load(J["ra"], fixed(rows(rwkv_a1[0]), rwkv_a2.rearrange("a p n -> p a n")))
        load(J["rk"], plain(rows(rwkv_w_k[0])))
        load(J["rr"], plain(rows(rwkv_w_r[0])))
        load(J["ro"], plain(rows(rwkv_w_o[0])), ahead=RAW, between=lambda: core_loads(sp))
        ffn(1)
        for tt in range(2):
            sp.wait_ge(out_ready, 8)
            sp.dma_start(out[0, tt * P:(tt + 1) * P, :], xo[:, tt, :]).then_inc(out_done, 16)
        sp.wait_ge(out_done, 32)

    @block.scalar
    def _(act):
        def split(eng, job, i, j):
            job, i, j = next_place(job, i, j)
            act.wait_ge(raw_landed[job.raw[j]], job.landed(i, j))
            act.wait_ge(panel_used, job.panel_end(i, j) - job.hl_gap[j])
            act.copy(wh[:, job.hl[j], :], raw[:, job.raw[j], :]).then_inc(hi_split, 1)

        for g in range(8):
            if g == 4:
                split(act, J["q"], 0, 0)
            act.wait_ge(turned, g + 1)
            act.copy(xT[:, 2 * g:2 * g + 2, :], bank(4 + g % 4)).then_inc(turned_out, 1)
            if g % 2:
                act.wait_ge(turned_out, g + 1)
                q = g // 2
                if q >= 2:
                    act.wait_ge(N["n0"]["summed"], q - 1)
                act.activation(quad((sqacc if q == 0 else sq)[:, :]), xT[:, 4 * q:4 * q + 4, :],
                               ACT.Square).then_inc(N["n0"]["squared"], 1)
        for g, tiles in enumerate(((0, 1, 2), (3, 4, 5, 6), (7, 8, 9, 10))):
            act.wait_ge(turned, 9 + g)
            cols = {0: (0, 240 + 34), 1: (PCV, 4 * 88), 2: (PCV + 4 * 88, 4 * 88)}[g]
            act.copy(prm[:, cols[0]:cols[0] + cols[1]], bank(4 + g)[:, 0:cols[1]]).then_inc(turned_out, 1)

        def norm_root(n):
            act.wait_ge(N[n]["total"], 1)
            act.activation(rstd[:, :], aux[1][:, 512:512 + T], ACT.Sqrt, bias=C("eps", 0, 1), scale=1.0 / D)\
               .then_inc(N[n]["rooted"], 1)

        def norm_hi(n, g, before):
            act.wait_ge(N[n]["normed"], 4 * (g + 1))
            act.wait_ge(panel_used, before)
            act.copy(hH[:, 4 * g:4 * g + 4, :], quad(hf[:, g % 2, :])).then_inc(N[n]["hi"], 1)

        norm_root("n0")
        norm_hi("n0", 0, SEED)

        def take_qkv(job, part, w):
            def step(i):
                act.wait_ge(panel_used, job.panel_end(i, 4 * w + 3))
                act.copy(QKV[:, bass.ds(part * KT + i * 8 + 4 * w, 4), :], quad(acc[job.unit(0, w) % 2][:, :]))\
                   .then_inc(unit_out, 1)
            return step

        def qk_square(which, w):
            def step(i):
                n = 4 * which + 2 * i + w
                act.wait_ge(unit_out, J["qk"[which]].unit_end(i, w))
                if n >= 2:
                    act.wait_ge(qk["summed"], n - 1)
                act.activation(quad(sq2[:, w, :]), QKV[:, bass.ds(which * KT + i * 8 + 4 * w, 4), :],
                               ACT.Square).then_inc(qk["squared"], 1)
            return step

        def qk_root(which, w):
            def step(i):
                n = 4 * which + 2 * i + w
                act.wait_ge(qk["summed"], n + 1)
                if n >= 2:
                    act.wait_ge(qk["inverse"], n - 1)
                act.activation(ssr[:, w, :], aux[0][0:4, w * 512:w * 512 + T], ACT.Sqrt,
                               bias=C("eps", 0, 1, p=4), scale=1.0 / HD).then_inc(qk["rooted"], 1)
            return step

        jq, jk, jv, jo = (J[k] for k in ("q", "k", "v", "wo"))
        run(act, jq, split, first={0: [lambda: norm_hi("n0", 1, SEED)], 1: [lambda: norm_hi("n0", 2, SEED)],
                                   2: [lambda: norm_hi("n0", 3, SEED)]},
            every={3: [take_qkv(jq, 0, 0)], 7: [take_qkv(jq, 0, 1)]})
        for which, job in ((0, jk), (1, jv)):
            run(act, job, split, every={0: [qk_square(which, 0)], 1: [qk_root(which, 0), qk_square(which, 1)],
                                        2: [qk_root(which, 1)], 3: [take_qkv(job, 1 + which, 0)],
                                        7: [take_qkv(job, 1 + which, 1)]})
        act.wait_ge(qk["roped"], 9)
        act.wait_ge(unit_out, jv.unit_end(1, 1))
        def body(i, n):
            for b in range(2):
                if i is None:
                    break
                for t, (a, e) in enumerate(((0, P), (P, 3 * P))):
                    act.wait_ge(at["neg"], 2 * i + (b + 1))
                    act.activation(ex[:, b, a:e], sc[:, b, a:e], ACT.Exp, bias=st[:, b, 2 + t:3 + t],
                                   scale=HD ** -0.5, accum_out=st[:, b, 4 + t:5 + t]).then_inc(at["exped"], 1)
            for b in range(2):
                if n is None:
                    break
                if i is not None:
                    act.wait_ge(at["scored"], 2 * i + (b + 1))
                act.copy(qs[:, b, :], QKV[:, bass.ds(2 * n + b, 1), :]).then_inc(at["staged"], 1)
            for b in range(2):
                if i is not None:
                    act.wait_ge(at["pturned"], 2 * i + (b + 1))
                    act.copy(pT[:, b, :], aux[b][:, 512:512 + 384]).then_inc(at["pout"], 1)
            for b in range(2):
                if n is None:
                    break
                if i is not None:
                    act.wait_ge(at["vturned"], 2 * i + (b + 1))
                act.copy(vs[:, b, :], QKV[:, bass.ds(2 * KT + 2 * n + b, 1), :]).then_inc(at["staged"], 1)
            for b in range(2):
                if i is not None:
                    act.wait_ge(at["mixed"], 2 * i + (b + 1))
                    act.copy(hH[:, bass.ds(2 * i + b, 1), :], acc[b][:, 0:T]).then_inc(at["hi"], 1)
            for b in range(2):
                if n is not None:
                    act.wait_ge(at["vturned"], 2 * n + (b + 1))
                    act.copy(vt[:, b, :], aux[b][:, 512:512 + T]).then_inc(at["vout"], 1)

        attention(body, act)

        def square(n, job, u):
            i, w = divmod(u, 2)

            def step(*_):
                act.wait_ge(unit_out, job.unit_end(i, w))
                if u >= 2:
                    act.wait_ge(N[n]["summed"], u - 1)
                act.activation(quad((sqacc if u == 0 else sq)[:, :]), xT[:, 4 * u:4 * u + 4, :],
                               ACT.Square).then_inc(N[n]["squared"], 1)
            return step

        def residual(n, job, first=None):
            a, b = job.units[0], job.m
            steps = dict(first or {})
            if n is None:
                run(act, job, split, first=steps)
                return
            steps.setdefault(a, []).append(square(n, job, 0))
            run(act, job, split, first=steps,
                late={0: [square(n, job, 1)]}, last={a: [square(n, job, 2)]})
            square(n, job, 3)()

        def ffn(layer):
            n = ("n1", "n3")[layer]
            ja, da, jb, db = (J[f"{k}{layer}{h}"] for k, h in (("up", "a"), ("dn", "a"), ("up", "b"), ("dn", "b")))
            norm_root(n)
            done = ja.first_panel
            norm_hi(n, 0, done)

            def steps(job, g0):
                u0 = layer * (HALF_A + HALF_B) + g0
                cw0 = PCV + layer * 4 * 88

                def take(w):
                    def step(i):
                        act.wait_ge(panel_used, job.panel_end(i, 4 * w + 3))
                        if not (u0 == 0 and w == 0 and isinstance(i, int)):
                            act.wait_ge(f["tap0"], (2 * (i + u0) + w) * 4)
                        act.copy(fu[:, :], acc[job.unit(0, w) % 2][:, :]).then_inc(unit_out, 1)
                    return step

                def init(w):
                    def step(i):
                        act.wait_ge(unit_out, job.unit_end(i, w))
                        if w:
                            act.wait_ge(f["silu"], i + u0 + 1)
                        elif not (u0 == 0 and isinstance(i, int)):
                            act.wait_ge(f["lo"], i + u0)
                        for k in range(4):
                            c = i * 4 + (g0 * 4 + w * FKT + k)
                            act.activation(fc[:, k * T:(k + 1) * T], fu[:, k * T:(k + 1) * T], ACT.Identity,
                                           bias=prm[:, bass.ds(c + (cw0 + 3 * 88), 1)],
                                           scale=prm[:, bass.ds(c + (cw0 + 2 * 88), 1)]).then_inc(f["init"], 1)
                    return step

                def silu(i):
                    act.wait_ge(f["tap0"], (2 * (i + u0)) * 4 + 4)
                    if not (u0 == 0 and isinstance(i, int)):
                        act.wait_ge(f["gated"], i + u0)
                    act.activation(sg[:, :], fc[:, :], ACT.Silu).then_inc(f["silu"], 1)

                def hi(i):
                    act.wait_ge(f["gated"], i + (u0 + 1))
                    act.copy(aH[:, bass.ds(i * 4, 4), :], quad(fc[:, :])).then_inc(f["hi"], 1)

                return ({3: [take(0)], 4: [init(0)], 5: [silu], 7: [take(1)]}, {0: [init(1)], 2: [hi]})

            for job, dn, g0 in ((ja, da, 0), (jb, db, HALF_A)):
                every, late = steps(job, g0)
                first = {}
                if g0 == 0:
                    first = {k: [lambda k=k: norm_hi(n, k + 1, done)] for k in range(3)}
                run(act, job, split, first=first, every=every, late=late)
                tail = {j: [lambda g=g, job=job: g(job.n - 1) for g in fs] for j, fs in late.items()}
                residual("n2" if layer == 0 and g0 else None, dn, first=tail)

        residual("n1", jo)
        ffn(0)

        norm_root("n2")
        mixes = {"rg": 5, "rv": 3, "rw": 1, "ra": 4, "rk": 2, "rr": 0}
        order_mix = list(mixes)

        def mix_hi(name, g, used):
            n = 4 * order_mix.index(name) + g

            def step(*_):
                act.wait_ge(M["mixed"], 4 * n + 4)
                act.wait_ge(panel_used, used)
                act.copy(hH[:, 4 * g:4 * g + 4, :], quad(mix_buffer(name, g))).then_inc(M["hi"], 1)
            return step

        used = mix_used(J)
        for g in range(4):
            mix_hi("rg", g, used["rg"][g])()
        jg = J["rg"]
        split(act, jg, 0, 1)
        split(act, jg, 0, 2)

        def low_rank(job, panels, parts, width, func):
            k = ("rg", "rw", "ra").index(job.name)
            act.wait_ge(panel_used, job.panel_end(0, panels - 1))
            if k == 1:
                act.wait_ge(M["v_spilled"], 64)
            if k:
                act.wait_ge(M["low_lo"], k)
            act.activation(ru[0:parts, 0:width], acc[job.unit(0, 0) % 2][0:parts, 0:width], func)\
               .then_inc(unit_out, 1)
            act.wait_ge(unit_out, job.unit_end(0, 0))
            act.copy(tH[0:parts, 0:width // T, :], ru[0:parts, 0:width].rearrange("p (f t) -> p f t", t=T))\
               .then_inc(M["low_hi"], 1)

        low_rank(jg, 2, P, 2 * T, ACT.Sigmoid)
        split(act, jg, 0, 3)
        for u in range(4):
            if u == 3:
                split(act, jg, 0, 4)
            act.wait_ge(M["low_unit"], u + 1)
            act.wait_ge(M["low_lo"], 1)
            act.copy(ab[:, 4 * u:4 * u + 4, :], quad(acc[jg.unit(0, 1 + u) % 2][:, :])).then_inc(unit_out, 1)

        def take_spill(job, done, before, w):
            def step(i):
                u = 2 * i + w
                act.wait_ge(panel_used, job.panel_end(i, 4 * w + 3))
                if u:
                    act.wait_ge(M[done], 16 * u)
                else:
                    act.wait_ge(before[0], before[1])
                act.copy(ru[:, :], acc[job.unit(0, w) % 2][:, :]).then_inc(unit_out, 1)
            return step

        mix_hi("rv", 0, used["rv"][0])()
        run(act, J["rv"], split, first={k: [mix_hi("rv", k + 1, used["rv"][k + 1])] for k in range(3)},
            every={3: [take_spill(J["rv"], "v_spilled", (M["g_spilled"], 64), 0)],
                   7: [take_spill(J["rv"], "v_spilled", None, 1)]})
        for name, func, bias in (("rw", ACT.Tanh, W0), ("ra", ACT.Copy, A0)):
            job = J[name]
            for g in range(4):
                mix_hi(name, g, used[name][g])()
            split(act, job, 0, 1)
            low_rank(job, 1, LORA, T, func)
            for u in range(4):
                if u == 3:
                    split(act, job, 0, 2)
                act.wait_ge(M["low_unit"], 4 + (4 if name == "ra" else 0) + u + 1)
                for k in range(4):
                    ft = 4 * u + k
                    src = acc[job.unit(0, 1 + u) % 2][:, k * T:(k + 1) * T]
                    dst = ab[:, ft, :]
                    if name == "rw":
                        src, dst = src.rearrange("p (c t) -> p c t", c=2), cw[:, ft, :, 1:129]
                    ins = act.activation(dst, src, ACT.Sigmoid, bias=prm[:, bias + ft:bias + ft + 1])
                ins.then_inc(unit_out, 1)

        def take_k(w):
            def step(i):
                job = J["rk"]
                act.wait_ge(panel_used, job.panel_end(i, 4 * w + 3))
                act.copy(kb[:, 8 * i + 4 * w:8 * i + 4 * w + 4, :], quad(acc[job.unit(0, w) % 2][:, :]))\
                   .then_inc(unit_out, 1)
            return step

        mix_hi("rk", 0, used["rk"][0])()
        run(act, J["rk"], split, first={k: [mix_hi("rk", k + 1, used["rk"][k + 1])] for k in range(3)},
            every={3: [take_k(0)], 7: [take_k(1)]})
        mix_hi("rr", 0, used["rr"][0])()

        def kk_square(w):
            def step(i):
                u = 2 * i + w
                act.wait_ge(unit_out, J["rk"].unit_end(i, w))
                act.wait_ge(M["lo"], 24)
                if u >= 2:
                    act.wait_ge(M["kk"], u - 1)
                for k in range(4):
                    ft = 4 * u + k
                    act.activation(kkr[:, w, k * T:(k + 1) * T], kb[:, ft, :], ACT.Copy,
                                   scale=prm[:, K_K + ft:K_K + ft + 1]).then_inc(M["kkr"], 1)
                if u:
                    act.wait_ge(M["ksum"], u)
                act.wait_ge(M["kkr"], 4 * u + 4)
                act.activation(kq[:, :], kkr[:, w, :], ACT.Square).then_inc(M["ksq"], 1)
            return step

        def kk_root(w):
            def step(i):
                u = 2 * i + w
                act.wait_ge(M["ksum"], u + 1)
                if u >= 2:
                    act.wait_ge(M["krec"], u - 1)
                act.activation(kss[:, w, :], aux[0][0:8, w * 512:w * 512 + T], ACT.Sqrt)\
                   .then_inc(M["kroot"], 1)
            return step

        run(act, J["rr"], split, first={k: [mix_hi("rr", k + 1, used["rr"][k + 1])] for k in range(3)},
            every={3: [kk_square(0), take_spill(J["rr"], "r_spilled", (M["v_spilled"], 64), 0)],
                   4: [kk_root(0), kk_square(1)], 5: [kk_root(1)],
                   7: [take_spill(J["rr"], "r_spilled", None, 1)]})
        core_act(act)
        residual("n3", J["ro"])
        ffn(1)
        for g in range(8):
            act.wait_ge(out_turned, g + 1)
            act.copy(xo[:, :, 2 * P * g:2 * P * (g + 1)].rearrange("p t (k q) -> p k t q", q=P),
                     bank(4 + g % 4).rearrange("p (k t q) -> p k t q", k=2, q=P)).then_inc(out_ready, 1)

    @block.vector
    def _(dve):
        def split(eng, job, i, j):
            job, i, j = next_place(job, i, j)
            dve.wait_ge(hi_split, job.panel_end(i, j))
            dve.tensor_tensor(wl[:, job.hl[j], :], raw[:, job.raw[j], :], wh[:, job.hl[j], :].bitcast(f32),
                              ALU.subtract).then_inc(lo_split, 1)

        def norm_rstd(n):
            dve.wait_ge(N[n]["rooted"], 1)
            dve.reciprocal(rstd[:, :], rstd[:, :]).then_inc(N[n]["rstd"], 1)

        def norm_scale(n, g, gain):
            dve.wait_ge(N[n]["rstd"], 1)
            if g >= 2:
                dve.wait_ge(N[n]["lo"], g - 1)
            for k in range(4):
                kt = 4 * g + k
                dve.scalar_tensor_tensor(hf[:, g % 2, k * T:(k + 1) * T], xT[:, kt, :],
                                         prm[:, gain + kt:gain + kt + 1], rstd[:, :], ALU.mult, ALU.mult)\
                   .then_inc(N[n]["normed"], 1)

        def norm_lo(n, g):
            dve.wait_ge(N[n]["hi"], g + 1)
            dve.tensor_tensor(hL[:, 4 * g:4 * g + 4, :], quad(hf[:, g % 2, :]),
                              hH[:, 4 * g:4 * g + 4, :].bitcast(f32), ALU.subtract).then_inc(N[n]["lo"], 1)

        def norm_start(n, gain):
            norm_scale(n, 0, gain)
            norm_scale(n, 1, gain)
            norm_lo(n, 0)

        def norm_steps(n, gain):
            def step(g):
                def go():
                    norm_lo(n, g)
                    if g + 1 < 4:
                        norm_scale(n, g + 1, gain)
                return go
            return {g - 1: [step(g)] for g in range(1, 4)}

        def add_squares(n, u):
            def step(*_):
                dve.wait_ge(N[n]["squared"], u + 1)
                if u >= 2:
                    dve.wait_ge(N[n]["summed"], u - 1)
                dve.tensor_tensor(sqacc[:, :], sqacc[:, :], sq[:, :], ALU.add).then_inc(N[n]["summed"], 1)
            return step

        add_squares("n0", 1)()
        split(dve, J["q"], 0, 0)
        add_squares("n0", 2)()
        dve.wait_ge(turned_out, 11)
        dve.tensor_scalar(prm[:, OMKA:OMKA + 16], prm[:, K_A:K_A + 16], -1.0, 1.0, ALU.mult, ALU.add)\
           .then_inc(omka_done, 1)
        norm_rstd("n0")
        norm_start("n0", G_MOBA)

        def qk_inverse(which, w):
            def step(i):
                n = 4 * which + 2 * i + w
                dve.wait_ge(qk["rooted"], n + 1)
                if n >= 2:
                    dve.wait_ge(qk["spread"], n - 1)
                dve.reciprocal(rsr[:, w, :], ssr[:, w, :]).then_inc(qk["inverse"], 1)
            return step

        def qk_norm(which, w):
            def step(i):
                n = 4 * which + 2 * i + w
                dve.wait_ge(qk["spread"], n + 1)
                for k in range(4):
                    dve.scalar_tensor_tensor(nrmd[:, k * T:(k + 1) * T], QKV[:, which * KT + i * 8 + (4 * w + k), :],
                                             prm[:, (QG, KG)[which]:(QG, KG)[which] + 1],
                                             aux[1][:, k * T:(k + 1) * T], ALU.mult, ALU.mult)\
                       .then_inc(qk["normed"], 1)
            return step

        def qk_rope(which, w):
            def step(i):
                n = 4 * which + 2 * i + w
                part = QKV[:, which * KT + i * 8 + 4 * w:which * KT + i * 8 + 4 * w + 4, :]
                dve.wait_ge(qk["turned"], n + 1)
                dve.wait_ge(qk["normed"], 4 * n + 4)
                dve.wait_ge(qk["roped"], n + 1)
                dve.tensor_tensor(quad(rot[:, :]), quad(aux[0][:, :]), spread(R("sin"), 4), ALU.mult)\
                   .then_inc(qk["sined"], 1)
                dve.tensor_tensor(part, quad(nrmd[:, :]), spread(R("cos"), 4), ALU.mult).then_inc(qk["cosed"], 1)
                dve.wait_ge(qk["sined"], n + 1)
                dve.wait_ge(qk["cosed"], n + 1)
                dve.tensor_tensor(part, part, quad(rot[:, :]), ALU.add).then_inc(qk["roped"], 1)
            return step

        jq, jk, jv, jo = (J[k] for k in ("q", "k", "v", "wo"))
        run(dve, jq, split, first=norm_steps("n0", G_MOBA))
        for which, job in ((0, jk), (1, jv)):
            run(dve, job, split, every={1: [qk_inverse(which, 0)], 2: [qk_inverse(which, 1)],
                                        3: [qk_norm(which, 0)], 4: [qk_rope(which, 0)],
                                        5: [qk_norm(which, 1)], 6: [qk_rope(which, 1)]})
        def body(i, n):
            for b in range(2):
                if i is None:
                    break
                dve.wait_ge(at["exped"], 4 * i + (2 * b + 2))
                dve.reciprocal(st[:, b, 6:8], st[:, b, 4:6]).then_inc(at["recip"], 1)
                dve.wait_ge(at["recip"], 2 * i + (b + 1))
                for t, (a, e) in enumerate(((0, P), (P, 3 * P))):
                    dve.tensor_scalar(ex[:, b, a:e], ex[:, b, a:e], st[:, b, 6 + t:7 + t], None, ALU.mult)\
                       .then_inc(at["probs"], 1)
            for b in range(2):
                if n is None:
                    break
                dve.wait_ge(at["scored"], 2 * n + (b + 1))
                dve.tensor_tensor(sc[:, b, :], aux[b][:, 0:384], R("cmask"), ALU.add).then_inc(at["masked"], 1)
                dve.wait_ge(at["masked"], 2 * n + (b + 1))
                for t, (a, e) in enumerate(((0, P), (P, 3 * P))):
                    dve.reduce_max(st[:, b, t:t + 1], sc[:, b, a:e], AX.X).then_inc(at["maxed"], 1)
                dve.wait_ge(at["maxed"], 4 * n + (2 * b + 2))
                dve.tensor_scalar(st[:, b, 2:4], st[:, b, 0:2], -(HD ** -0.5), None, ALU.mult)\
                   .then_inc(at["neg"], 1)
            for b in range(2):
                if i is not None:
                    dve.wait_ge(at["hi"], 2 * i + (b + 1))
                    dve.tensor_tensor(hL[:, bass.ds(2 * i + b, 1), :], acc[b][:, 0:T].unsqueeze(1),
                                      hH[:, bass.ds(2 * i + b, 1), :].bitcast(f32), ALU.subtract)\
                       .then_inc(at["lo"], 1)

        attention(body, dve)

        def add_unit(job, n, before):
            def step(w):
                def go(i):
                    dve.wait_ge(panel_used, job.panel_end(i, job.last_panel[w]))
                    if before:
                        before()
                    u = 2 * i + w
                    part = xT[:, 4 * u:4 * u + 4, :]
                    dve.tensor_tensor(part, part, quad(acc[job.unit(0, w) % 2][:, :]), ALU.add)\
                       .then_inc(unit_out, 1)
                return go
            return step

        def residual(n, job, first=None, before=None):
            a, m = job.units[0], job.m
            add = add_unit(job, n, before)
            steps = {k: list(v) for k, v in (first or {}).items()}
            if n is None:
                run(dve, job, split, first=steps, every={a - 1: [add(0)], m - 1: [add(1)]})
                return
            run(dve, job, split, first=steps, every={a - 1: [add(0)], m - 1: [add(1)]},
                late={1: [add_squares(n, 1)]}, last={a: [add_squares(n, 2)]})

        def ffn(layer):
            n = ("n1", "n3")[layer]
            gain = G_FFN + 16 * layer
            ja, da, jb, db = (J[f"{k}{layer}{h}"] for k, h in (("up", "a"), ("dn", "a"), ("up", "b"), ("dn", "b")))
            norm_rstd(n)
            norm_start(n, gain)

            def steps(job, g0):
                u0 = layer * (HALF_A + HALF_B) + g0
                cw0 = PCV + layer * 4 * 88

                def conv(w):
                    def step(i):
                        t0 = (2 * (i + u0) + w) * 4
                        for name, tap in (("tap1", 1), ("tap0", 2)):
                            for k in range(4):
                                a, e = k * T, (k + 1) * T
                                if tap == 1:
                                    dve.wait_ge(f["init"], t0 + (k + 1))
                                else:
                                    dve.wait_ge(f["tap1"], t0 + (k + 1))
                                c = i * 4 + (g0 * 4 + w * FKT + k + cw0 + (2 - tap) * 88)
                                dve.scalar_tensor_tensor(fc[:, a + tap:e], fu[:, a:e - tap],
                                                         prm[:, bass.ds(c, 1)], fc[:, a + tap:e],
                                                         ALU.mult, ALU.add).then_inc(f[name], 1)
                    return step

                def gate(i):
                    dve.wait_ge(f["silu"], i + (u0 + 1))
                    dve.wait_ge(f["tap0"], i * 8 + (8 * u0 + 8))
                    dve.tensor_tensor(fc[:, :], fc[:, :], sg[:, :], ALU.mult).then_inc(f["gated"], 1)

                def lo(i):
                    dve.wait_ge(f["hi"], i + (u0 + 1))
                    dve.tensor_tensor(aL[:, bass.ds(i * 4, 4), :], quad(fc[:, :]),
                                      aH[:, bass.ds(i * 4, 4), :].bitcast(f32), ALU.subtract).then_inc(f["lo"], 1)

                return {4: [conv(0)]}, {0: [conv(1)], 1: [gate], 2: [lo]}

            for job, dn, g0 in ((ja, da, 0), (jb, db, HALF_A)):
                every, late = steps(job, g0)
                first = {}
                if g0 == 0:
                    first = norm_steps(n, gain)
                run(dve, job, split, first=first, every=every, late=late)
                tail = {j: [lambda g=g, job=job: g(job.n - 1) for g in fs] for j, fs in late.items()}
                residual("n2" if layer == 0 and g0 else None, dn, first=tail)

        residual("n1", jo)
        ffn(0)

        norm_rstd("n2")
        dve.wait_ge(N["n2"]["rstd"], 1)
        for kt in range(KT):
            dve.scalar_tensor_tensor(hb[:, kt, :], xT[:, kt, :], prm[:, G_RWKV + kt:G_RWKV + kt + 1], rstd[:, :],
                                     ALU.mult, ALU.mult).then_inc(M["h"], 1)
        mixes = {"rg": 5, "rv": 3, "rw": 1, "ra": 4, "rk": 2, "rr": 0}
        order_mix = list(mixes)

        def mix_sum(name, g):
            n = 4 * order_mix.index(name) + g
            dve.wait_ge(M["xx"], 3 * g + 3)
            back = 1 if name in ("rk", "rr") else 2
            if n >= back:
                dve.wait_ge(M["lo"], n - back + 1)
            for k in range(4):
                kt = 4 * g + k
                col = MU + 16 * mixes[name] + kt
                dve.scalar_tensor_tensor(mix_buffer(name, g)[:, k * T:(k + 1) * T], xx[:, kt, :], prm[:, col:col + 1],
                                         hb[:, kt, :], ALU.mult, ALU.add).then_inc(M["mixed"], 1)

        def mix_lo(name, g):
            dve.wait_ge(M["hi"], 4 * order_mix.index(name) + g + 1)
            dve.tensor_tensor(hL[:, 4 * g:4 * g + 4, :], quad(mix_buffer(name, g)),
                              hH[:, 4 * g:4 * g + 4, :].bitcast(f32), ALU.subtract).then_inc(M["lo"], 1)

        def mix(name, g):
            def step(*_):
                mix_sum(name, g)
                mix_lo(name, g)
            return step

        def mix_all(name):
            mix_sum(name, 0)
            for g in range(1, 4):
                mix_sum(name, g)
                mix_lo(name, g - 1)
            mix_lo(name, 3)

        def low_lo(k, parts, width):
            dve.wait_ge(M["low_hi"], k + 1)
            dve.tensor_tensor(tL[0:parts, 0:width // T, :],
                              ru[0:parts, 0:width].rearrange("p (f t) -> p f t", t=T),
                              tH[0:parts, 0:width // T, :].bitcast(f32), ALU.subtract).then_inc(M["low_lo"], 1)

        jg = J["rg"]
        mix_all("rg")
        split(dve, jg, 0, 1)
        split(dve, jg, 0, 2)
        low_lo(0, P, 2 * T)
        split(dve, jg, 0, 3)
        split(dve, jg, 0, 4)
        mix("rv", 0)()
        run(dve, J["rv"], split, first={k: [mix("rv", k + 1)] for k in range(3)})
        dve.memset(cw[:, :, :, 0:1], 0.0).then_inc(M["zeroed"], 1)
        for k, name in ((1, "rw"), (2, "ra")):
            mix_all(name)
            split(dve, J[name], 0, 1)
            low_lo(k, LORA, T)
            split(dve, J[name], 0, 2)

        def decay_sum(j):
            def step(i):
                ft = 8 * i + j
                dve.wait_ge(unit_out, J["rw"].unit_end(0, 1 + ft // 4))
                dve.wait_ge(M["zeroed"], 1)
                for c in range(2):
                    dve.tensor_tensor_scan(cw[:, ft, c, 1:129], C("ones"), cw[:, ft, c, 1:129], 0.0,
                                           ALU.mult, ALU.add).then_inc(M["scan"], 1)
                dve.wait_ge(M["scan"], 2 * ft + 2)
                if ft:
                    dve.wait_ge(M["cw"], 2 * ft)
                dve.tensor_copy(mid[:, 0:2].unsqueeze(2), cw[:, ft, :, 64:65]).then_inc(M["mid"], 1)
                dve.wait_ge(M["mid"], ft + 1)
                for c in range(2):
                    dve.tensor_scalar(cw[:, ft, c, :], cw[:, ft, c, :], mid[:, c:c + 1], -EXPM05,
                                      ALU.subtract, ALU.mult).then_inc(M["cw"], 1)
            return step

        mix("rk", 0)()
        run(dve, J["rk"], split, first={k: [mix("rk", k + 1)] for k in range(3)},
            every={j: [decay_sum(j)] for j in range(8)})
        mix("rr", 0)()

        def kk_inverse(w):
            def step(i):
                u = 2 * i + w
                dve.wait_ge(M["kroot"], u + 1)
                if u >= 2:
                    dve.wait_ge(M["kspread"], u - 1)
                dve.tensor_scalar(kss[:, w, :], kss[:, w, :], 1e-12, None, ALU.max).then_inc(M["kmax"], 1)
                dve.wait_ge(M["kmax"], u + 1)
                dve.reciprocal(krs[:, w, :], kss[:, w, :]).then_inc(M["krec"], 1)
            return step

        def kk_finish(w):
            def step(i):
                u = 2 * i + w
                a, e = 4 * u, 4 * u + 4
                dve.wait_ge(M["kspread"], u + 1)
                dve.tensor_tensor(kkb[:, a:e, :], quad(aux[1][:, :]), quad(kkr[:, w, :]), ALU.mult)\
                   .then_inc(M["kk"], 1)
                dve.wait_ge(M["lo"], 24)
                if u:
                    dve.wait_ge(M["kmod"], u)
                dve.wait_ge(unit_out, J["ra"].unit_end(0, 4))
                for k in range(4):
                    ft = 4 * u + k
                    dve.tensor_scalar(mt[:, k * T:(k + 1) * T], ab[:, ft, :], prm[:, K_A + ft:K_A + ft + 1],
                                      prm[:, OMKA + ft:OMKA + ft + 1], ALU.mult, ALU.add).then_inc(M["kfac"], 1)
                dve.wait_ge(M["kfac"], 4 * u + 4)
                dve.tensor_tensor(kb[:, a:e, :], kb[:, a:e, :], quad(mt[:, :]), ALU.mult).then_inc(M["kmod"], 1)
                dve.wait_ge(M["kk"], u + 1)
                dve.tensor_tensor(ab[:, a:e, :], ab[:, a:e, :], kkb[:, a:e, :], ALU.mult).then_inc(M["kb"], 1)
            return step

        run(dve, J["rr"], split, first={k: [mix("rr", k + 1)] for k in range(3)},
            every={4: [kk_inverse(0)], 5: [kk_inverse(1)], 6: [kk_finish(0)], 7: [kk_finish(1)]})

        dve.wait_ge(M["x_spilled"], 16)
        dve.tensor_copy(Qb[:, :, :], spread(C("ident"), LEVELS * 4)).then_inc(W["zeroed"], 1)
        dve.wait_ge(M["kb"], 4)
        dve.wait_ge(M["r_spilled"], 64)
        for k in range(2):
            dve.memset(ars[k][:, :, :, :, :].rearrange("p h c a t -> p (h c a t)"), 0.0)\
               .then_inc(W["zeroed"], 1)
        dve.wait_ge(W["zeroed"], 3)

        def core_lo(p):
            dve.wait_ge(W["hi"], p + 1)
            dve.tensor_tensor(hL[:, bass.ds(p, 1), :], y2[:, :].unsqueeze(1),
                              hH[:, bass.ds(p, 1), :].bitcast(f32), ALU.subtract).then_inc(W["lo"], 1)

        def body(b, f, n):
            def gram(c):
                p, k = f
                dve.wait_ge(W["gram"], p * 2 + (c + 1))
                if has(p, 2):
                    dve.wait_ge(W["ymm"], pairs_before(p, 2, 1))
                dve.tensor_tensor(mBs[k][:, c], bank(c).rearrange("p (h n) -> p h n", h=2),
                                  spread(C("mb"), 2), ALU.mult).then_inc(W["gmask"], 1)
                dve.wait_ge(W["gmask"], p * 4 + (c + 1))
                dve.tensor_tensor(mBs[k][:, c, :, 0:P], mBs[k][:, c, :, 0:P], spread(C("ident"), 2), ALU.add)\
                   .then_inc(W["geye"], 1)

            def gram_k(c):
                p, k = f
                dve.tensor_tensor(mKs[k][:, c], bank(2 + c).rearrange("p (h n) -> p h n", h=2),
                                  spread(C("mk"), 2), ALU.mult).then_inc(W["gmask"], 1)

            def xt0(c):
                p, k = f
                dve.wait_ge(W["geye"], p * 2 + (c + 1))
                dve.tensor_tensor(XTs[k][:, c], mBs[k][:, c, :, 0:P], spread(C("mx1t"), 2), ALU.mult)\
                   .then_inc(W["xt0"], 1)

            def x0(c):
                p, k = f
                dve.wait_ge(W["lev0"], p * 2 + (c + 1))
                dve.tensor_tensor(X[:, c], bank(c)[:, 0:T].rearrange("p (h n) -> p h n", h=2),
                                  spread(C("mx1"), 2), ALU.mult).then_inc(W["x0"], 1)

            def level(lev, *chunks):
                p, k = f
                s = 1 << lev
                lv = C("lv", P * (lev - 1), P * lev)
                for c in chunks or range(2):
                    dve.wait_ge(W["lp"], p * 12 + (2 * (lev - 1) + c + 1))
                    dve.tensor_tensor(blocks(Ql(lev, c), s, 0), compact(bank(c)[:, 0:P], s), compact(lv, s),
                                      ALU.mult).then_inc(W["lq"], 1)

            if f:
                gram(0)
                gram(1)
            if b:
                p, k = b
                dve.wait_ge(W["smm"], p + 1)
                dve.tensor_scalar(s0[:, :], bank(6)[:, 0:RH], scl[:, k:k + 1], None, ALU.mult)\
                   .then_inc(W["sout"], 1)
            if f:
                x0(0)
                x0(1)
                for c in range(2):
                    xt0(c)
                    gram_k(c)
                    level(1, c)
                level(2)
            if b:
                p, k = b
                dve.wait_ge(W["bmm"], p + 1)
                dve.tensor_tensor(bps[k][:, :], bank(6)[:, 0:T], vbs[k][:, :], ALU.mult).then_inc(W["bon"], 1)
                if has(p, 1):
                    core_lo(p - 1)
                dve.wait_ge(W["mean"], p + 1)
                if has(p, 1):
                    dve.wait_ge(W["lo"], p)
                dve.scalar_tensor_tensor(y2[:, :], bank(5)[:, 0:T], -1.0 / RH, ys[:, :], ALU.mult, ALU.add)\
                   .then_inc(W["cent"], 1)
            if f:
                level(3)
            if f:
                p, k = f
                dve.wait_ge(W["scaled"], p * 6 + 6)
                if has(p, 2):
                    dve.wait_ge(W["ysum"], pairs_before(p, 2, 1))
                for h, r in heads:
                    dve.scalar_tensor_tensor(bps[k][r, :].rearrange("p (c t) -> p c t", c=2),
                                             ars[k][r, h, :, 1, :], prm[r, bass.ds(p + R_K, 1)],
                                             kt_[r, :, :], ALU.mult, ALU.mult).then_inc(W["bonusp"], 1)
            if n:
                p, k = n
                dve.wait_ge(W["exps"], p * 3 + 3)
                if has(p, 2):
                    dve.wait_ge(W["bmm"], pairs_before(p, 2, 1))
                if has(p, 1):
                    dve.wait_ge(W["gram"], p * 2)
                    dve.wait_ge(W["bonusp"], p * 2)
                for h, r in heads:
                    dve.scalar_tensor_tensor(ars[k][r, h, :, 0, :],
                                             kkp(p, rows=r).rearrange("p (c t) -> p c t", c=2),
                                             -1.0, e1[r, :, 0:P], ALU.mult, ALU.mult).then_inc(W["scaled"], 1)
                dve.tensor_tensor(bt[:, :, :], abp(p).rearrange("p (c t) -> p c t", c=2), e2[:, :, :], ALU.mult)\
                   .then_inc(W["scaled"], 1)
            if f:
                level(4)
            if n:
                p, k = n
                dve.tensor_tensor(kt_[:, :, :], kbp(p).rearrange("p (c t) -> p c t", c=2), e2[:, :, :], ALU.mult)\
                   .then_inc(W["scaled"], 1)
                dve.wait_ge(W["r_in"], p * 16 + 16)
                for h, r in heads:
                    dve.tensor_tensor(ars[k][r, h, :, 1, :], rb[r, :].rearrange("p (c t) -> p c t", c=2),
                                      e1[r, :, 1:129], ALU.mult).then_inc(W["scaled"], 1)
            if f:
                level(5)
            if f:
                level(6)
            if b:
                dve.wait_ge(W["std"], b[0] + 1)
                dve.reciprocal(y3[:, :], y3[:, :]).then_inc(W["rec"], 1)

        core(body, dve)
        core_lo(KT - 1)

        residual("n3", J["ro"], before=lambda: dve.wait_ge(M["x_back"], 16))
        ffn(1)

    @block.gpsimd
    def _(pool):
        def vec(v):
            return v.rearrange("(t p) -> t p", p=P)

        prows = [(0, 0, vec(moba_norm[0])), (0, 16, vec(rwkv_norm[0])),
                 (0, 32, rwkv_mu[0].rearrange("a (t p) -> (a t) p", p=P))]
        for k, v in enumerate((rwkv_w0, rwkv_a0, rwkv_k_k, rwkv_k_a)):
            prows.append((1, 16 * k, vec(v[0])))
        prows.append((1, 64, rwkv_r_k[0].rearrange("(t h) n -> t (h n)", h=2)))
        prows += [(1, 80, vec(rwkv_lnx_w[0])), (1, 96, vec(rwkv_lnx_b[0]))]
        prows += [(2, 0, ffn_norm.rearrange("a (t p) -> (a t) p", p=P)), (2, 32, moba_q_gain), (2, 33, moba_k_gain)]
        for layer in range(2):
            for k in range(3):
                prows.append((3 + 4 * layer + k, 0, vec(ffn_conv_w[layer, k])))
            prows.append((6 + 4 * layer, 0, vec(ffn_conv_b[layer])))
        assert len(prows) == ROW_LOADS
        for k, (tile, r0, src) in enumerate(prows):
            if k == ROW_LOADS // 2:
                pool.dma_start(cst[:, P:], const_all[:, P:]).then_inc(rows_in, 16)
            pool.dma_start(prow[r0:r0 + src.shape[0], tile, :], src).then_inc(rows_in, 16)
        pool.dma_start(cr[:, :], const_rope).then_inc(rows_in, 16)

        xs = x_spill
        for g in range(4):
            a, e = 4 * g, 4 * g + 4
            pool.wait_ge(M["h"], e)
            pool.memset(xx[:, a:e, 0:1], 0.0).then_inc(M["xx"], 1)
            pool.tensor_tensor(xx[:, a:e, 1:T], hb[:, a:e, 0:T - 1], hb[:, a:e, 1:T], ALU.subtract)\
                .then_inc(M["xx"], 1)
            pool.wait_ge(M["xx"], 3 * g + 1)
            pool.tensor_tensor(xx[:, a:e, 0:1], xx[:, a:e, 0:1], hb[:, a:e, 0:1], ALU.subtract)\
                .then_inc(M["xx"], 1)
        pool.wait_ge(M["h"], KT)
        pool.dma_start(xs, xT[:, :, :]).then_inc(M["x_spilled"], 16)
        for u in range(4):
            pool.wait_ge(unit_out, J["rg"].unit_end(0, 1 + u))
            pool.dma_start(g_spill[:, 4 * u:4 * u + 4, :], ab[:, 4 * u:4 * u + 4, :]).then_inc(M["g_spilled"], 16)
        for name, dst, done in (("rv", v_spill, "v_spilled"), ("rr", r_spill, "r_spilled")):
            for u in range(4):
                pool.wait_ge(unit_out, J[name].unit_end(*divmod(u, 2)))
                pool.dma_start(dst[:, 4 * u:4 * u + 4, :], quad(ru[:, :])).then_inc(M[done], 16)

        def body(b, f, n):
            if not b:
                return
            p, k = b
            pool.wait_ge(W["cent"], p + 1)
            pool.wait_ge(W["rec"], p + 1)
            pool.tensor_tensor(y2[:, :], y2[:, :], y3[:, :], ALU.mult).then_inc(W["norm"], 1)
            pool.wait_ge(W["bon"], p + 1)
            pool.wait_ge(W["aff"], p + 1)
            pool.tensor_tensor(y2[:, :], y2[:, :], bps[k][:, :], ALU.add).then_inc(W["ysum"], 1)
            pool.wait_ge(W["g_in"], p * 16 + 16)
            pool.wait_ge(W["ysum"], p + 1)
            pool.tensor_tensor(y2[:, :], y2[:, :], gb[:, :], ALU.mult).then_inc(W["gate"], 1)

        core(body, pool)
        pool.wait_ge(W["lo"], KT)
        pool.dma_start(xT[:, :, :], xs).then_inc(M["x_back"], 16)
        for s, n in ((M["x_spilled"], 16), (M["g_spilled"], 64), (M["v_spilled"], 64), (M["r_spilled"], 64),
                     (M["x_back"], 16)):
            pool.wait_ge(s, n)

    @block.tensor
    def _(pe):
        def products(job, src, ready, every=None):
            every = every or {}

            def body(i):
                j = 0
                for w, panels in enumerate(job.units):
                    a = acc[job.unit(0, w) % 2]
                    for p in range(panels):
                        pe.wait_ge(lo_split, job.panel_end(i, j))
                        if p == 0:
                            pe.wait_ge(unit_out, job.unit_end(i, w) - 2)
                        ready(p)
                        s = job.hl[j]
                        for q in range(4):
                            hi, lo = src(4 * p + q)
                            for ft in range(4):
                                at_ = q * UNIT + ft * P
                                for n, (wt, h) in enumerate(((wh, hi), (wh, lo), (wl, hi))):
                                    mm = pe.matmul(a[:, ft * T:(ft + 1) * T], wt[:, s, at_:at_ + P], h,
                                                   start=(p == 0 and q == 0 and n == 0 and ft % 2 == 0),
                                                   stop=(p == panels - 1 and q == 3 and n == 2),
                                                   skip_group_check=True)
                        mm.then_inc(panel_used, 1)
                        for f in every.get(j, ()):
                            f(i)
                        j += 1

            if job.n == 1:
                body(0)
            else:
                with pe.Fori(0, job.n) as i:
                    body(i)

        def h_in(kt):
            return hH[:, kt, :], hL[:, kt, :]

        def a_in(kt):
            return aH[:, kt, :], aL[:, kt, :]

        pe.sem_inc(panel_used, SEED)
        pe.sem_inc(hi_split, SEED)
        pe.sem_inc(lo_split, SEED)
        pe.sem_inc(unit_out, 2)
        pe.sem_inc(qk["roped"], 1)
        pe.wait_ge(const_in, 16)
        pe.wait_ge(x_in, 32)
        for g in range(8):
            if g >= 4:
                pe.wait_ge(turned_out, g - 3)
            for k in range(2):
                for tt in range(2):
                    mm = pe.transpose(bank(4 + g % 4)[:, (2 * k + tt) * P:(2 * k + tt + 1) * P],
                                      xin[:, tt, (2 * g + k) * P:(2 * g + k + 1) * P], C("ident"))
            mm.then_inc(turned, 1)
        def total_first(n):
            pe.wait_ge(N[n]["summed"], 2)
            for k in range(4):
                pe.matmul(aux[1][:, 512:512 + T], C("ones"), sqacc[:, k * T:(k + 1) * T], start=(k == 0), stop=False)

        def total_last(n):
            pe.wait_ge(N[n]["squared"], 4)
            for k in range(4):
                mm = pe.matmul(aux[1][:, 512:512 + T], C("ones"), sq[:, k * T:(k + 1) * T], start=False, stop=(k == 3))
            mm.then_inc(N[n]["total"], 1)

        def norm_total(n):
            total_first(n)
            total_last(n)

        pe.wait_ge(rows_in, 16 * (ROW_LOADS + 2))
        pe.wait_ge(turned_out, 8)
        total_first("n0")
        for g, tiles in enumerate(((0, 1, 2), (3, 4, 5, 6), (7, 8, 9, 10))):
            pe.wait_ge(turned_out, 5 + g)
            at_ = 0
            for tile in tiles:
                n = {0: 128, 1: 112, 2: 34}.get(tile, 88)
                mm = pe.transpose(bank(4 + g)[:, at_:at_ + n], prow[0:n, tile, :], C("ident", 0, n, p=n))
                at_ += n
            mm.then_inc(turned, 1)

        pe.wait_ge(turned_out, 9)
        total_last("n0")

        def qk_sum(which, w):
            def step(i):
                n = i * 2 + (4 * which + w)
                pe.wait_ge(qk["squared"], n + 1)
                pe.wait_ge(qk["roped"], n - (w - 1))
                for k in range(4):
                    mm = pe.matmul(aux[0][0:4, w * 512:w * 512 + T], R("ssum", 4 * k, 4 * k + 4),
                                   sq2[:, w, k * T:(k + 1) * T], start=(k == 0), stop=(k == 3))
                mm.then_inc(qk["summed"], 1)
            return step

        def qk_spread(which, w):
            def step(i):
                n = i * 2 + (4 * which + w)
                pe.wait_ge(qk["inverse"], n + 1)
                if which or w:
                    pe.wait_ge(qk["normed"], 4 * n)
                for k in range(4):
                    mm = pe.matmul(aux[1][:, k * T:(k + 1) * T], R("sbc", k * P, (k + 1) * P, p=4), rsr[:, w, :],
                                   start=True, stop=True)
                mm.then_inc(qk["spread"], 1)
            return step

        def qk_turn(which, w):
            def step(i):
                n = i * 2 + (4 * which + w)
                pe.wait_ge(qk["normed"], 4 * n + 4)
                for k in range(2):
                    mm = pe.matmul(aux[0][:, k * 512:(k + 1) * 512], R("perm"), nrmd[:, k * 512:(k + 1) * 512],
                                   start=True, stop=True)
                mm.then_inc(qk["turned"], 1)
            return step

        def normed(n):
            return lambda p: pe.wait_ge(N[n]["lo"], p + 1)

        jq, jk, jv, jo = (J[k] for k in ("q", "k", "v", "wo"))
        products(jq, h_in, normed("n0"))
        for which, job in ((0, jk), (1, jv)):
            products(job, h_in, normed("n0"),
                     every={0: [qk_sum(which, 0)], 1: [qk_sum(which, 1)], 2: [qk_spread(which, 0)],
                            3: [qk_turn(which, 0)], 4: [qk_spread(which, 1)], 5: [qk_turn(which, 1)]})
        pe.wait_ge(qk["roped"], 9)
        def body(i, n):
            for b in range(2):
                if i is None:
                    break
                pe.wait_ge(at["probs"], 4 * i + (2 * b + 2))
                pe.wait_ge(at["vout"], 2 * i + (b + 1))
                for k, a in enumerate((0, P, 2 * P)):
                    mm = pe.transpose(aux[b][:, 512 + k * P:512 + (k + 1) * P], ex[:, b, a:a + P], C("ident"))
                mm.then_inc(at["pturned"], 1)
            for b in range(2):
                if n is None:
                    break
                pe.wait_ge(at["staged"], 4 * n + (b + 1))
                if i is not None:
                    pe.wait_ge(at["masked"], 2 * i + (b + 1))
                for (a, e), qa in (((0, P), 0), ((P, 3 * P), P)):
                    k = QKV[:, bass.ds(n * 2 + (KT + b), 1), 0:e - a].rearrange("p a t -> p (a t)")
                    mm = pe.matmul(aux[b][:, a:e], qs[:, b, qa:qa + P], k, start=True, stop=True)
                mm.then_inc(at["scored"], 1)
            for b in range(2):
                if i is None:
                    break
                pe.wait_ge(at["pout"], 2 * i + (b + 1))
                if has(i, 1):
                    pe.wait_ge(at["lo"], 2 * i + (b - 1))
                pe.matmul(acc[b][:, 0:T], vt[:, b, 0:P], pT[:, b, 0:T], start=True, stop=True,
                          skip_group_check=True)
                pe.matmul(acc[b][:, P:T], vt[:, b, P:T], pT[:, b, T:T + P], start=False, stop=True,
                          skip_group_check=True).then_inc(at["mixed"], 1)
            for b in range(2):
                if n is None:
                    break
                pe.wait_ge(at["staged"], 4 * n + (b + 3))
                for t in range(2):
                    mm = pe.transpose(aux[b][:, 512 + t * P:512 + (t + 1) * P], vs[:, b, t * P:(t + 1) * P],
                                      C("ident"))
                mm.then_inc(at["vturned"], 1)

        attention(body, pe)

        products(jo, h_in, lambda p: pe.wait_ge(at["lo"], NH))

        def ffn(layer):
            n = ("n1", "n3")[layer]
            norm_total(n)
            for h, g0 in (("a", 0), ("b", HALF_A)):
                products(J[f"up{layer}{h}"], h_in, normed(n))
                u0 = layer * (HALF_A + HALF_B) + g0
                products(J[f"dn{layer}{h}"], a_in, lambda p, u0=u0: pe.wait_ge(f["lo"], u0 + p + 1))

        ffn(0)
        norm_total("n2")
        mixed = {name: (lambda p, k=k: pe.wait_ge(M["lo"], 4 * k + p + 1))
                 for k, name in enumerate(("rg", "rv", "rw", "ra", "rk", "rr"))}

        def triple(out_, lhs, kt_hi, kt_lo, first, last, clear):
            for n, (wt, h) in enumerate(((wh, kt_hi), (wh, kt_lo), (wl, kt_hi))):
                mm = pe.matmul(out_, lhs(wt), h, start=(first and clear and n == 0), stop=(last and n == 2),
                               skip_group_check=True)
            return mm

        def low_units(job, k, slots, parts):
            pe.wait_ge(M["low_lo"], k + 1)
            for u in range(4):
                a = acc[job.unit(0, 1 + u) % 2]
                pe.wait_ge(unit_out, job.unit_end(0, 1 + u) - 2)
                for ft in range(4):
                    col = (4 * u + ft) * P
                    for q, s in enumerate(slots):
                        mm = triple(a[:, ft * T:(ft + 1) * T], lambda wt, s=s: wt[0:parts, s, col:col + P],
                                    tH[0:parts, q, :], tL[0:parts, q, :], q == 0, q == len(slots) - 1,
                                    ft % 2 == 0)
                mm.then_inc(M["low_unit"], 1)

        jg = J["rg"]
        pe.wait_ge(unit_out, jg.unit_end(0, 0) - 2)
        for j in range(2):
            pe.wait_ge(lo_split, jg.panel_end(0, j))
            for q in range(8):
                kt = 8 * j + q
                if kt % 4 == 0:
                    mixed["rg"](kt // 4)
                for ft in range(2):
                    at_ = q * T + ft * P
                    mm = triple(acc[jg.unit(0, 0) % 2][:, ft * T:(ft + 1) * T],
                                lambda wt: wt[:, jg.hl[j], at_:at_ + P], hH[:, kt, :], hL[:, kt, :],
                                kt == 0, kt == KT - 1, ft == 0)
            mm.then_inc(panel_used, 1)
        pe.wait_ge(lo_split, jg.panel_end(0, 3))
        low_units(jg, 0, jg.hl[2:4], P)
        pe.drain().then_inc(panel_used, 2)
        products(J["rv"], h_in, mixed["rv"])
        for k, name in ((1, "rw"), (2, "ra")):
            job = J[name]
            pe.wait_ge(lo_split, job.panel_end(0, 0))
            pe.wait_ge(unit_out, job.unit_end(0, 0) - 2)
            for kt in range(KT):
                if kt % 4 == 0:
                    mixed[name](kt // 4)
                mm = triple(acc[job.unit(0, 0) % 2][0:LORA, 0:T],
                            lambda wt: wt[:, job.hl[0], kt * LORA:(kt + 1) * LORA], hH[:, kt, :], hL[:, kt, :],
                            kt == 0, kt == KT - 1, True)
            mm.then_inc(panel_used, 1)
            pe.wait_ge(lo_split, job.panel_end(0, 1))
            low_units(job, k, job.hl[1:2], LORA)
            pe.drain().then_inc(panel_used, 1)
        products(J["rk"], h_in, mixed["rk"])

        def kk_sum(w):
            def step(i):
                pe.wait_ge(M["ksq"], i * 2 + (w + 1))
                for k in range(4):
                    mm = pe.matmul(aux[0][0:8, w * 512:w * 512 + T], C("ksum", 8 * k, 8 * k + 8),
                                   kq[:, k * T:(k + 1) * T], start=(k == 0), stop=(k == 3))
                mm.then_inc(M["ksum"], 1)
            return step

        def kk_spread(w):
            def step(i):
                pe.wait_ge(M["krec"], i * 2 + (w + 1))
                if w:
                    pe.wait_ge(M["kk"], i * 2 + w)
                for k in range(4):
                    mm = pe.matmul(aux[1][:, k * T:(k + 1) * T], C("kbc", k * P, (k + 1) * P, p=8),
                                   krs[:, w, :], start=True, stop=True)
                mm.then_inc(M["kspread"], 1)
            return step

        products(J["rr"], h_in, mixed["rr"],
                 every={3: [kk_sum(0)], 4: [kk_sum(1)], 5: [kk_spread(0)], 6: [kk_spread(1)]})
        core_pe(pe)
        products(J["ro"], h_in, lambda p: pe.wait_ge(W["lo"], KT))
        ffn(1)
        pe.wait_ge(unit_out, final_job.unit_end(final_job.n - 1, 1))
        for g in range(8):
            if g >= 4:
                pe.wait_ge(out_ready, g - 3)
            for k in range(2):
                for tt in range(2):
                    mm = pe.transpose(bank(4 + g % 4)[:, (2 * k + tt) * P:(2 * k + tt + 1) * P],
                                      xT[:, 2 * g + k, tt * P:(tt + 1) * P], C("ident"))
            mm.then_inc(out_turned, 1)

    block_ctx.__exit__(None, None, None)


def constants():
    import numpy as np
    r, c = np.arange(P)[:, None], np.arange(P)[None, :]
    parts = {
        "ident": np.eye(P), "ones": np.ones((P, P)), "blk": r // RH == c // RH,
        "mb": np.hstack([-1.0 * (r < c), r <= c]), "mk": np.hstack([r < c, r <= c]),
        "mx1": 1.0 * (r == c) - ((r == c + 1) & (c % 2 == 0)), "mx1t": 1.0 * (r == c) - ((c == r + 1) & (r % 2 == 0)),
        "ksum": np.hstack([np.stack([r[:, 0] // RH + 2 * k == j for j in range(8)], 1) for k in range(4)]),
        "eps": np.array([[NORM_EPS, GN_EPS, 0, 0]] * P),
    }
    kbc = np.zeros((P, 4 * P))
    for k in range(4):
        for j in range(8):
            kbc[j, k * P:(k + 1) * P] = np.arange(P) // RH + 2 * k == j
    parts["kbc"] = kbc
    levels = []
    for level in range(1, LEVELS + 1):
        s = 1 << level
        cols = np.array([q for q in range(P) if q % (2 * s) < s])[None, :]
        one = 1.0 * (r == cols) - ((r // (2 * s) == cols // (2 * s)) & (r % (2 * s) >= s))
        levels += [one, one]
    parts["lv"] = np.hstack(levels)
    a = np.zeros((P, NCONST), np.float32)
    for name, (lo, hi) in CONST.items():
        a[:, lo:hi] = parts[name]
    half = HD // 8
    freq = np.float32(500000.0) ** (-np.arange(0, 2 * half, 2, dtype=np.float32) / np.float32(2 * half))
    ang = np.arange(T, dtype=np.float32)[None, :] * freq.astype(np.float32)[:, None]
    cos, sin = np.ones((P, T), np.float32), np.zeros((P, T), np.float32)
    cos[0:half], cos[half:2 * half] = np.cos(ang), np.cos(ang)
    sin[0:half], sin[half:2 * half] = -np.sin(ang), np.sin(ang)
    perm = np.zeros((P, P))
    for d in range(half):
        perm[d + half, d] = perm[d, d + half] = 1.0
    causal = np.where(c <= r, 0.0, -1e30)
    ssum, sbc = np.zeros((P, 16)), np.zeros((P, 4 * P))
    for k in range(4):
        ssum[:, 4 * k + k] = 1.0
        sbc[k, k * P:(k + 1) * P] = 1.0
    rope = {"perm": perm, "cos": cos, "sin": sin, "cmask": np.hstack([causal, np.zeros((P, P)), causal]),
            "ssum": ssum, "sbc": sbc}
    b = np.zeros((P, NROPE), np.float32)
    for name, (lo, hi) in ROPE.items():
        b[:, lo:hi] = rope[name]
    return a, b


_INS = ["x", "moba_norm", "moba_wqkv", "moba_q_gain", "moba_k_gain", "moba_wo",
        "rwkv_norm", "rwkv_mu", "rwkv_w_r", "rwkv_w_k", "rwkv_w_v", "rwkv_w_o",
        "rwkv_w0", "rwkv_w1", "rwkv_w2", "rwkv_a0", "rwkv_a1", "rwkv_a2", "rwkv_g1", "rwkv_g2",
        "rwkv_k_k", "rwkv_k_a", "rwkv_r_k", "rwkv_lnx_w", "rwkv_lnx_b",
        "ffn_norm", "ffn_w_up", "ffn_conv_w", "ffn_conv_b", "ffn_w_down"]


def kernel(**inputs):
    import numpy as _np
    import concourse.bacc as _bacc
    from concourse import mybir as _mybir
    from concourse.bass_utils import run_bass_kernel_spmd as _run

    nc = _bacc.Bacc("TRN2", target_bir_lowering=False, num_devices=1)
    arrays, args = {}, []
    const_all, const_rope = constants()
    for name, a in [(n, inputs[n]) for n in _INS] + [("const_all", const_all), ("const_rope", const_rope)]:
        a = _np.ascontiguousarray(a)
        arrays[f"in_{name}_dram"] = a
        args.append(nc.dram_tensor(f"in_{name}_dram", a.shape, _mybir.dt.from_np(a.dtype), kind="ExternalInput").ap())
    args.append(nc.dram_tensor("out_0_dram", (1, T, D), _mybir.dt.float32, kind="ExternalOutput").ap())
    for name in ("x", "r", "v", "g"):
        args.append(nc.dram_tensor(f"{name}_spill", (P, KT, T), _mybir.dt.float32, kind="Internal").ap())
    hybrid_trunk(nc, *args)
    r = _run(nc, [arrays], core_ids=[0])
    return r.results[0]["out_0_dram"]
```
